# Optimizing a Trainium2 kernel written in Bass

```python
import math
import jax, jax.numpy as jnp
from jax import lax
import numpy as np

D_MODEL = 1024
BATCH = 1
SEQ = 256
DEPTH = 1
DEC_BATCH = 1
DEC_SEQ = 1024
PAST_LEN = 512

GRID_W = 64
EPS = 1e-6
H_A = 8
DK = 128
DV = 128
CONV_W = 5
CHUNK = 64
S5_W = 1024
S5_P = 16
S5_G = S5_W // S5_P
S5_N = 64
D_FF = -(-8 * D_MODEL // (3 * 256)) * 256
QKV_DIM = 2 * H_A * DK + H_A * DV
Z_DIM = H_A * DV
IN_DIM = QKV_DIM + Z_DIM + 4 * H_A + S5_W + 2 * D_MODEL

kernel_name = 'bidir_deltanet_s5_prefix_dit_step'

def rmsnorm(x, g):
    xf = x.astype(jnp.float32)
    return xf * lax.rsqrt(jnp.mean(xf * xf, axis=-1, keepdims=True) + EPS) * g.astype(jnp.float32)

def l2norm(x):
    return x * lax.rsqrt(jnp.sum(x * x, axis=-1, keepdims=True) + EPS)

def centred_conv(x, w):
    ch = x.shape[-1]
    return lax.conv_general_dilated(
        x, w.astype(jnp.float32)[:, None, :], window_strides=(1,),
        padding=[(CONV_W // 2, CONV_W // 2)], dimension_numbers=('NWC', 'WIO', 'NWC'),
        feature_group_count=ch)

def grid_pos_embed(rows):
    quarter = D_MODEL // 4
    omega = 1.0 / (10000.0 ** (jnp.arange(quarter, dtype=jnp.float32) / quarter))
    r = jnp.repeat(jnp.arange(rows, dtype=jnp.float32), GRID_W)[:, None] * omega
    col = jnp.tile(jnp.arange(GRID_W, dtype=jnp.float32), rows)[:, None] * omega
    return jnp.concatenate([jnp.sin(r), jnp.cos(r), jnp.sin(col), jnp.cos(col)], axis=-1)

def _to_chunks(t):
    b, l, h = t.shape[:3]
    t = t.reshape((b, l // CHUNK, CHUNK, h) + t.shape[3:])
    return t.transpose((0, 3, 1, 2) + tuple(range(4, t.ndim)))

def gated_delta_chunked(q, k, v, beta, g, s0):
    bsz, n_tok, n_h, _ = q.shape
    qc, kc, vc = _to_chunks(q), _to_chunks(k), _to_chunks(v)
    bc, gc = _to_chunks(beta), _to_chunks(g)
    cum = jnp.cumsum(gc, axis=-1)
    idx = jnp.arange(CHUNK)
    strict = idx[:, None] > idx[None, :]
    incl = idx[:, None] >= idx[None, :]
    diff = cum[..., :, None] - cum[..., None, :]
    dec_strict = jnp.exp(jnp.where(strict, diff, -jnp.inf))
    dec_incl = jnp.exp(jnp.where(incl, diff, -jnp.inf))
    gam = jnp.exp(cum)
    tmat = jnp.eye(CHUNK, dtype=q.dtype) + bc[..., :, None] * jnp.einsum('bhnid,bhnjd->bhnij', kc, kc) * dec_strict
    rhs = jnp.concatenate([(bc * gam)[..., None] * kc, bc[..., None] * vc], axis=-1)
    sol = lax.linalg.triangular_solve(tmat, rhs, left_side=True, lower=True, unit_diagonal=True)
    wk, uv = sol[..., :DK], sol[..., DK:]
    a_qk = jnp.einsum('bhnid,bhnjd->bhnij', qc, kc) * dec_incl
    g_end = cum[..., -1]
    k_dec = kc * jnp.exp(g_end[..., None] - cum)[..., None]
    xs = tuple(jnp.moveaxis(t, 2, 0) for t in (qc, k_dec, wk, uv, a_qk, gam, jnp.exp(g_end)))

    def step(s, xs_c):
        q_c, kd_c, wk_c, uv_c, aqk_c, gam_c, gend_c = xs_c
        u_c = uv_c - jnp.einsum('bhid,bhde->bhie', wk_c, s)
        o_c = gam_c[..., None] * jnp.einsum('bhid,bhde->bhie', q_c, s) + jnp.einsum('bhij,bhje->bhie', aqk_c, u_c)
        s = gend_c[..., None, None] * s + jnp.einsum('bhjd,bhje->bhde', kd_c, u_c)
        return s, o_c

    s_fin, o = lax.scan(step, s0, xs)
    o = o.transpose(1, 0, 3, 2, 4).reshape(bsz, n_tok, n_h, DV)
    return o, s_fin

def _scan_combine(e_i, e_j):
    a_i, b_i = e_i
    a_j, b_j = e_j
    return a_j * a_i, a_j * b_i + b_j

def s5_direction(u, h0_re, h0_im, a_re, a_im, log_dt, b_re, b_im, c_re, c_im, reverse):
    f32 = jnp.float32
    n_tok = u.shape[1]
    lam = lax.complex(a_re.astype(f32), a_im.astype(f32))
    dt = jnp.exp(log_dt.astype(f32))[:, None]
    a_bar = jnp.exp(lam * dt)
    b_bar = ((a_bar - 1.0) / lam)[..., None] * lax.complex(b_re.astype(f32), b_im.astype(f32))
    bu = lax.complex(jnp.einsum('blgp,gnp->blgn', u, jnp.real(b_bar)),
                     jnp.einsum('blgp,gnp->blgn', u, jnp.imag(b_bar)))
    pos = n_tok - 1 if reverse else 0
    bu = bu.at[:, pos].add(a_bar * lax.complex(h0_re.astype(f32), h0_im.astype(f32)))
    a_seq = jnp.broadcast_to(a_bar, (1, n_tok) + a_bar.shape)
    _, hs = lax.associative_scan(_scan_combine, (a_seq, bu), reverse=reverse, axis=1)
    y = (jnp.einsum('blgn,gpn->blgp', jnp.real(hs), c_re.astype(f32))
         - jnp.einsum('blgn,gpn->blgp', jnp.imag(hs), c_im.astype(f32)))
    h_fin = hs[:, pos]
    return y, jnp.real(h_fin), jnp.imag(h_fin)

def setup_inputs(seed: int = 0) -> dict:
    key = jax.random.key(seed)
    ks = iter(jax.random.split(key, 40))
    f32 = jnp.float32

    def nrm(shape, scale):
        return jax.random.normal(next(ks), shape, f32) * scale

    def unif(shape, lo, hi):
        return jax.random.uniform(next(ks), shape, f32, lo, hi)

    dt = jnp.exp(unif((DEPTH, 2, H_A), math.log(1e-3), math.log(1e-1)))
    return {
        'x_prompt': nrm((BATCH, SEQ, D_MODEL), 1.0),
        'x_sample': nrm((DEC_BATCH, DEC_SEQ, D_MODEL), 1.0),
        'c': nrm((DEC_BATCH, D_MODEL), 1.0),
        'state_delta': nrm((DEC_BATCH, DEPTH, 2, H_A, DK, DV), DK ** -0.5),
        'state_s5_re': nrm((DEC_BATCH, DEPTH, 2, S5_G, S5_N), 0.1),
        'state_s5_im': nrm((DEC_BATCH, DEPTH, 2, S5_G, S5_N), 0.1),
        'c_ctx': nrm((D_MODEL,), 1.0),
        'w_ada': nrm((DEPTH, D_MODEL, 6 * D_MODEL), 0.5 * D_MODEL ** -0.5),
        'b_ada': nrm((DEPTH, 6 * D_MODEL), 0.02),
        'norm1': 1.0 + nrm((DEPTH, D_MODEL), 0.02),
        'w_in': nrm((DEPTH, D_MODEL, IN_DIM), D_MODEL ** -0.5),
        'conv_w': nrm((DEPTH, CONV_W, QKV_DIM), CONV_W ** -0.5),
        'a_log': jnp.log(unif((DEPTH, 2, H_A), 1.0, 16.0)),
        'dt_bias': dt + jnp.log(-jnp.expm1(-dt)),
        'dn_norm': 1.0 + nrm((DEPTH, DV), 0.02),
        'w_br_a': nrm((DEPTH, H_A * DV, D_MODEL), (H_A * DV) ** -0.5),
        's5_a_re': -0.5 + nrm((DEPTH, 2, S5_G, S5_N), 0.01),
        's5_a_im': jnp.pi * jnp.arange(S5_N, dtype=f32) + nrm((DEPTH, 2, S5_G, S5_N), 0.01),
        's5_log_dt': unif((DEPTH, 2, S5_G), math.log(1e-3), math.log(1e-1)),
        's5_b_re': nrm((DEPTH, 2, S5_G, S5_N, S5_P), (2 * S5_P) ** -0.5),
        's5_b_im': nrm((DEPTH, 2, S5_G, S5_N, S5_P), (2 * S5_P) ** -0.5),
        's5_c_re': nrm((DEPTH, 2, S5_G, S5_P, S5_N), S5_N ** -0.5),
        's5_c_im': nrm((DEPTH, 2, S5_G, S5_P, S5_N), S5_N ** -0.5),
        's5_d': nrm((DEPTH, S5_G, S5_P), 1.0),
        'w_glu': nrm((DEPTH, S5_W, S5_W), S5_W ** -0.5),
        'b_glu': nrm((DEPTH, S5_W), 0.02),
        'w_br_b': nrm((DEPTH, S5_W, D_MODEL), S5_W ** -0.5),
        'w_out': nrm((DEPTH, D_MODEL, D_MODEL), D_MODEL ** -0.5),
        'norm2': 1.0 + nrm((DEPTH, D_MODEL), 0.02),
        'w_gu': nrm((DEPTH, D_MODEL, 2 * D_FF), D_MODEL ** -0.5),
        'w_down': nrm((DEPTH, D_FF, D_MODEL), D_FF ** -0.5),
        'norm_f': 1.0 + nrm((D_MODEL,), 0.02),
    }

def reference(x_prompt, x_sample, c, state_delta, state_s5_re, state_s5_im, c_ctx,
              w_ada, b_ada, norm1, w_in, conv_w, a_log, dt_bias, dn_norm, w_br_a,
              s5_a_re, s5_a_im, s5_log_dt, s5_b_re, s5_b_im, s5_c_re, s5_c_im, s5_d,
              w_glu, b_glu, w_br_b, w_out, norm2, w_gu, w_down, norm_f):
    f32 = jnp.float32
    cut1 = QKV_DIM
    cut2 = cut1 + Z_DIM
    cut3 = cut2 + 2 * H_A
    cut4 = cut3 + 2 * H_A
    cut5 = cut4 + S5_W
    cut6 = cut5 + D_MODEL

    def mixer(h, l, st_delta, st_re, st_im):
        bsz, n_tok, _ = h.shape
        proj = h @ w_in[l].astype(f32)
        qkv, z, b_raw, a_raw, u, gate_a, gate_b = jnp.split(proj, [cut1, cut2, cut3, cut4, cut5, cut6], axis=-1)
        qkv = jax.nn.silu(centred_conv(qkv, conv_w[l]))
        q, k, v = jnp.split(qkv, [H_A * DK, 2 * H_A * DK], axis=-1)
        q = l2norm(q.reshape(bsz, n_tok, H_A, DK)) * DK ** -0.5
        k = l2norm(k.reshape(bsz, n_tok, H_A, DK))
        v = v.reshape(bsz, n_tok, H_A, DV)
        beta = jax.nn.sigmoid(b_raw).reshape(bsz, n_tok, 2, H_A)
        g = -jnp.exp(a_log[l].astype(f32)) * jax.nn.softplus(a_raw.reshape(bsz, n_tok, 2, H_A) + dt_bias[l].astype(f32))
        s0 = st_delta.astype(f32)
        rev = lambda t: jnp.flip(t, axis=1)
        o_f, s_f = gated_delta_chunked(q, k, v, beta[:, :, 0], g[:, :, 0], s0[:, 0])
        o_b, s_b = gated_delta_chunked(rev(q), rev(k), rev(v), rev(beta[:, :, 1]), rev(g[:, :, 1]), s0[:, 1])
        o = rmsnorm(o_f + rev(o_b), dn_norm[l]) * jax.nn.silu(z.reshape(bsz, n_tok, H_A, DV))
        y_a = o.reshape(bsz, n_tok, H_A * DV) @ w_br_a[l].astype(f32)
        ug = u.reshape(bsz, n_tok, S5_G, S5_P)
        y_f, hf_re, hf_im = s5_direction(ug, st_re[:, 0], st_im[:, 0], s5_a_re[l, 0], s5_a_im[l, 0], s5_log_dt[l, 0],
                                         s5_b_re[l, 0], s5_b_im[l, 0], s5_c_re[l, 0], s5_c_im[l, 0], False)
        y_r, hb_re, hb_im = s5_direction(ug, st_re[:, 1], st_im[:, 1], s5_a_re[l, 1], s5_a_im[l, 1], s5_log_dt[l, 1],
                                         s5_b_re[l, 1], s5_b_im[l, 1], s5_c_re[l, 1], s5_c_im[l, 1], True)
        y_s = jax.nn.gelu((y_f + y_r + s5_d[l].astype(f32) * ug).reshape(bsz, n_tok, S5_W))
        y_s = y_s * jax.nn.sigmoid(y_s @ w_glu[l].astype(f32) + b_glu[l].astype(f32))
        y_b = y_s @ w_br_b[l].astype(f32)
        merged = jax.nn.sigmoid(gate_a) * y_a + jax.nn.sigmoid(gate_b) * y_b
        out = merged @ w_out[l].astype(f32)
        return (out, jnp.stack([s_f, s_b], axis=1),
                jnp.stack([hf_re, hb_re], axis=1), jnp.stack([hf_im, hb_im], axis=1))

    def modulation(cond, l):
        return jax.nn.silu(cond.astype(f32)) @ w_ada[l].astype(f32) + b_ada[l].astype(f32)

    def layer(x, mod, l, st_delta, st_re, st_im):
        sh1, sc1, gt1, sh2, sc2, gt2 = jnp.split(mod, 6, axis=-1)
        hn = rmsnorm(x, norm1[l]) * (1.0 + sc1) + sh1
        y, sd, sr, si = mixer(hn, l, st_delta, st_re, st_im)
        x = x + gt1 * y
        hn = rmsnorm(x, norm2[l]) * (1.0 + sc2) + sh2
        gate, up = jnp.split(hn @ w_gu[l].astype(f32), 2, axis=-1)
        x = x + gt2 * ((jax.nn.silu(gate) * up) @ w_down[l].astype(f32))
        return x, sd, sr, si

    xp = x_prompt.astype(f32)
    bp = xp.shape[0]
    zero_delta = jnp.zeros((bp, 2, H_A, DK, DV), f32)
    zero_s5 = jnp.zeros((bp, 2, S5_G, S5_N), f32)
    sd_list, sr_list, si_list = [], [], []
    for l in range(DEPTH):
        xp, sd, sr, si = layer(xp, modulation(c_ctx, l)[None, None, :], l, zero_delta, zero_s5, zero_s5)
        sd_list.append(sd)
        sr_list.append(sr)
        si_list.append(si)
    y_prompt = rmsnorm(xp, norm_f).astype(x_prompt.dtype)
    new_state_delta = jnp.stack(sd_list, axis=1).astype(x_prompt.dtype)
    new_state_s5_re = jnp.stack(sr_list, axis=1).astype(x_prompt.dtype)
    new_state_s5_im = jnp.stack(si_list, axis=1).astype(x_prompt.dtype)

    rows = x_sample.shape[1] // GRID_W
    xs = x_sample.astype(f32) + grid_pos_embed(rows)[None]
    for l in range(DEPTH):
        xs, _, _, _ = layer(xs, modulation(c, l)[:, None, :], l,
                            state_delta[:, l], state_s5_re[:, l], state_s5_im[:, l])
    y_sample = rmsnorm(xs, norm_f).astype(x_sample.dtype)

    return (y_prompt, y_sample, new_state_delta, new_state_s5_re, new_state_s5_im)


_drawn_inputs = setup_inputs


def setup_inputs(seed=0):
    import zlib

    import numpy as np

    out = dict(_drawn_inputs(seed))
    spreads = {}
    factors = {'state_delta': 8.0,
     'state_s5_re': 27.18,
     'state_s5_im': 27.493,
     'dn_norm': 24.647,
     's5_a_re': 200.0,
     's5_c_re': 27.311,
     's5_c_im': 26.3,
     'w_glu': 2.969,
     'b_glu': 200.0,
     'norm2': 8.0,
     'norm_f': 25.581}
    for name, (base, spread) in spreads.items():
        noise = np.random.default_rng([zlib.crc32(name.encode()), seed]).standard_normal(out[name].shape)
        drawn = base * np.exp(spread * noise) if base else spread * noise
        out[name] = __import__('jax').numpy.asarray(drawn.astype(out[name].dtype))
    for name, factor in factors.items():
        out[name] = (out[name] * factor).astype(out[name].dtype)
    return out
```

```python
from contextlib import ExitStack

import numpy as np
import concourse.bass as bass
from concourse import mybir

F32 = mybir.dt.float32
BF16 = mybir.dt.bfloat16
ALU = mybir.AluOpType
ACT = mybir.ActivationFunctionType

P = 128
D = 1024
KT = D // P
NS, NP_ = 1024, 256
T = NS + NP_
CHUNKS = ((0, 512), (512, 512), (1024, 256))
SEGS = ((0, NS, 0), (NS, NP_, 1))
GRID_W = 64
EPS = 1e-6
H = 8
DK = 128
C = 64
NC_S, NC_P = NS // C, NP_ // C
NPACK = NC_S + NC_P
QKV = 3 * H * DK
Z0 = QKV
B0 = Z0 + H * DK
A0 = B0 + 2 * H
U0 = A0 + 2 * H
GA0 = U0 + D
GB0 = GA0 + D
IN_DIM = GB0 + D
D_FF = 2816
FT = D_FF // P
CONV_W = 5
PADW = T + 2 * CONV_W - 2
LEVELS = 6
G_S5, N_S5, P_S5 = 64, 64, 16
L5 = 8
NC5_S, NC5_P = NS // L5, NP_ // L5
NC5 = NC5_S + NC5_P
GB = 4


class Names:
    pass


def constants():
    c = {}
    c["ident"] = np.eye(P, dtype=np.float32)
    quarter = D // 4
    omega = (1.0 / (np.float32(10000.0) ** (np.arange(quarter, dtype=np.float32) / np.float32(quarter)))).astype(np.float32)
    r = np.arange(NS // GRID_W, dtype=np.float32)[None, :] * omega[:, None]
    col = np.arange(GRID_W, dtype=np.float32)[None, :] * omega[:, None]
    rows = np.concatenate([np.sin(r), np.cos(r)], 0).astype(np.float32)
    cols = np.concatenate([np.sin(col), np.cos(col)], 0).astype(np.float32)
    c["pos_row"] = rows.reshape(4, P, -1).transpose(1, 0, 2).copy()
    c["pos_col"] = cols.reshape(4, P, -1).transpose(1, 0, 2).copy()
    i = np.arange(C)
    lvl = np.zeros((LEVELS, 2, C, 2, C), np.float32)
    for l in range(LEVELS):
        same = (i[:, None] >> (l + 1)) == (i[None, :] >> (l + 1))
        up, lo = (i >> l) & 1 == 1, (i >> l) & 1 == 0
        lvl[l, 0, :, 0] = same & up[:, None] & lo[None, :]
        lvl[l, 1, :, 1] = same & lo[:, None] & up[None, :]
    c["level"] = lvl.reshape(LEVELS, P, P).transpose(1, 0, 2).copy()
    c["level0_t"] = lvl[0].reshape(P, P).T.copy()
    seen = np.stack([i[None, :] >= i[:, None], i[None, :] <= i[:, None]])
    c["seen"] = np.where(seen, np.float32(1e30), np.float32(-1e30)).reshape(P, C).astype(np.float32)
    m = np.ones((2 * 32, T), np.float32)
    m[:, ::C] = 0.0
    c["restart"] = m
    sel = np.zeros((64, H, 2, C), np.float32)
    for h in range(H):
        sel[h, h, 0], sel[32 + h, h, 1] = 1.0, 1.0
    c["pick_head"] = sel.reshape(64, H, P)
    return c


CONST_SHAPES = {k: v.shape for k, v in constants().items()}


def setup(nc, ins, outs, consts, ctx):
    K = Names()
    K.nc, K.i, K.o, K.c = nc, ins, outs, consts

    def sb(name, shape, dt=F32, stack=ctx):
        return stack.enter_context(nc.sbuf_tensor(name, list(shape), dt))

    def ps(name, shape, stack):
        return stack.enter_context(nc.psum_tensor(name, list(shape), F32))

    K.phase_sems = []

    def sem(name):
        K.phase_sems.append(nc.alloc_semaphore(name=name))
        return K.phase_sems[-1]

    K.sb, K.ps, K.sem = sb, ps, sem
    K.hn = sb("hn", [P, 2, KT, T], BF16)
    K.w_raw = sb("w_raw", [P, 2, KT, P])
    K.w_pair = sb("w_pair", [P, 2, 2, KT, P], BF16)
    K.ident = sb("ident", [P, P])
    K.ones = sb("ones", [P, P])
    K.eps = sb("eps", [P, 1])
    K.mod = sb("mod", [P, 6 * KT, 2])
    K.vec = sb("vec", [P, 7 * KT + 1])
    K.conv_w = sb("conv_w_t", [P, CONV_W * 3 * H])
    K.norm_g = [K.vec[:, j * KT:(j + 1) * KT] for j in (2, 3, 4)]
    K.b_glu = K.vec[:, 5 * KT:6 * KT]
    K.s5_d = K.vec[:, 6 * KT:7 * KT]
    K.dn_norm = K.vec[:, 7 * KT:7 * KT + 1]
    K.mul1 = sb("mul1", [P, KT, 2])
    K.mul2 = sb("mul2", [P, KT, 2])
    K.w_loaded = [sem("w_loaded_0"), sem("w_loaded_1")]
    K.w_high = sem("w_high")
    K.w_low = sem("w_low")
    K.tile_done = sem("tile_done")
    K.tile_read = [sem("tile_read_0"), sem("tile_read_1")]
    K.pulse = sem("pulse")
    K.scratch_x = nc.dram_tensor("scratch_x", [P, KT, T], F32, kind="Internal").ap()
    K.scratch_o = nc.dram_tensor("scratch_o", [H, P, 2, T], BF16, kind="Internal").ap()
    K.scratch_u = nc.dram_tensor("scratch_u", [KT, P, L5, NC5], F32, kind="Internal").ap()
    K.scratch_y = nc.dram_tensor("scratch_y", [KT, P, L5, NC5], F32, kind="Internal").ap()
    K.q = 0
    K.phase_sems.clear()
    return K


def end_phase(K):
    K.nc.clear_and_free_semaphores(K.phase_sems)
    K.phase_sems.clear()
    K.nc.all_engine_barrier()



def load_tile(K, sync, q, slot, src, kt=KT):
    sync.wait_ge(K.w_low, 2 * q + slot + 1)
    sync.sem_inc(K.pulse, 1)
    sync.dma_start(K.w_raw[:, slot, 0:kt, :], src.rearrange("(k p) c -> p k c", p=P)).then_inc(K.w_loaded[slot], 16)


def split_high(K, act, q, slot, kt=KT):
    act.wait_ge(K.w_loaded[slot], (q + 1) * 16)
    act.wait_ge(K.tile_done, 2 * q + slot + 1)
    act.activation(K.w_pair[:, slot, 0, 0:kt, :], K.w_raw[:, slot, 0:kt, :], ACT.Copy).then_inc(K.w_high, 1)


def split_low(K, pool, q, slot, kt=KT):
    pool.wait_ge(K.w_high, 2 * q + slot + 1)
    pool.tensor_tensor(K.w_pair[:, slot, 1, 0:kt, :], K.w_raw[:, slot, 0:kt, :], K.w_pair[:, slot, 0, 0:kt, :],
                       ALU.subtract).then_inc(K.w_low, 1)


def multiply_tile(K, pe, q, slot, out, x, kt=KT):
    pe.wait_ge(K.w_low, 2 * q + slot + 3)
    pe.wait_ge(K.tile_read[slot], q + 1)
    last = (kt - 1, 1, 0)
    for k in range(kt):
        for w, a in ((0, 0), (0, 1), (1, 0)):
            for c0, cn in CHUNKS:
                mm = pe.matmul(out[:, c0:c0 + cn], K.w_pair[:, slot, w, k, :], x[:, a, k, c0:c0 + cn],
                               start=(k, w, a) == (0, 0, 0), stop=(k, w, a) == last)
    mm.then_inc(K.tile_done, 1)


def wait_tile(K, eng, q, slot):
    eng.wait_ge(K.tile_done, 2 * q + slot + 3)



def phase_input(K):
    nc = K.nc
    with ExitStack() as outer, ExitStack() as st:
        x = K.sb("x_t", [P, KT, T], stack=outer)
        vrow = K.sb("vec_rows", [7 * KT + 1, P], stack=st)
        crow = K.sb("conv_rows", [CONV_W * 3 * H, P], stack=st)
        cond_s = K.sb("cond_s", [P, KT, 2], stack=st)
        HALF = 3 * D
        w = K.sb("w_ada_rows", [P, 2, HALF], stack=st)
        bias = K.sb("b_ada_rows", [2, 6 * D], stack=st)
        row = K.sb("mod_rows", [2, 6 * D], stack=st)
        tok = K.sb("x_rows", [P, 2, D], stack=st)
        pr = K.sb("pos_row_t", [P, 4, NS // GRID_W], stack=st)
        pc = K.sb("pos_col_t", [P, 4, GRID_W], stack=st)
        acc = K.ps("mod_acc", [P, 6, 512], st)
        tr = K.ps("tr", [P, 2, 512], st)
        s_small, s_cond, s_silu, s_w = K.sem("in_small"), K.sem("in_cond"), K.sem("in_silu"), [K.sem("in_w_0"), K.sem("in_w_1")]
        s_bias, s_pc, s_vt, s_vec = K.sem("in_bias"), K.sem("in_pos"), K.sem("vec_turned"), K.sem("vec_done")
        s_modk, s_modrow, s_modt = K.sem("mod_k_done"), K.sem("mod_row_done"), K.sem("mod_t_done")
        s_x, s_tr, s_trr, s_trd = [K.sem("x_in_0"), K.sem("x_in_1")], K.sem("x_turned"), K.sem("x_read_dve"), K.sem("x_spill")
        s_ones = K.sem("ones_done")
        s_modc = K.sem("mod_copied")
        NT = T // P

        with nc.Block() as block:
            @block.sync
            def _(sync):
                flat = {"c": K.i["c"][0], "c_ctx": K.i["c_ctx"], "norm1": K.i["norm1"][0], "norm2": K.i["norm2"][0],
                        "norm_f": K.i["norm_f"], "b_glu": K.i["b_glu"][0], "s5_d": K.i["s5_d"][0].rearrange("g p -> (g p)")}
                for j, v in enumerate(flat.values()):
                    sync.dma_start(vrow[j * KT:(j + 1) * KT, :], v.rearrange("(k p) -> k p", p=P)).then_inc(s_cond, 16)
                sync.dma_start(vrow[7 * KT:7 * KT + 1, :], K.i["dn_norm"]).then_inc(s_cond, 16)
                for j in range(CONV_W):
                    sync.dma_start(crow[j * 3 * H:(j + 1) * 3 * H, :], K.i["conv_w"][0, j].rearrange("(t p) -> t p", p=P)).then_inc(s_cond, 16)
                sync.dma_start(K.ident[:, :], K.c["ident"]).then_inc(s_small, 16)
                sync.dma_start(pr[:, :, :], K.c["pos_row"]).then_inc(s_pc, 16)
                sync.dma_start(pc[:, :, :], K.c["pos_col"]).then_inc(s_pc, 16)
                for half in range(2):
                    for k in range(KT):
                        n = half * KT + k
                        if n >= 2:
                            sync.wait_ge(s_modk, n - 1)
                        sync.dma_start(w[:, n % 2, :], K.i["w_ada"][0, k * P:(k + 1) * P, half * HALF:(half + 1) * HALF]).then_inc(s_w[n % 2], 16)

            @block.gpsimd
            def _(pool):
                pool.memset(K.ones[:, :], 1.0).then_inc(s_ones, 1)
                pool.memset(K.eps[:, :], EPS).then_inc(s_ones, 1)
                for c in range(2):
                    pool.dma_start(bias[c:c + 1, :], K.i["b_ada"]).then_inc(s_bias, 16)
                for s, n in ((K.w_low, 2), (K.tile_done, 2), (K.tile_read[0], 1), (K.tile_read[1], 1)):
                    pool.sem_inc(s, n)
                for t in range(NT):
                    if t >= 2:
                        pool.wait_ge(s_tr, 2 * (t - 1))
                    src = K.i["x_sample"][0, t * P:(t + 1) * P] if t < NS // P else K.i["x_prompt"][0, t * P - NS:(t + 1) * P - NS]
                    pool.dma_start(tok[:, t % 2, :], src).then_inc(s_x[t % 2], 16)
                pool.wait_ge(s_trr, 2 * NT)
                pool.dma_start(K.scratch_x, x[:, :, :]).then_inc(s_trd, 16)
                pool.wait_ge(s_trd, 16)

            @block.tensor
            def _(pe):
                pe.wait_ge(s_small, 16)
                pe.wait_ge(s_cond, 16 * 13)
                pe.transpose(tr[:, 0, 0:7 * KT + 1], vrow[:, :], K.ident[0:7 * KT + 1, 0:7 * KT + 1])
                pe.transpose(tr[:, 1, 0:CONV_W * 3 * H], crow[:, :], K.ident[0:120, 0:120]).then_inc(s_vt, 1)
                pe.wait_ge(s_vec, 1)
                for t in range(NT):
                    pe.wait_ge(s_x[t % 2], 16 * (t // 2 + 1))
                    for half in range(2):
                        n = 2 * t + half
                        if n >= 2:
                            pe.wait_ge(s_trr, n - 1)
                        for k in range(4):
                            c = (half * 4 + k) * P
                            mm = pe.transpose(tr[:, n % 2, k * P:(k + 1) * P], tok[:, t % 2, c:c + P], K.ident[:, :])
                        mm.then_inc(s_tr, 1)
                pe.wait_ge(s_silu, 1)
                for half in range(2):
                    if half:
                        pe.wait_ge(s_modrow, 6)
                    for k in range(KT):
                        n = half * KT + k
                        pe.wait_ge(s_w[n % 2], 16 * (n // 2 + 1))
                        for j in range(6):
                            mm = pe.matmul(acc[0:2, j, :], cond_s[:, k, :], w[:, n % 2, j * 512:(j + 1) * 512],
                                           start=k == 0, stop=k == KT - 1)
                        mm.then_inc(s_modk, 1)
                pe.wait_ge(s_modrow, 12)
                pe.wait_ge(s_trr, 2 * NT)
                for j in range(6 * KT):
                    mm = pe.transpose(tr[:, 0, 2 * j:2 * j + 2], row[0:2, j * P:(j + 1) * P], K.ident[0:2, 0:2])
                mm.then_inc(s_modt, 1)

            @block.scalar
            def _(act):
                act.wait_ge(s_vec, 1)
                for c in range(2):
                    i = act.activation(cond_s[:, :, c], K.vec[:, c * KT:(c + 1) * KT], ACT.Silu)
                i.then_inc(s_silu, 1)

            @block.vector
            def _(dve):
                dve.wait_ge(s_vt, 1)
                dve.tensor_copy(K.vec[:, :], tr[:, 0, 0:7 * KT + 1])
                dve.tensor_copy(K.conv_w[:, :], tr[:, 1, 0:CONV_W * 3 * H]).then_inc(s_vec, 1)
                dve.wait_ge(s_pc, 32)
                for t in range(NT):
                    for half in range(2):
                        n = 2 * t + half
                        dve.wait_ge(s_tr, n + 1)
                        dst = x[:, half * 4:half * 4 + 4, t * P:(t + 1) * P]
                        src = tr[:, n % 2, :]
                        if t < NS // P:
                            dst = dst.rearrange("p k (r c) -> p k r c", c=GRID_W)
                            src = src.rearrange("p (k r c) -> p k r c", k=4, c=GRID_W)
                            rows = P // GRID_W
                            if half == 0:
                                pos = pr[:, :, t * rows:(t + 1) * rows].unsqueeze(3).to_broadcast([P, 4, rows, GRID_W])
                            else:
                                pos = pc[:, :, :].unsqueeze(2).to_broadcast([P, 4, rows, GRID_W])
                            for r in range(rows):
                                i = dve.tensor_tensor(dst[:, :, r, :], src[:, :, r, :], pos[:, :, r, :], ALU.add)
                            i.then_inc(s_trr, 1)
                        else:
                            dve.tensor_copy(dst, src.rearrange("p (k c) -> p k c", k=4)).then_inc(s_trr, 1)
                dve.wait_ge(s_bias, 32)
                for half in range(2):
                    dve.wait_ge(s_modk, KT * (half + 1))
                    for j in range(6):
                        c = half * HALF + j * 512
                        dve.tensor_tensor(row[:, c:c + 512], acc[0:2, j, :], bias[:, c:c + 512], ALU.add).then_inc(s_modrow, 1)
                dve.wait_ge(s_modt, 1)
                dve.tensor_copy(K.mod[:, :, :], tr[:, 0, 0:12 * KT].rearrange("p (j c) -> p j c", c=2)).then_inc(s_modc, 1)
                dve.wait_ge(s_modc, 1)
                for m, j, s in ((K.mul1, 0, 1), (K.mul2, 1, 4)):
                    for c in range(2):
                        dve.tensor_tensor(m[:, :, c], K.norm_g[j], K.mod[:, s * KT:(s + 1) * KT, c], ALU.mult)
                dve.drain()
                for m, j in ((K.mul1, 0), (K.mul2, 1)):
                    for c in range(2):
                        dve.tensor_tensor(m[:, :, c], m[:, :, c], K.norm_g[j], ALU.add)

        st.close()
        norm_modulate(K, outer, x, K.mul1, 0, "n1")


def rstd_stages(K, st, x, name):
    sq = K.sb(name + "_sq", [P, 2, T], stack=st)
    ss = K.ps(name + "_ss", [P, 1536], st)
    rstd = K.sb(name + "_rstd", [P, T], stack=st)
    s_sq, s_k, s_r = K.sem(name + "_squared"), K.sem(name + "_summed"), K.sem(name + "_rstd_done")

    def act_part(act):
        for k in range(KT):
            if k >= 2:
                act.wait_ge(s_k, k - 1)
            act.activation(sq[:, k % 2, :], x[:, k, :], ACT.Square).then_inc(s_sq, 1)
        act.wait_ge(s_k, KT)
        act.activation(rstd[:, :], ss[:, 0:T], ACT.Ln, scale=1.0 / D, bias=K.eps[:, :])
        act.drain()
        act.activation(rstd[:, :], rstd[:, :], ACT.Exp, scale=-0.5).then_inc(s_r, 1)

    def pe_part(pe):
        for k in range(KT):
            pe.wait_ge(s_sq, k + 1)
            for c0, cn in CHUNKS:
                mm = pe.matmul(ss[:, c0:c0 + cn], K.ones[:, :], sq[:, k % 2, c0:c0 + cn], start=k == 0, stop=k == KT - 1)
            mm.then_inc(s_k, 1)

    return act_part, pe_part, rstd, s_r


def norm_modulate(K, st, x, mul, shift, name):
    t = K.sb(name + "_t", [P, 2, T], stack=st)
    act_part, pe_part, rstd, s_r = rstd_stages(K, st, x, name)
    s_h, s_hi, s_lo = K.sem(name + "_hn"), K.sem(name + "_high"), K.sem(name + "_low")
    with K.nc.Block() as block:
        @block.scalar
        def _(act):
            act_part(act)
            for k in range(KT):
                act.wait_ge(s_h, k + 1)
                act.activation(K.hn[:, 0, k, :], t[:, k % 2, :], ACT.Copy).then_inc(s_hi, 1)

        @block.tensor
        def _(pe):
            pe_part(pe)

        @block.vector
        def _(dve):
            dve.wait_ge(s_r, 1)
            for k in range(KT):
                dve.tensor_tensor(t[:, k % 2, :], x[:, k, :], rstd[:, :], ALU.mult)
                dve.drain()
                for a, n, c in SEGS:
                    i = dve.tensor_scalar(t[:, k % 2, a:a + n], t[:, k % 2, a:a + n], mul[:, k, c:c + 1],
                                          K.mod[:, shift * KT + k, c:c + 1], ALU.mult, ALU.add)
                i.then_inc(s_h, 1)
                dve.wait_ge(s_h, k + 1)
                dve.wait_ge(s_hi, k + 1)
                dve.tensor_tensor(K.hn[:, 1, k, :], t[:, k % 2, :], K.hn[:, 0, k, :], ALU.subtract).then_inc(s_lo, 1)
                dve.wait_ge(s_lo, k + 1)



def phase_decays(K, outer):
    rows = ((0, 0), (1, 32))
    K.cum_row = K.sb("cum_row", [64, NPACK, C], stack=outer)
    K.beta = K.sb("beta", [P, H, NPACK], stack=outer)
    K.neg_beta = K.sb("neg_beta", [P, H, NPACK], stack=outer)
    K.cum = K.sb("cum", [P, H, NPACK], stack=outer)
    K.gamma = K.sb("gamma", [P, H, NPACK], stack=outer)
    K.to_end = K.sb("to_end", [P, H, NPACK], stack=outer)
    K.carry = K.sb("carry", [P, 2, H, NPACK], stack=outer)
    with ExitStack() as st:
        w = K.sb("w_ba", [P, KT, 4 * H], stack=st)
        wp = K.sb("w_ba_pair", [P, 2, 2, KT, 64], BF16, stack=st)
        restart = K.sb("restart_t", [64, T], stack=st)
        par = K.sb("decay_par", [64, 2], stack=st)
        neg_a = K.sb("neg_a", [64, 1], stack=st)
        b_row = K.sb("b_row", [64, T], stack=st)
        s_row = K.sb("s_row", [64, T], stack=st)
        e_row = K.sb("e_row", [64, T], stack=st)
        c_row = K.sb("c_row", [64, T], stack=st)
        b_dup = K.sb("b_dup", [64, NPACK, 2, C], stack=st)
        c_dup = K.sb("c_dup", [64, NPACK, 2, C], stack=st)
        end = K.sb("end_rows", [64, NPACK], stack=st)
        diag = K.sb("end_diag", [64, 64, NPACK], stack=st)
        tmp = K.sb("to_end_log", [P, H, NPACK], stack=st)
        pb = K.ps("pb", [P, 1536], st)
        pa = K.ps("pa", [P, 1536], st)
        s_in, s_par, s_z, s_wh, s_wl = (K.sem("ba_" + n) for n in ("in", "par", "zeroed", "high", "low"))
        s_mm, s_act, s_dve, s_tr, s_pool = (K.sem("ba_" + n) for n in ("products", "act", "dve", "turned", "dup"))
        col = lambda x, j: x[:, 2 * H * j + 0:2 * H * (j + 1)]

        def segments():
            return ((0, NC_S), (NC_S, NC_P))

        with K.nc.Block() as block:
            @block.sync
            def _(sync):
                sync.dma_start(w[:, :, :], K.i["w_in"][0, :, B0:B0 + 4 * H].rearrange("(k p) c -> p k c", p=P)).then_inc(s_in, 16)
                sync.dma_start(restart[:, :], K.c["restart"]).then_inc(s_in, 16)
                sync.wait_ge(s_z, 1)
                with K.nc.allow_non_contiguous_dma(reason="32 values"):
                    for j, name in enumerate(("dt_bias", "a_log")):
                        for d, r in rows:
                            sync.dma_start(par[r:r + H, j:j + 1], K.i[name][0, d].rearrange("(h o) -> h o", o=1)).then_inc(s_par, 16)

            @block.gpsimd
            def _(pool):
                pool.memset(par[:, :], 0.0).then_inc(s_z, 1)
                pool.memset(wp[:, :, :, :, :], 0.0).then_inc(s_z, 1)
                pool.wait_ge(s_wh, 4)
                for j in range(2):
                    for d, r in rows:
                        s = w[:, :, 2 * H * j + H * d:2 * H * j + H * (d + 1)]
                        i = pool.tensor_tensor(wp[:, j, 1, :, r:r + H], s, wp[:, j, 0, :, r:r + H], ALU.subtract)
                i.then_inc(s_wl, 1)

            @block.tensor
            def _(pe):
                pe.wait_ge(s_wl, 1)
                for j, out in ((0, pb), (1, pa)):
                    for k in range(KT):
                        for v, a in ((0, 0), (0, 1), (1, 0)):
                            for c0, cn in CHUNKS:
                                mm = pe.matmul(out[0:64, c0:c0 + cn], wp[:, j, v, k, :], K.hn[:, a, k, c0:c0 + cn],
                                               start=(k, v, a) == (0, 0, 0), stop=(k, v, a) == (KT - 1, 1, 0))
                    mm.then_inc(s_mm, 1)
                pe.wait_ge(s_pool, 1)
                for t in range(NPACK):
                    mm = pe.transpose(pb[:, t * 64:(t + 1) * 64], b_dup[:, t, :, :], K.ident[0:64, 0:64])
                mm.then_inc(s_tr, 1)
                pe.wait_ge(s_dve, 6)
                for t in range(NPACK):
                    mm = pe.transpose(pa[:, t * 64:(t + 1) * 64], c_dup[:, t, :, :], K.ident[0:64, 0:64])
                mm.then_inc(s_tr, 1)
                pe.wait_ge(s_dve, 8)
                flat = diag[:, :, :].rearrange("p r t -> p (r t)")
                for c0, cn in CHUNKS:
                    mm = pe.matmul(pb[:, c0:c0 + cn], K.ones[0:64, :], flat[:, c0:c0 + cn], start=True, stop=True)
                mm.then_inc(s_tr, 1)

            @block.scalar
            def _(act):
                act.wait_ge(s_in, 32)
                act.wait_ge(s_z, 2)
                for j in range(2):
                    for d, r in rows:
                        act.activation(wp[:, j, 0, :, r:r + H], w[:, :, 2 * H * j + H * d:2 * H * j + H * (d + 1)], ACT.Copy).then_inc(s_wh, 1)
                act.wait_ge(s_mm, 1)
                act.activation(b_row[:, :], pb[0:64, 0:T], ACT.Sigmoid)
                act.drain()
                for d, r in rows:
                    for t0, tn in segments():
                        src = b_row[r:r + 32, :].rearrange("p (t c) -> p t c", c=C)[:, t0:t0 + tn]
                        src = src[:, ::-1] if d else src
                        for u in range(2):
                            i = act.activation(b_dup[r:r + 32, t0:t0 + tn, u, :], src, ACT.Copy)
                i.then_inc(s_pool, 1)
                act.wait_ge(s_dve, 2)
                act.activation(e_row[:, :], s_row[:, :], ACT.Abs)
                act.activation(neg_a[:, :], par[:, 1:2], ACT.Exp)
                act.drain()
                act.activation(e_row[:, :], e_row[:, :], ACT.Exp, scale=-1.0)
                act.drain()
                act.activation(e_row[:, :], e_row[:, :], ACT.Ln, bias=K.ones[0:64, 0:1]).then_inc(s_act, 1)
                act.wait_ge(s_dve, 9)
                act.activation(K.gamma[:, :, :], K.cum[:, :, :], ACT.Exp)
                act.activation(K.to_end[:, :, :], tmp[:, :, :], ACT.Exp)
                g = pb[:, 0:T].rearrange("p (r t) -> p r t", t=NPACK)
                for d, r in rows:
                    act.activation(K.carry[:, d, :, :], g[:, r:r + H, :], ACT.Exp)

            @block.vector
            def _(dve):
                dve.wait_ge(s_par, 64)
                dve.wait_ge(s_mm, 2)
                dve.tensor_scalar(s_row[:, :], pa[0:64, 0:T], par[:, 0:1], None, ALU.add).then_inc(s_dve, 2)
                dve.wait_ge(s_act, 1)
                dve.scalar_tensor_tensor(out=s_row[:, :], in0=s_row[:, :], scalar=0.0, in1=e_row[:, :], op0=ALU.max, op1=ALU.add)
                dve.drain()
                dve.tensor_scalar(s_row[:, :], s_row[:, :], neg_a[:, :], -1.0, ALU.mult, ALU.mult)
                dve.drain()
                dve.tensor_tensor_scan(c_row[0:32, :], restart[0:32, :], s_row[0:32, :], 0.0, ALU.mult, ALU.add)
                dve.tensor_tensor_scan(c_row[32:64, ::-1], restart[32:64, :], s_row[32:64, ::-1], 0.0, ALU.mult, ALU.add)
                dve.drain()
                for d, r in rows:
                    for t0, tn in segments():
                        src = c_row[r:r + 32, :].rearrange("p (t c) -> p t c", c=C)[:, t0:t0 + tn]
                        src = src[:, ::-1] if d else src
                        dve.tensor_copy(K.cum_row[r:r + 32, t0:t0 + tn, :], src)
                        for u in range(2):
                            i = dve.tensor_copy(c_dup[r:r + 32, t0:t0 + tn, u, :], src)
                dve.drain().then_inc(s_dve, 4)
                dve.tensor_copy(end[0:32, :], K.cum_row[0:32, :, C - 1])
                dve.tensor_copy(end[32:64, :], K.cum_row[32:64, :, 0])
                dve.drain()
                dve.tensor_tensor(diag[:, :, :], end[:, :].unsqueeze(1).to_broadcast([64, 64, NPACK]),
                                  K.ident[0:64, 0:64].unsqueeze(2).to_broadcast([64, 64, NPACK]), ALU.mult)
                dve.wait_ge(s_tr, 2)
                for out, src in ((K.beta, pb), (K.cum, pa)):
                    v = src[:, 0:T].rearrange("p (t r) -> p r t", r=64)
                    for d, r in rows:
                        i = dve.tensor_copy(out[64 * d:64 * d + 64, :, :], v[64 * d:64 * d + 64, r:r + H, :])
                i.then_inc(s_dve, 2)
                dve.wait_ge(s_dve, 8)
                dve.tensor_scalar(K.neg_beta[:, :, :], K.beta[:, :, :], -1.0, None, ALU.mult)
                dve.wait_ge(s_tr, 3)
                g = pb[:, 0:T].rearrange("p (r t) -> p r t", t=NPACK)
                for d, r in rows:
                    i = dve.tensor_tensor(tmp[64 * d:64 * d + 64, :, :], g[64 * d:64 * d + 64, r:r + H, :], K.cum[64 * d:64 * d + 64, :, :], ALU.subtract)
                i.then_inc(s_dve, 1)


D_USES, S_USES = 148, 54
STEPS = [t for p in zip(range(NC_P), range(NC_S, NPACK)) for t in p] + list(range(NC_P, NC_S))
SEQ_END = {NC_S - 1, NPACK - 1}


def phase_heads(K, outer):
    nc = K.nc
    with ExitStack() as st:
        SLOT = 2 * PADW
        big = lambda name: K.sb(name, [P, SLOT if name in ("xi", "xti", "vi", "kd") else NPACK * P], stack=st)
        pack = lambda t: t[:, 0:NPACK * P].rearrange("p (t c) -> p t c", c=P)
        kp_, qp_, at_, mt_, x_, xt_, v_, vt_, gk_, kd_ = (big(n) for n in ("kp", "qp", "at", "mt", "xi", "xti", "vi", "vt", "gk", "kd"))
        kp, qp, at, mt, xi, xti, vi, vt, gk, kd = (pack(t) for t in (kp_, qp_, at_, mt_, x_, xt_, v_, vt_, gk_, kd_))
        op = gk
        uv, wk = vi, xi
        two = lambda t: t[:, :].rearrange("p (a c) -> p a c", a=2)
        raw, cv, silu, sq = two(x_), two(xt_), two(v_), two(kd_)
        dt = K.sb("dt", [P, NPACK, C], stack=st)
        dtb = K.sb("dtb", [P, NPACK, C], stack=st)
        zs = K.sb("zs", [P, T], stack=st)
        os_ = K.sb("os", [P, 2, PADW], stack=st)
        opair = K.sb("o_pair", [P, 2, T], BF16, stack=st)
        state = K.sb("state", [P, 2, 2, P], stack=st)
        u = K.sb("u", [P, 2, 2, P], stack=st)
        tq = K.sb("tq", [P, 2, P], stack=st)
        hs = K.sb("head_scalars", [P, 5, NPACK], stack=st)
        hc = K.sb("head_carry", [P, 2, NPACK], stack=st)
        hw = K.sb("head_conv", [P, CONV_W, 3], stack=st)
        pick_h = K.sb("pick_h", [64, P], stack=st)
        level = K.sb("level_t", [P, LEVELS, P], stack=st)
        level0_t = K.sb("level0_t_t", [P, P], stack=st)
        seen = K.sb("seen_t", [P, C], stack=st)
        bank = K.ps("bank", [P, 8, 512], st)
        gemm_out = [bank[:, 3 * s:3 * s + 3, :].rearrange("p b c -> p (b c)") for s in range(2)]
        s = Names()
        s.consts = K.sem("h_consts")
        s.head_end = K.sem("h_head_end")
        s.state_in = K.sem("h_state_in")
        s.pick_in = K.sem("h_pick_in")
        s.pads = K.sem("h_pads")
        s.conv = K.sem("h_conv")
        s.silu = K.sem("h_silu")
        s.squared = K.sem("h_squared")
        s.inv_norm = K.sem("h_inv_norm")
        s.packed = K.sem("h_packed")
        s.turned_packs = K.sem("h_turned_packs")
        s.scal = K.sem("h_scal")
        s.full_d = K.sem("h_full_d")
        s.free_d = K.sem("h_free_d")
        s.full_s = K.sem("h_full_s")
        s.free_s = K.sem("h_free_s")
        s.dt_log = K.sem("h_dt_log")
        s.dt = K.sem("h_dt")
        s.dtb = K.sem("h_dtb")
        s.mt = K.sem("h_mt")
        s.inv = K.sem("h_inv")
        s.vmask = K.sem("h_vmask")
        s.tok_v = K.sem("h_tok_v")
        s.wkt = K.sem("h_wkt")
        s.u = K.sem("h_u")
        s.state_new = K.sem("h_state_new")
        s.o_add = K.sem("h_o_add")
        s.o_sum = K.sem("h_o_sum")
        s.o_sq = K.sem("h_o_sq")
        s.o_rstd = K.sem("h_o_rstd")
        s.o_fin = K.sem("h_o_fin")
        s.o_high = K.sem("h_o_high")
        s.o_low = K.sem("h_o_low")
        s.o_store = K.sem("h_o_store")
        s.s_store = K.sem("h_s_store")
        s.state_zero = K.sem("h_state_zero")
        s.dx = K.sem("h_dx")
        q0 = K.q
        K.q += 2 * H
        SEG = ((0, NC_S, 0, 0), (NC_S, NC_P, NS, NS + CONV_W - 1))
        toks = lambda x, t0, n: x[:, t0:t0 + n * C].rearrange("p (t c) -> p t c", c=C)
        grp = lambda g: slice(4 * g, 4 * g + 4)
        NG = NPACK // 4

        class Ring:
            def __init__(self, full, free, first, size, uses):
                self.full, self.free, self.first, self.size, self.uses = full, free, first, size, uses

            def bank(self, n):
                return bank[:, self.first + n % self.size, :]

            def to_write(self, pe, h, n):
                pe.wait_ge(self.free, h * self.uses + n + 1)
                return self.bank(n)

            def to_read(self, eng, h, n):
                eng.wait_ge(self.full, h * self.uses + n + 1)
                return self.bank(n)

        rd = Ring(s.full_d, s.free_d, 0, 4, D_USES)
        rs = Ring(s.full_s, s.free_s, 4, 3, S_USES)
        D_DT, D_KK, D_INV0 = 0, 3, 3 + 2 * NG
        D_LEVEL = [None] + [D_INV0 + NG + 3 * NG * (l - 1) for l in range(1, LEVELS)]
        D_SCAN = D_LEVEL[LEVELS - 1] + 2 * NG
        assert D_SCAN + 3 * NPACK == D_USES
        S_SS, S_KT, S_UV, S_Q = 0, 6, 6 + 2 * NG, 6 + 4 * NG
        S_OT = S_Q + NPACK
        S_RMS = S_OT + NG
        assert S_RMS + 3 == S_USES
        quad = lambda b: b[:, :].rearrange("p (t c) -> p t c", c=P)

        with nc.Block() as block:
            @block.sync
            def _(sync):
                for dst, name in ((level[:, :, :], "level"), (level0_t[:, :], "level0_t"), (seen[:, :], "seen")):
                    sync.dma_start(dst, K.c[name]).then_inc(s.consts, 16)
                with sync.Fori(0, H) as h:
                    for t, c0 in enumerate((H * DK, 0, 2 * H * DK, Z0)):
                        load_tile(K, sync, q0 + 2 * h + t // 2, t % 2, K.i["w_in"][0][:, bass.ds(h * P + c0, P)])
                    sync.wait_ge(s.head_end, 4 * h + 4)
                    sync.sem_inc(K.pulse, 1)
                    for d in range(2):
                        if d == 0:
                            sync.dma_start(pick_h[:, :].unsqueeze(1), K.c["pick_head"][:, bass.ds(h, 1), :]).then_inc(s.pick_in, 16)
                        sync.dma_start(state[:, 0, d, :], K.i["state_delta"][0, 0, d][bass.ds(h, 1)].rearrange("o k v -> (o k) v")).then_inc(s.state_in, 16)

            @block.gpsimd
            def _(pool):
                pool.memset(at[:, :, :], 0.0)
                pool.memset(mt[:, :, :], 0.0)
                pool.memset(u[:, :, :, :], 0.0).then_inc(s.pads, 1)
                pool.sem_inc(s.free_d, 4)
                pool.sem_inc(s.free_s, 3)
                pool.sem_inc(s.head_end, 4)
                with pool.Fori(0, H) as h:
                    pool.wait_ge(s.head_end, 4 * h + 4)
                    pool.sem_inc(K.pulse, 1)
                    for a in (0, 2 + NS, 2 * CONV_W - 4 + NS + NP_ + 0):
                        n = 4 if a == 2 + NS else 2
                        i = pool.memset(raw[:, :, a:a + n], 0.0)
                    i.then_inc(s.pads, 1)
                    pool.memset(state[:, 1, :, :], 0.0).then_inc(s.state_zero, 1)
                    pool.wait_ge(s.scal, h + 1)
                    for t in range(4):
                        split_low(K, pool, q0 + 2 * h + t // 2, t % 2)
                    pool.wait_ge(s.dt, h + 1)
                    pool.tensor_tensor(dtb[:, :, :], dt[:, :, :], hs[:, 0, :].unsqueeze(2).to_broadcast([P, NPACK, C]), ALU.mult).then_inc(s.dtb, 1)
                    pool.wait_ge(s.state_new, (h + 1) * NPACK)
                    for d in range(2):
                        pool.dma_start(K.o["new_state_delta"][0, 0, d][bass.ds(h, 1)].rearrange("o k v -> (o k) v"), state[:, 1, d, :]).then_inc(s.s_store, 16)
                    pool.wait_ge(s.o_low, h + 1)
                    pool.dma_start(K.scratch_o[bass.ds(h, 1)].rearrange("o p a t -> (o p) a t"), opair[:, :, :]).then_inc(s.o_store, 16)
                    pool.wait_ge(s.o_store, 16 * (h + 1))
                    pool.wait_ge(s.s_store, 32 * (h + 1))
                    pool.sem_inc(s.head_end, 1)

            @block.tensor
            def _(pe):
                with pe.Fori(0, H) as h:
                    pe.wait_ge(s.head_end, 4 * h + 4)
                    for t in range(4):
                        multiply_tile(K, pe, q0 + 2 * h + t // 2, t % 2, gemm_out[t % 2], K.hn)
                    for slot in range(2):
                        pe.wait_ge(K.tile_read[slot], q0 + 2 * h + 3)
                    n = S_SS
                    for j in range(2):
                        pe.wait_ge(s.squared, 2 * h + j + 1)
                        for c0, cn in ((0, 512), (512, 512), (1024, PADW - 1024 - CONV_W + 1)):
                            b = rs.to_write(pe, h, n)
                            pe.matmul(b[:, 0:cn], K.ones[:, :], sq[:, j, c0:c0 + cn], start=True, stop=True).then_inc(rs.full, 1)
                            n += 1
                    pe.wait_ge(s.pick_in, 16 * (h + 1))
                    for j, (t0, tn) in enumerate(((0, 8), (8, 8), (16, 4))):
                        b = rd.to_write(pe, h, D_DT + j)
                        pe.matmul(b[:, 0:tn * C], pick_h[:, :], K.cum_row[:, t0:t0 + tn, :], start=True, stop=True).then_inc(rd.full, 1)
                    pe.wait_ge(s.turned_packs, 3 * h + 2)
                    for g in range(NG):
                        for j, rhs in enumerate((kp, qp)):
                            b = quad(rd.to_write(pe, h, D_KK + 2 * g + j))
                            for t in range(4):
                                mm = pe.matmul(b[:, t, :], kp[:, 4 * g + t, :], rhs[:, 4 * g + t, :], start=True, stop=True)
                            mm.then_inc(rd.full, 1)
                    pe.wait_ge(s.turned_packs, 3 * h + 3)
                    for g in range(NG):
                        for j, src in enumerate((kp, vt)):
                            b = quad(rs.to_write(pe, h, S_KT + 2 * g + j))
                            for t in range(4):
                                mm = pe.transpose(b[:, t, :], src[:, 4 * g + t, :], K.ident[:, :])
                            mm.then_inc(rs.full, 1)
                    for g in range(NG):
                        pe.wait_ge(s.mt, NG * h + g + 1)
                        b = quad(rd.to_write(pe, h, D_INV0 + g))
                        for t in range(4):
                            mm = pe.transpose(b[:, t, :], mt[:, 4 * g + t, :], K.ident[:, :])
                        mm.then_inc(rd.full, 1)
                    for l in range(1, LEVELS):
                        n = D_LEVEL[l]
                        for g in range(NG):
                            pe.wait_ge(s.inv, NG * (LEVELS * h + l - 1) + g + 1)
                            b = quad(rd.to_write(pe, h, n))
                            n += 1
                            for t in range(4):
                                mm = pe.matmul(b[:, t, :], mt[:, 4 * g + t, :], xi[:, 4 * g + t, :], start=True, stop=True)
                            mm.then_inc(rd.full, 1)
                        for g in range(NG):
                            pe.wait_ge(s.vmask, NG * ((LEVELS - 1) * h + l - 1) + g + 1)
                            if l < LEVELS - 1:
                                b = quad(rd.to_write(pe, h, n))
                                n += 1
                                for t in range(4):
                                    mm = pe.matmul(b[:, t, :], xti[:, 4 * g + t, :], vi[:, 4 * g + t, :], start=True, stop=True)
                                mm.then_inc(rd.full, 1)
                            b = quad(rd.to_write(pe, h, n))
                            n += 1
                            for t in range(4):
                                mm = pe.matmul(b[:, t, :], vi[:, 4 * g + t, :], xti[:, 4 * g + t, :], start=True, stop=True)
                            mm.then_inc(rd.full, 1)
                    for g in range(NG):
                        pe.wait_ge(s.inv, NG * (LEVELS * h + LEVELS - 1) + g + 1)
                        pe.wait_ge(s.tok_v, NG * h + g + 1)
                        b = quad(rs.to_write(pe, h, S_UV + 2 * g))
                        for t in range(4):
                            mm = pe.matmul(b[:, t, :], xti[:, 4 * g + t, :], vt[:, 4 * g + t, :], start=True, stop=True)
                        mm.then_inc(rs.full, 1)
                        b = quad(rs.to_write(pe, h, S_UV + 2 * g + 1))
                        for t in range(4):
                            mm = pe.matmul(b[:, t, :], gk[:, 4 * g + t, :], xti[:, 4 * g + t, :], start=True, stop=True)
                        mm.then_inc(rs.full, 1)
                    pe.wait_ge(s.state_in, 32 * (h + 1))
                    pe.wait_ge(s.state_zero, h + 1)
                    done = {}
                    for i, t in enumerate(STEPS):
                        q = int(t >= NC_S)
                        pe.wait_ge(s.wkt, NG * h + t // 4 + 1)
                        if q in done:
                            pe.wait_ge(s.state_new, NPACK * h + done[q] + 1)
                        done[q] = i
                        b = rd.to_write(pe, h, D_SCAN + 3 * i)
                        for d in range(2):
                            mm = pe.matmul(b[64 * d:64 * d + 64, 0:P], wk[:, t, 64 * d:64 * d + 64], state[:, q, d, :], start=True, stop=True)
                        mm.then_inc(rd.full, 1)
                        b = rs.to_write(pe, h, S_Q + i)
                        for d in range(2):
                            mm = pe.matmul(b[64 * d:64 * d + 64, 0:P], qp[:, t, 64 * d:64 * d + 64], state[:, q, d, :], start=True, stop=True)
                        mm.then_inc(rs.full, 1)
                        pe.wait_ge(s.u, NPACK * h + i + 1)
                        b = rd.to_write(pe, h, D_SCAN + 3 * i + 1)
                        pe.matmul(b[:, 0:2 * P], kd[:, t, :], u[:, i % 2, :, :].rearrange("p d c -> p (d c)"), start=True, stop=True).then_inc(rd.full, 1)
                        b = rd.to_write(pe, h, D_SCAN + 3 * i + 2)
                        pe.matmul(b[:, 0:P], at[:, t, :], u[:, i % 2, 0, :], start=True, stop=False)
                        pe.matmul(b[:, 0:P], at[:, t, :], u[:, i % 2, 1, :], start=False, stop=True).then_inc(rd.full, 1)
                    pe.wait_ge(s.o_add, NPACK * (h + 1))
                    for g in range(NG):
                        b = quad(rs.to_write(pe, h, S_OT + g))
                        for t in range(4):
                            mm = pe.transpose(b[:, t, :], op[:, 4 * g + t, :], K.ident[:, :])
                        mm.then_inc(rs.full, 1)
                    pe.wait_ge(s.o_sq, h + 1)
                    for j, (c0, cn) in enumerate(CHUNKS):
                        b = rs.to_write(pe, h, S_RMS + j)
                        pe.matmul(b[:, 0:cn], K.ones[:, :], sq[:, 0, c0:c0 + cn], start=True, stop=True).then_inc(rs.full, 1)
                    pe.drain().then_inc(s.head_end, 1)

            @block.scalar
            def _(act):
                def to_pad(j, q, slot):
                    wait_tile(K, act, q, slot)
                    if j == 2:
                        act.wait_ge(s.conv, 3 * h + 1)
                    for a, n, _ in SEGS:
                        b = 2 + a + (4 if a else 0)
                        i = act.activation(raw[:, slot, b:b + n], gemm_out[slot][:, a:a + n], ACT.Copy)
                    i.then_inc(K.tile_read[slot], 1)

                act.wait_ge(s.consts, 48)
                with act.Fori(0, H) as h:
                    act.wait_ge(s.head_end, 4 * h + 4)
                    act.wait_ge(s.pads, h + 2)
                    act.wait_ge(s.scal, h + 1)
                    q = q0 + 2 * h
                    split_high(K, act, q, 0)
                    split_high(K, act, q, 1)
                    to_pad(0, q, 0)
                    split_high(K, act, q + 1, 0)
                    to_pad(1, q, 1)
                    split_high(K, act, q + 1, 1)
                    for j in range(2):
                        act.wait_ge(s.conv, 3 * h + j + 1)
                        act.activation(silu[:, j, 0:PADW - 4], cv[:, j, 0:PADW - 4], ACT.Silu).then_inc(s.silu, 1)
                        if j == 0:
                            to_pad(2, q + 1, 0)
                    wait_tile(K, act, q + 1, 1)
                    act.activation(zs[:, :], gemm_out[1][:, 0:T], ACT.Silu).then_inc(K.tile_read[1], 1)
                    act.wait_ge(s.conv, 3 * h + 3)
                    for t0, tn, _, p0 in SEG:
                        src = toks(cv[:, 0, :], p0, tn)
                        act.activation(vt[:, t0:t0 + tn, 0:C], src, ACT.Silu)
                        act.activation(vt[:, t0:t0 + tn, C:P], src[:, ::-1], ACT.Silu)
                    act.wait_ge(s.silu, 2 * h + 2)
                    for j in range(2):
                        act.activation(sq[:, j, 0:PADW - 4], silu[:, j, 0:PADW - 4], ACT.Square).then_inc(s.squared, 1)
                    for j in range(2):
                        for m, (c0, cn) in enumerate(((0, 512), (512, 512), (1024, PADW - 4 - 1024))):
                            b = rs.to_read(act, h, S_SS + 3 * j + m)
                            act.activation(os_[:, j, c0:c0 + cn], b[:, 0:cn], ACT.Ln, bias=K.eps[:, :]).then_inc(rs.free, 1)
                        act.drain()
                        act.activation(os_[:, j, 0:PADW - 4], os_[:, j, 0:PADW - 4], ACT.Exp, scale=-0.5).then_inc(s.inv_norm, 1)
                    act.wait_ge(s.dt_log, h + 1)
                    act.activation(dt[:, :, :], dt[:, :, :], ACT.Exp).then_inc(s.dt, 1)
                    for j, x in enumerate((kp, qp)):
                        act.wait_ge(s.packed, 2 * h + j + 1)
                        for t0, tn, _, _ in SEG:
                            i = act.activation(x[:, t0:t0 + tn, C:P], x[:, t0:t0 + tn, 0:C][:, ::-1], ACT.Copy)
                        i.then_inc(s.turned_packs, 1)
                    act.drain().then_inc(s.turned_packs, 1)
                    for g in range(NG):
                        b = quad(rs.to_read(act, h, S_KT + 2 * g))
                        for t in range(4):
                            act.activation(gk[:, 4 * g + t, :], b[:, t, :], ACT.Copy, scale=hs[:, 3, 4 * g + t:4 * g + t + 1])
                        for t in range(4):
                            i = act.activation(kd[:, 4 * g + t, :], b[:, t, :], ACT.Copy, scale=hs[:, 4, 4 * g + t:4 * g + t + 1])
                        i.then_inc(rs.free, 1)
                        b = rs.to_read(act, h, S_KT + 2 * g + 1)
                        act.activation(vt[:, grp(g), :], quad(b), ACT.Copy).then_inc(rs.free, 1)
                        act.drain().then_inc(s.tok_v, 1)
                    for g in range(NG):
                        b = quad(rs.to_read(act, h, S_UV + 2 * g))
                        for t in range(4):
                            i = act.activation(uv[:, 4 * g + t, :], b[:, t, :], ACT.Copy, scale=hs[:, 0, 4 * g + t:4 * g + t + 1])
                        i.then_inc(rs.free, 1)
                        b = rs.to_read(act, h, S_UV + 2 * g + 1)
                        act.activation(wk[:, grp(g), :], quad(b), ACT.Copy).then_inc(rs.free, 1)
                        act.drain().then_inc(s.wkt, 1)
                    for i, t in enumerate(STEPS):
                        b = rs.to_read(act, h, S_Q + i)
                        if i >= 2:
                            act.wait_ge(s.o_add, NPACK * h + i - 1)
                        act.activation(tq[:, i % 2, :], b[:, 0:P], ACT.Copy, scale=hs[:, 3, t:t + 1]).then_inc(rs.free, 1)
                    for g in range(NG):
                        b = quad(rs.to_read(act, h, S_OT + g))
                        t0, tn, _, _ = SEG[g // 4]
                        lo = 4 * g - t0
                        f = os_[:, 0, 0:T].rearrange("p (t c) -> p t c", c=C)
                        r = os_[:, 1, 0:T].rearrange("p (t c) -> p t c", c=C)
                        first = t0 + tn - 1 - lo
                        act.activation(f[:, grp(g), :], b[:, :, 0:C], ACT.Copy)
                        act.activation(r[:, first - 3:first + 1, :][:, ::-1], b[:, :, C:P], ACT.Copy).then_inc(rs.free, 1)
                    act.wait_ge(s.o_sum, h + 1)
                    act.activation(sq[:, 0, 0:T], os_[:, 0, 0:T], ACT.Square).then_inc(s.o_sq, 1)
                    for m, (c0, cn) in enumerate(CHUNKS):
                        b = rs.to_read(act, h, S_RMS + m)
                        act.activation(os_[:, 1, c0:c0 + cn], b[:, 0:cn], ACT.Ln, scale=1.0 / DK, bias=K.eps[:, :]).then_inc(rs.free, 1)
                    act.drain()
                    act.activation(os_[:, 1, 0:T], os_[:, 1, 0:T], ACT.Exp, scale=-0.5).then_inc(s.o_rstd, 1)
                    act.wait_ge(s.o_fin, h + 1)
                    act.activation(opair[:, 0, :], os_[:, 0, 0:T], ACT.Copy).then_inc(s.o_high, 1)
                    act.drain().then_inc(s.head_end, 1)

            @block.vector
            def _(dve):
                dve.wait_ge(s.consts, 48)
                dve.wait_ge(s.pads, 1)
                with dve.Fori(0, H) as h:
                    dve.wait_ge(s.head_end, 4 * h + 4)
                    one = bass.ds(h, 1)
                    for j, x in enumerate((K.beta, K.neg_beta, K.cum, K.gamma, K.to_end)):
                        dve.tensor_copy(hs[:, j:j + 1, :], x[:, one, :])
                    dve.tensor_copy(hc[:, :, :].unsqueeze(2), K.carry[:, :, one, :])
                    dve.tensor_copy(hw[:, :, :].unsqueeze(3), K.conv_w[:, :].rearrange("p (w a h) -> p w a h", w=CONV_W, h=H)[:, :, :, one])
                    dve.drain().then_inc(s.scal, 1)
                    N = PADW - 4
                    for j, part in enumerate((1, 0, 2)):
                        slot = j % 2
                        dve.wait_ge(K.tile_read[j % 2], q0 + 2 * h + j // 2 + 2)
                        if j == 2:
                            dve.wait_ge(s.silu, 2 * h + 1)
                        dve.tensor_scalar(cv[:, slot, 0:N], raw[:, slot, 0:N], hw[:, 0, part:part + 1], None, ALU.mult)
                        for w in range(1, CONV_W):
                            dve.drain()
                            i = dve.scalar_tensor_tensor(out=cv[:, slot, 0:N], in0=raw[:, slot, w:w + N], scalar=hw[:, w, part:part + 1],
                                                         in1=cv[:, slot, 0:N], op0=ALU.mult, op1=ALU.add)
                        i.then_inc(s.conv, 1)
                    for j, x in enumerate((kp, qp)):
                        dve.wait_ge(s.inv_norm, 2 * h + j + 1)
                        for t0, tn, _, p0 in SEG:
                            i = dve.scalar_tensor_tensor(out=x[:, t0:t0 + tn, 0:C], in0=toks(silu[:, j, :], p0, tn), scalar=1.0 if j == 0 else DK ** -0.5,
                                                         in1=toks(os_[:, j, :], p0, tn), op0=ALU.mult, op1=ALU.mult)
                        i.then_inc(s.packed, 1)
                    for j, (t0, tn) in enumerate(((0, 8), (8, 8), (16, 4))):
                        b = rd.to_read(dve, h, D_DT + j)[:, 0:tn * C].rearrange("p (t c) -> p t c", c=C)
                        dve.tensor_tensor(dt[:, t0:t0 + tn, :], b, hs[:, 2, t0:t0 + tn].unsqueeze(2).to_broadcast([P, tn, C]), ALU.subtract).then_inc(rd.free, 1)
                    dve.drain()
                    dve.tensor_tensor(dt[:, :, :], dt[:, :, :], seen[:, :].unsqueeze(1).to_broadcast([P, NPACK, C]), ALU.min).then_inc(s.dt_log, 1)
                    dve.wait_ge(s.dtb, h + 1)
                    for g in range(NG):
                        for j, (out, f) in enumerate(((mt, dtb), (at, dt))):
                            b = quad(rd.to_read(dve, h, D_KK + 2 * g + j))
                            for d in range(2):
                                r = slice(64 * d, 64 * d + 64)
                                i = dve.tensor_tensor(out[r, grp(g), 64 * d:64 * d + 64], b[r, :, 64 * d:64 * d + 64], f[r, grp(g), :], ALU.mult)
                            i.then_inc(rd.free, 1)
                        dve.drain().then_inc(s.mt, 1)
                    ident4 = K.ident[:, :].unsqueeze(1).to_broadcast([P, 4, P])
                    for g in range(NG):
                        b = quad(rd.to_read(dve, h, D_INV0 + g))
                        dve.tensor_tensor(xi[:, grp(g), :], b, level[:, 0, :].unsqueeze(1).to_broadcast([P, 4, P]), ALU.mult).then_inc(rd.free, 1)
                        dve.tensor_tensor(xti[:, grp(g), :], mt[:, grp(g), :], level0_t[:, :].unsqueeze(1).to_broadcast([P, 4, P]), ALU.mult)
                        dve.drain()
                        dve.tensor_tensor(xi[:, grp(g), :], ident4, xi[:, grp(g), :], ALU.subtract)
                        dve.tensor_tensor(xti[:, grp(g), :], ident4, xti[:, grp(g), :], ALU.subtract).then_inc(s.inv, 1)
                    for l in range(1, LEVELS):
                        n = D_LEVEL[l]
                        for g in range(NG):
                            b = quad(rd.to_read(dve, h, n))
                            n += 1
                            dve.tensor_tensor(vi[:, grp(g), :], b, level[:, l, :].unsqueeze(1).to_broadcast([P, 4, P]), ALU.mult).then_inc(rd.free, 1)
                            dve.drain().then_inc(s.vmask, 1)
                        for g in range(NG):
                            for x in (xi, xti) if l < LEVELS - 1 else (xti,):
                                b = quad(rd.to_read(dve, h, n))
                                n += 1
                                dve.tensor_tensor(x[:, grp(g), :], x[:, grp(g), :], b, ALU.subtract).then_inc(rd.free, 1)
                            dve.drain().then_inc(s.inv, 1)
                    for i, t in enumerate(STEPS):
                        q = int(t >= NC_S)
                        dve.wait_ge(s.wkt, NG * h + t // 4 + 1)
                        b = rd.to_read(dve, h, D_SCAN + 3 * i)
                        for d in range(2):
                            r = slice(64 * d, 64 * d + 64)
                            dve.scalar_tensor_tensor(out=u[r, i % 2, d, :], in0=b[r, 0:P], scalar=hs[r, 1, t:t + 1], in1=uv[r, t, :],
                                                     op0=ALU.mult, op1=ALU.add).then_inc(s.u if d else s.dx, 1)
                        b = rd.to_read(dve, h, D_SCAN + 3 * i + 1)
                        for d in range(2):
                            dve.scalar_tensor_tensor(out=state[:, q, d, :], in0=state[:, q, d, :], scalar=hc[:, d, t:t + 1], in1=b[:, d * P:(d + 1) * P],
                                                     op0=ALU.mult, op1=ALU.add).then_inc(s.state_new if d else s.dx, 1)
                        b2 = rd.to_read(dve, h, D_SCAN + 3 * i + 2)
                        dve.wait_ge(rs.free, S_USES * h + S_Q + i + 1 + 3)
                        dve.tensor_tensor(op[:, t, :], tq[:, i % 2, :], b2[:, 0:P], ALU.add).then_inc(s.o_add, 1)
                        dve.drain().then_inc(rd.free, 3)
                    dve.wait_ge(rs.free, S_USES * h + S_OT + NG + 3)
                    dve.tensor_tensor(os_[:, 0, 0:T], os_[:, 0, 0:T], os_[:, 1, 0:T], ALU.add).then_inc(s.o_sum, 1)
                    dve.wait_ge(s.o_rstd, h + 1)
                    dve.tensor_tensor(os_[:, 0, 0:T], os_[:, 0, 0:T], os_[:, 1, 0:T], ALU.mult)
                    dve.drain()
                    dve.scalar_tensor_tensor(out=os_[:, 0, 0:T], in0=os_[:, 0, 0:T], scalar=K.dn_norm, in1=zs[:, :],
                                             op0=ALU.mult, op1=ALU.mult).then_inc(s.o_fin, 1)
                    dve.wait_ge(s.o_high, h + 1)
                    dve.wait_ge(s.o_fin, h + 1)
                    dve.tensor_tensor(opair[:, 1, :], os_[:, 0, 0:T], opair[:, 0, :], ALU.subtract).then_inc(s.o_low, 1)
                    dve.drain().then_inc(s.head_end, 1)



def phase_branch_a(K, mg, opairs):
    s_o = [K.sem(f"a_o_in_{h}") for h in range(H)]
    s_sg, s_mg = K.sem("a_gate"), K.sem("a_mg")
    q0 = K.q
    K.q += KT
    with ExitStack() as st:
        sg = K.sb("a_sg", [P, T], stack=st)
        out = [K.ps(f"a_out{s}", [P, 1536], st) for s in range(2)]
        with K.nc.Block() as block:
            @block.sync
            def _(sync):
                for h in range(H):
                    sync.dma_start(opairs[:, :, h, :], K.scratch_o[h]).then_inc(s_o[h], 16)
                with sync.Fori(0, KT) as j:
                    load_tile(K, sync, q0 + j, 0, K.i["w_in"][0][:, bass.ds(j * P + GA0, P)])
                    load_tile(K, sync, q0 + j, 1, K.i["w_br_a"][0][:, bass.ds(j * P, P)])

            @block.gpsimd
            def _(pool):
                with pool.Fori(0, KT) as j:
                    for slot in range(2):
                        split_low(K, pool, q0 + j, slot)

            @block.tensor
            def _(pe):
                for h in range(H):
                    pe.wait_ge(s_o[h], 16)
                with pe.Fori(0, KT) as j:
                    multiply_tile(K, pe, q0 + j, 0, out[0], K.hn)
                    multiply_tile(K, pe, q0 + j, 1, out[1], opairs)

            @block.scalar
            def _(act):
                with act.Fori(0, KT) as j:
                    for slot in range(2):
                        split_high(K, act, q0 + j, slot)
                    act.wait_ge(s_mg, j + 1)
                    wait_tile(K, act, q0 + j, 0)
                    act.activation(sg[:, :], out[0][:, 0:T], ACT.Sigmoid).then_inc(K.tile_read[0], 1)

            @block.vector
            def _(dve):
                dve.sem_inc(s_mg, 1)
                with dve.Fori(0, KT) as j:
                    wait_tile(K, dve, q0 + j, 1)
                    dve.wait_ge(K.tile_read[0], q0 + j + 2)
                    dve.tensor_tensor(mg[:, bass.ds(j, 1), :].rearrange("p o t -> p (o t)"), out[1][:, 0:T], sg[:, :], ALU.mult).then_inc(s_mg, 1)
                    dve.wait_ge(s_mg, j + 2)
                    dve.sem_inc(K.tile_read[1], 1)


def phase_u(K):
    q0 = K.q
    K.q += KT // 2
    with ExitStack() as st:
        u = K.sb("u_rows", [P, 2, L5, NC5], stack=st)
        out = [K.ps(f"u_out{s}", [P, 1536], st) for s in range(2)]
        s_st = [K.sem("u_stored_0"), K.sem("u_stored_1")]
        s_u = K.sem("u_copied")
        with K.nc.Block() as block:
            @block.sync
            def _(sync):
                with sync.Fori(0, KT // 2) as j:
                    for slot in range(2):
                        load_tile(K, sync, q0 + j, slot, K.i["w_in"][0][:, bass.ds(j * 2 * P + (U0 + slot * P), P)])

            @block.gpsimd
            def _(pool):
                with pool.Fori(0, KT // 2) as j:
                    for slot in range(2):
                        split_low(K, pool, q0 + j, slot)

            @block.tensor
            def _(pe):
                with pe.Fori(0, KT // 2) as j:
                    for slot in range(2):
                        multiply_tile(K, pe, q0 + j, slot, out[slot], K.hn)

            @block.scalar
            def _(act):
                for slot in range(2):
                    act.sem_inc(s_st[slot], 16)
                with act.Fori(0, KT // 2) as j:
                    for slot in range(2):
                        split_high(K, act, q0 + j, slot)
                    for slot in range(2):
                        act.wait_ge(s_st[slot], 16 * j + 16)
                        wait_tile(K, act, q0 + j, slot)
                        act.activation(u[:, slot, :, :], out[slot][:, 0:T].rearrange("p (c t) -> p t c", t=L5), ACT.Copy).then_inc(K.tile_read[slot], 1)
                        act.wait_ge(K.tile_read[slot], q0 + j + 2)
                        act.dma_start(K.scratch_u[bass.ds(2 * j + slot, 1)].rearrange("o p t c -> (o p) t c"), u[:, slot, :, :]).then_inc(s_st[slot], 16)
                for slot in range(2):
                    act.wait_ge(s_st[slot], 16 * (KT // 2) + 16)


def phase_s5(K):
    nc = K.nc
    NG2 = 2 * G_S5
    TWO_PI = 6.283185307179586
    with ExitStack() as st:
        f = lambda name, shape, stack=st: K.sb(name, shape, stack=stack)
        pa = [f(n, [P, 2, G_S5, 9]) for n in ("pa_re", "pa_im")]
        pb = [f(n, [P, 2, G_S5, L5]) for n in ("pb_re", "pb_im")]
        e1 = [f(n, [P, 2, G_S5]) for n in ("e1_cos", "e1_sin")]
        r8 = f("r8", [P, 2, G_S5])
        h0 = f("h0", [P, 2, G_S5])
        bst = f("bst", [P, 2, G_S5, P_S5])
        b2st = f("b2st", [P, 2, G_S5, P_S5])
        c1 = f("c1", [P, 2, G_S5, P_S5])
        c2 = f("c2", [P, 2, G_S5, P_S5])
        fin = f("s5_fin", [P, 2, G_S5])
        with ExitStack() as s2:
            g = lambda name, shape: K.sb(name, shape, stack=s2)
            nat = g("s5_nat", [P, 6, 2, N_S5])
            ldt = g("s5_ldt", [P, 1])
            tr = g("s5_tr", [P, 5, 2, G_S5])
            w = g("s5_w", [P, 8, 2, G_S5])
            b1, b2 = g("s5_b1", [P, 2, G_S5, P_S5]), g("s5_b2", [P, 2, G_S5, P_S5])
            bn = [g(n, [P, 2, N_S5 * P_S5]) for n in ("bn1", "bn2")]
            cn = [g(n, [P, 16, 2, N_S5]) for n in ("cn1", "cn2")]
            ct = g("ct", [P, P])
            bank = K.ps("s5_bank", [P, 8, 512], s2)
            s_nat, s_b, s_c = K.sem("s5p_nat"), K.sem("s5p_b"), K.sem("s5p_c")
            s_bm, s_bt = K.sem("s5p_b_turned"), K.sem("s5p_b_read")
            s_dt, s_xy, s_t, s_red, s_trig, s_dve, s_ct, s_ce = (K.sem("s5p_" + n) for n in ("dt", "xy", "turned", "reduced", "trig", "dve", "c_turned", "c_read"))
            dgn = lambda a: a.rearrange("d g n -> (d g) n")
            W = lambda j: w[:, j, :, :]
            with nc.Block() as block:
                @block.sync
                def _(sync):
                    for u in range(2):
                        sync.dma_start(nat[:, 0, u, :], dgn(K.i["s5_a_re"][0])).then_inc(s_nat, 16)
                        sync.dma_start(nat[:, 1, u, :], dgn(K.i["s5_a_im"][0])).then_inc(s_nat, 16)
                    sync.dma_start(nat[:, 4, 0, :], dgn(K.i["state_s5_re"][0, 0])).then_inc(s_nat, 16)
                    sync.dma_start(nat[:, 4, 1, :], dgn(K.i["state_s5_im"][0, 0])).then_inc(s_nat, 16)
                    with nc.allow_non_contiguous_dma(reason="128 values"):
                        sync.dma_start(ldt[:, :], K.i["s5_log_dt"][0].rearrange("d (g o) -> (d g) o", o=1)).then_inc(s_nat, 16)
                    for j, (x, y) in enumerate((("s5_c_re", "s5_c_im"), ("s5_c_im", "s5_c_re"))):
                        for u, name in enumerate((x, y)):
                            sync.dma_start(cn[j][:, :, u, :], K.i[name][0].rearrange("d (k g) p n -> (g p) (d k) n", g=8)).then_inc(s_c, 16)

                @block.gpsimd
                def _(pool):
                    for x, names in zip(bn, (("s5_b_re", "s5_b_im"), ("s5_b_im", "s5_b_re"))):
                        for u, name in enumerate(names):
                            pool.dma_start(x[:, u, :], K.i[name][0].rearrange("d g n p -> (d g) (n p)")).then_inc(s_b, 16)

                @block.tensor
                def _(pe):
                    pe.wait_ge(s_xy, 1)
                    for j, src in enumerate((0, 1, 2, 3, 4)):
                        mm = pe.transpose(bank[:, j, 0:P], nat[:, src, :, :], K.ident[:, :])
                    mm.then_inc(s_t, 1)
                    pe.wait_ge(s_b, 64)
                    pe.wait_ge(s_bt, 1)
                    for j in range(2):
                        rows = bn[j][:, :, :].rearrange("q u (n p) -> q p (u n)", p=P_S5)
                        for c in range(P_S5):
                            if j and c % 4 == 0:
                                pe.wait_ge(s_bt, 2 + c // 4)
                            mm = pe.transpose(bank[:, c // 4, (c % 4) * P:(c % 4 + 1) * P], rows[:, c, :], K.ident[:, :])
                            if c % 4 == 3:
                                mm.then_inc(s_bm, 1)
                    pe.wait_ge(s_c, 64)
                    for i in range(16):
                        for j in range(2):
                            n = 2 * i + j
                            if n >= 2:
                                pe.wait_ge(s_ce, n - 1)
                            pe.transpose(bank[:, 6 + j, 0:P], cn[j][:, i, :, :], K.ident[:, :]).then_inc(s_ct, 1)

                @block.scalar
                def _(act):
                    act.wait_ge(s_nat, 16 * 7)
                    act.activation(ldt[:, :], ldt[:, :], ACT.Exp).then_inc(s_dt, 1)
                    act.wait_ge(s_red, 1)
                    act.activation(W(0), tr[:, 2, :, :], ACT.Exp)
                    act.activation(r8[:, :, :], tr[:, 2, :, :], ACT.Exp, scale=float(L5))
                    act.activation(W(1), W(5), ACT.Sin)
                    act.activation(W(2), W(5), ACT.Sin, scale=0.5)
                    act.activation(e1[1][:, :, :], W(6), ACT.Sin)
                    act.activation(W(3), W(6), ACT.Sin, scale=0.5).then_inc(s_trig, 1)
                    for i in range(16):
                        d, k = i // 8, i % 8
                        gs = slice(8 * k, 8 * k + 8)
                        v = lambda lo, b: bank[lo:lo + 64, 6 + b, 0:P].rearrange("p (g c) -> p g c", c=P_S5)
                        act.wait_ge(s_ct, 2 * i + 1)
                        act.activation(c1[0:64, d, gs, :], v(0, 0), ACT.Copy)
                        act.activation(c1[64:P, d, gs, :], v(64, 0), ACT.Copy, scale=-1.0).then_inc(s_ce, 1)
                        act.wait_ge(s_ct, 2 * i + 2)
                        act.activation(c2[:, d, gs, :], bank[:, 7, 0:P].rearrange("p (g c) -> p g c", c=P_S5), ACT.Copy, scale=-1.0).then_inc(s_ce, 1)

                @block.vector
                def _(dve):
                    def tt(o, a, b, op):
                        return dve.tensor_tensor(o, a, b, op)

                    def reduce_angle(dst, y, k):
                        big = 12582912.0
                        dve.tensor_scalar(k, y, 1.0 / TWO_PI, None, ALU.mult)
                        dve.drain()
                        dve.tensor_scalar(k, k, big, None, ALU.add)
                        dve.drain()
                        dve.tensor_scalar(k, k, big, None, ALU.subtract)
                        dve.drain()
                        dve.scalar_tensor_tensor(out=dst, in0=k, scalar=-6.28125, in1=y, op0=ALU.mult, op1=ALU.add)
                        dve.drain()
                        dve.scalar_tensor_tensor(out=dst, in0=k, scalar=-(TWO_PI - 6.28125), in1=dst, op0=ALU.mult, op1=ALU.add)
                        dve.drain()
                        dve.tensor_scalar(dst, dst, 3.1415925, -3.1415925, ALU.min, ALU.max)
                        dve.drain()

                    dve.wait_ge(s_dt, 1)
                    dve.tensor_scalar(nat[:, 2, :, :], nat[:, 0, :, :], ldt[:, :], None, ALU.mult)
                    dve.tensor_scalar(nat[:, 3, :, :], nat[:, 1, :, :], ldt[:, :], None, ALU.mult).then_inc(s_xy, 1)
                    dve.wait_ge(s_t, 1)
                    for j in range(5):
                        dst = tr[:, j, :, :] if j < 4 else h0[:, :, :]
                        dve.tensor_copy(dst, bank[:, j, 0:P].rearrange("p (d g) -> p d g", d=2))
                    dve.drain().then_inc(s_bt, 1)
                    for j, x in enumerate((b1, b2)):
                        for c in range(4):
                            dve.wait_ge(s_bm, 4 * j + c + 1)
                            dve.tensor_copy(x[:, :, :, 4 * c:4 * c + 4].rearrange("p d g c -> p c (d g)"),
                                            bank[:, c, :].rearrange("p (c q) -> p c q", c=4)).then_inc(s_bt, 1)
                    reduce_angle(W(5), tr[:, 3, :, :], W(7))
                    dve.tensor_scalar(W(4), W(5), float(L5), None, ALU.mult)
                    dve.drain()
                    reduce_angle(W(6), W(4), W(7))
                    dve.drain().then_inc(s_red, 1)
                    dve.wait_ge(s_trig, 1)
                    for src, dst in ((W(2), W(4)), (W(3), e1[0][:, :, :])):
                        tt(dst, src, src, ALU.mult)
                        dve.drain()
                        dve.tensor_scalar(dst, dst, -2.0, 1.0, ALU.mult, ALU.add)
                        dve.drain()
                    sl = lambda t, d, k: t[:, d, :, k if d == 0 else 8 - k]
                    for d in range(2):
                        dve.memset(sl(pa[0], d, 0), 1.0)
                        dve.memset(sl(pa[1], d, 0), 0.0)
                        tt(sl(pa[0], d, 1), w[:, 0, d, :], w[:, 4, d, :], ALU.mult)
                        tt(sl(pa[1], d, 1), w[:, 0, d, :], w[:, 1, d, :], ALU.mult)
                    dve.drain()
                    for k in range(2, 9):
                        for d in range(2):
                            ar, ai, pr, pi = sl(pa[0], d, 1), sl(pa[1], d, 1), sl(pa[0], d, k - 1), sl(pa[1], d, k - 1)
                            for j, (x, y) in enumerate(((pr, ar), (pi, ai), (pr, ai), (pi, ar))):
                                tt(w[:, j if j < 3 else 5, d, :], x, y, ALU.mult)
                        dve.drain()
                        for d in range(2):
                            tt(sl(pa[0], d, k), w[:, 0, d, :], w[:, 1, d, :], ALU.subtract)
                            tt(sl(pa[1], d, k), w[:, 2, d, :], w[:, 5, d, :], ALU.add)
                        dve.drain()
                    for t in range(2):
                        dve.tensor_copy(pb[t][:, 0, :, :], pa[t][:, 0, :, 7::-1])
                        dve.tensor_copy(pb[t][:, 1, :, :], pa[t][:, 1, :, 8:0:-1])
                    lr, li = tr[:, 0, :, :], tr[:, 1, :, :]
                    for d in range(2):
                        dve.tensor_scalar(w[:, 0, d, :], sl(pa[0], d, 1), -1.0, None, ALU.add)
                        dve.tensor_copy(w[:, 1, d, :], sl(pa[1], d, 1))
                    tt(W(2), lr, lr, ALU.mult)
                    tt(W(3), li, li, ALU.mult)
                    dve.drain()
                    tt(W(2), W(2), W(3), ALU.add)
                    dve.drain()
                    dve.reciprocal(W(2), W(2))
                    tt(W(4), W(0), lr, ALU.mult)
                    tt(W(5), W(1), li, ALU.mult)
                    tt(W(6), W(1), lr, ALU.mult)
                    tt(W(7), W(0), li, ALU.mult)
                    dve.drain()
                    tt(W(4), W(4), W(5), ALU.add)
                    tt(W(6), W(6), W(7), ALU.subtract)
                    dve.drain()
                    tt(W(4), W(4), W(2), ALU.mult)
                    tt(W(6), W(6), W(2), ALU.mult)
                    dve.drain()
                    dve.tensor_scalar(b2[0:64, :, :, :], b2[0:64, :, :, :], -1.0, None, ALU.mult)
                    dve.drain()
                    cr = W(4).unsqueeze(3).to_broadcast([P, 2, G_S5, P_S5])
                    ci = W(6).unsqueeze(3).to_broadcast([P, 2, G_S5, P_S5])
                    tt(bst[:, :, :, :], b1[:, :, :, :], cr, ALU.mult)
                    tt(b2st[:, :, :, :], b2[:, :, :, :], cr, ALU.mult)
                    tt(b2[:, :, :, :], b2[:, :, :, :], ci, ALU.mult)
                    tt(b1[:, :, :, :], b1[:, :, :, :], ci, ALU.mult)
                    dve.drain()
                    tt(bst[:, :, :, :], bst[:, :, :, :], b2[:, :, :, :], ALU.add)
                    tt(b2st[:, :, :, :], b2st[:, :, :, :], b1[:, :, :, :], ALU.subtract)

        NB = G_S5 // GB
        NE = NC5_S + 1
        tcs, tss = f("rot_cos", [P, 2, 2, GB, NE]), f("rot_sin", [P, 2, 2, GB, NE])
        rt = f("rot_tmp", [P, 4, 2, GB, NC5_S // 2])
        cc, cq = f("cc", [P, 2, 2, GB, 9, P_S5]), f("cq", [P, 2, 2, GB, 9, P_S5])
        ctmp = f("c_tmp", [P, 2, 2, GB, 9, P_S5])
        wt = f("wt", [P, 2, GB, L5, P_S5])
        w1, w2 = f("w1", [P, 2, GB, P]), f("w2", [P, 2, GB, P])
        bb = f("b_block", [P, 2, 2, GB, P_S5])
        ks = f("k_rows", [P_S5, GB, 15 * P_S5])
        m = f("m_block", [P, GB, P])
        u = f("u_block", [P, 2, GB, NC5])
        y = f("y_block", [P, GB, NC5])
        gt = f("g_tmp", [P, 2, GB, NC5])
        gs = f("g_scan", [P, 2, GB, NE])
        gp = f("g_scan_p", [P, 2, GB, NC5_P + 1])
        pq = f("pq", [P, 2, 2, GB, NC5])
        bank = K.ps("s5_banks", [P, 8, 512], st)
        ends = rt[0:1, :, :, :, :].rearrange("p a d g c -> p (a d g c)")[:, 0:2 * D].rearrange("p (d c) -> p d c", d=2)
        halves = lambda b: bank[:, b:b + 2, :].rearrange("p b (g c) -> p (b g) c", c=256)
        xb, x2b, yb = halves(0), halves(2), halves(4)
        s = Names()
        s.u_in = [K.sem("s5_u_in_0"), K.sem("s5_u_in_1")]
        s.tables = K.sem("s5_tables")
        s.cc = K.sem("s5_cc")
        s.wt = K.sem("s5_wt")
        s.wtr = K.sem("s5_wtr")
        s.w = K.sem("s5_w")
        s.k = K.sem("s5_k")
        s.ks = K.sem("s5_ks")
        s.m_in = K.sem("s5_m_in")
        s.x = K.sem("s5_x")
        s.xread = K.sem("s5_xread")
        s.pq = K.sem("s5_pq")
        s.y = K.sem("s5_y")
        s.yread = K.sem("s5_yread")
        s.y_out = K.sem("s5_y_out")
        s.fin_t = K.sem("s5_fin_t")
        s.fin_in = K.sem("s5_fin_in")
        s.fin_u = K.sem("s5_fin_u")
        s.fin_c = K.sem("s5_fin_c")
        s.fin_d = K.sem("s5_fin_d")
        s.fin_out = K.sem("s5_fin_out")
        su = K.scratch_u.rearrange("k q t c -> (k q) t c").rearrange("(g p) t c -> t p g c", p=P_S5)
        sy = K.scratch_y.rearrange("k q t c -> (k q) t c").rearrange("(g p) t c -> t p g c", p=P_S5)
        with nc.Block() as block:
            @block.sync
            def _(sync):
                def load(b, slot):
                    sync.wait_ge(s.y, b + 1)
                    sync.sem_inc(K.pulse, 1)
                    for t in range(L5):
                        sync.dma_start(u[t * P_S5:(t + 1) * P_S5, slot, :, :], su[t][:, bass.ds(b * GB, GB), :]).then_inc(s.u_in[slot], 16)

                def toeplitz(b):
                    sync.wait_ge(s.ks, b + 1)
                    for t in range(L5):
                        sync.dma_start(m[t * P_S5:(t + 1) * P_S5, :, :], ks[:, :, (7 - t) * P_S5:(7 - t) * P_S5 + P]).then_inc(s.m_in, 16)

                def store(b):
                    sync.wait_ge(s.yread, b + 2)
                    sync.sem_inc(K.pulse, 1)
                    for t in range(L5):
                        sync.dma_start(sy[t][:, bass.ds(b * GB, GB), :], y[t * P_S5:(t + 1) * P_S5, :, :]).then_inc(s.y_out, 16)

                sync.sem_inc(s.y_out, 16 * L5)
                load(0, 0)
                toeplitz(0)
                with sync.Fori(0, NB // 2 - 1) as i:
                    for k in (1, 2):
                        load(2 * i + k, k % 2)
                        store(2 * i + (k - 1))
                        toeplitz(2 * i + k)
                load(NB - 1, 1)
                store(NB - 2)
                toeplitz(NB - 1)
                store(NB - 1)
                sync.wait_ge(s.y_out, 16 * L5 * (NB + 1))
                sync.wait_ge(s.tables, NB)
                with nc.allow_non_contiguous_dma(reason="one token's channels"):
                    for d, (t, c) in enumerate(((0, NC5_S), (L5 - 1, NC5 - 1))):
                        sync.dma_start(ends[0:1, d, :], K.scratch_u.rearrange("k q t c -> t c (k q)")[t, c].unsqueeze(0)).then_inc(s.fin_in, 16)
                sync.wait_ge(s.fin_d, 1)
                for j, name in enumerate(("new_state_s5_re", "new_state_s5_im")):
                    sync.dma_start(K.o[name][0, 0].rearrange("d g n -> (d g) n"), w1[:, 0, 0, j * N_S5:(j + 1) * N_S5]).then_inc(s.fin_out, 16)
                sync.wait_ge(s.fin_out, 32)

            @block.gpsimd
            def _(pool):
                def block_tables(b, slot):
                    tc, ts = tcs[:, slot, :, :, :], tss[:, slot, :, :, :]
                    pool.wait_ge(s.pq, b + 1)
                    pool.sem_inc(K.pulse, 1)
                    blk = bass.ds(b * GB, GB)
                    pool.memset(tc[:, :, :, 0:1], 1.0)
                    pool.memset(ts[:, :, :, 0:1], 0.0)
                    pool.tensor_copy(tc[:, :, :, 1:2], e1[0][:, :, blk].unsqueeze(3))
                    pool.tensor_copy(ts[:, :, :, 1:2], e1[1][:, :, blk].unsqueeze(3))
                    pool.tensor_copy(bb[:, slot, :, :, :], bst[:, :, blk, :])
                    pool.drain()
                    n = 1
                    while n < NC5_S:
                        for j, (x, z) in enumerate(((tc, tc), (ts, ts), (ts, tc), (tc, ts))):
                            pool.tensor_tensor(rt[:, j, :, :, 0:n], x[:, :, :, 1:n + 1], z[:, :, :, n:n + 1].to_broadcast([P, 2, GB, n]), ALU.mult)
                        pool.drain()
                        pool.tensor_tensor(tc[:, :, :, n + 1:2 * n + 1], rt[:, 0, :, :, 0:n], rt[:, 1, :, :, 0:n], ALU.subtract)
                        pool.tensor_tensor(ts[:, :, :, n + 1:2 * n + 1], rt[:, 2, :, :, 0:n], rt[:, 3, :, :, 0:n], ALU.add)
                        pool.drain()
                        n *= 2
                    pool.drain().then_inc(s.tables, 1)

                with pool.Fori(0, NB // 2) as i:
                    for slot in range(2):
                        block_tables(2 * i + slot, slot)

            @block.tensor
            def _(pe):
                def block_products(i, slot):
                    b = 2 * i + slot
                    pe.wait_ge(s.wt, b + 1)
                    for d in range(2):
                        for g in range(GB):
                            mm = pe.transpose(bank[:, 6 + d, g * P:(g + 1) * P], wt[:, d, g, :, :], K.ident[:, :])
                    mm.then_inc(s.wtr, 1)
                    pe.wait_ge(s.w, b + 1)
                    pe.wait_ge(s.u_in[slot], 16 * L5 * (i + 1))
                    for d in range(2):
                        if d:
                            pe.wait_ge(s.xread, 2 * b + 1)
                        for out, lhs in ((xb, w1), (x2b, w2)):
                            for g in range(GB):
                                mm = pe.matmul(out[:, g, 0:NC5], lhs[:, d, g, :], u[:, slot, g, :], start=True, stop=True)
                        mm.then_inc(s.x, 1)
                        if d == 0:
                            pe.wait_ge(s.cc, b + 1)
                            pe.wait_ge(s.tables, b + 1)
                            pe.wait_ge(s.yread, b + 1)
                            for g in range(GB):
                                back = cc[:, slot, 1, g, 1:9, :]
                                fwd = cc[:, slot, 0, g, 0:8, :]
                                o = yb[0:P_S5, g, :]
                                pe.matmul(o[:, 0:P], bb[:, slot, 1, g, :], back, start=True, stop=False, skip_group_check=True)
                                pe.matmul(o[:, 7 * P_S5:P], bb[:, slot, 0, g, :], fwd[:, 0:1, :], start=False, stop=True, skip_group_check=True)
                                mm = pe.matmul(o[:, P:15 * P_S5], bb[:, slot, 0, g, :], fwd[:, 1:8, :], start=True, stop=True, skip_group_check=True)
                            mm.then_inc(s.k, 1)
                    pe.wait_ge(s.m_in, 16 * L5 * (b + 1))
                    pe.wait_ge(s.pq, b + 3)
                    for g in range(GB):
                        o = yb[:, g, 0:NC5]
                        pe.matmul(o, m[:, g, :], u[:, slot, g, :], start=True, stop=False, skip_group_check=True)
                        for d in range(2):
                            k0 = 1 - d
                            pe.matmul(o, cc[:, slot, d, g, k0:k0 + 8, :].rearrange("p k c -> p (k c)"), pq[:, d, 0, g, :], start=False, stop=False, skip_group_check=True)
                            mm = pe.matmul(o, cq[:, slot, d, g, k0:k0 + 8, :].rearrange("p k c -> p (k c)"), pq[:, d, 1, g, :], start=False, stop=d == 1, skip_group_check=True)
                    mm.then_inc(s.y, 1)

                pe.sem_inc(s.y, 2)
                pe.sem_inc(s.wtr, 1)
                with pe.Fori(0, NB // 2) as i:
                    for slot in range(2):
                        block_products(i, slot)
                pe.wait_ge(s.pq, NB + 2)
                pe.wait_ge(s.fin_in, 32)
                for d in range(2):
                    for j in range(2):
                        mm = pe.matmul(bank[:, 2 * d + j, :], K.ones[0:1, :], ends[0:1, d, j * 512:(j + 1) * 512], start=True, stop=True)
                    mm.then_inc(s.fin_u, 1)
                pe.wait_ge(s.fin_t, 2)
                mm = pe.transpose(bank[:, 4, 0:P], fin[:, :, :], K.ident[:, :])
                mm.then_inc(s.fin_c, 1)

            @block.scalar
            def _(act):
                def block_copies(b):
                    act.wait_ge(s.wtr, b + 2)
                    for d in range(2):
                        v = bank[:, 6 + d, :].rearrange("p (g c) -> p g c", c=P)
                        act.activation(w1[:, d, :, :], v, ACT.Copy)
                        act.activation(w2[:, d, :, 0:64], v[:, :, 64:P], ACT.Copy)
                        c = act.activation(w2[:, d, :, 64:P], v[:, :, 0:64], ACT.Copy, scale=-1.0)
                    c.then_inc(s.w, 1)
                    act.wait_ge(s.k, b + 1)
                    act.activation(ks[:, :, :], yb[0:P_S5, :, 0:15 * P_S5], ACT.Copy).then_inc(s.ks, 1)
                    act.wait_ge(s.y, b + 3)
                    act.wait_ge(s.y_out, 16 * L5 * (b + 1))
                    act.activation(y[:, :, :], yb[:, :, 0:NC5], ACT.Copy).then_inc(s.yread, 1)

                act.sem_inc(s.yread, 1)
                with act.Fori(0, NB) as b:
                    block_copies(b)

            @block.vector
            def _(dve):
                for d in range(2):
                    dve.memset(gp[:, d, :, 0:1] if d == 0 else gp[:, d, :, NC5_P:], 0.0)

                def block_scans(b, slot):
                    blk = bass.ds(b * GB, GB)
                    tc, ts = tcs[:, slot, :, :, :], tss[:, slot, :, :, :]
                    dve.wait_ge(s.wtr, b + 1)
                    for d in range(2):
                        sh = [P, GB, L5, P_S5]
                        br = lambda x: x[:, d:d + 1, blk, :].rearrange("p o g c -> p (o g) c").unsqueeze(2).to_broadcast(sh)
                        pw = lambda x: x[:, d:d + 1, blk, :].rearrange("p o g c -> p (o g) c").unsqueeze(3).to_broadcast(sh)
                        t = ctmp[:, 0, d, :, 0:8, :]
                        dve.tensor_tensor(wt[:, d, :, :, :], br(bst), pw(pb[0]), ALU.mult)
                        dve.tensor_tensor(t, br(b2st), pw(pb[1]), ALU.mult)
                        dve.drain()
                        i = dve.tensor_tensor(wt[:, d, :, :, :], wt[:, d, :, :, :], t, ALU.add)
                    i.then_inc(s.wt, 1)
                    dve.drain()
                    dve.wait_ge(s.y, b + 1)
                    for d in range(2):
                        sh = [P, GB, 9, P_S5]
                        br = lambda x: x[:, d:d + 1, blk, :].rearrange("p o g c -> p (o g) c").unsqueeze(2).to_broadcast(sh)
                        pw = lambda x: x[:, d:d + 1, blk, :].rearrange("p o g c -> p (o g) c").unsqueeze(3).to_broadcast(sh)
                        dve.tensor_tensor(cc[:, slot, d, :, :, :], br(c1), pw(pa[0]), ALU.mult)
                        dve.tensor_tensor(ctmp[:, 0, d, :, :, :], br(c2), pw(pa[1]), ALU.mult)
                        dve.tensor_tensor(cq[:, slot, d, :, :, :], br(c2), pw(pa[0]), ALU.mult)
                        dve.tensor_tensor(ctmp[:, 1, d, :, :, :], br(c1), pw(pa[1]), ALU.mult)
                        dve.drain()
                        dve.tensor_tensor(cc[:, slot, d, :, :, :], cc[:, slot, d, :, :, :], ctmp[:, 0, d, :, :, :], ALU.add)
                        i = dve.tensor_tensor(cq[:, slot, d, :, :, :], cq[:, slot, d, :, :, :], ctmp[:, 1, d, :, :, :], ALU.subtract)
                    i.then_inc(s.cc, 1)
                    dve.wait_ge(s.tables, b + 1)
                    spans = ((0, NC5_S), (NC5_S, NC5_P))
                    for d in range(2):
                        tab = lambda x, n, o: x[:, d, :, o:n + o] if d == 0 else x[:, d, :, o:n + o][:, :, ::-1]
                        dve.wait_ge(s.x, 2 * b + d + 1)
                        for c0, n in spans:
                            dve.tensor_tensor(gt[:, 0, :, c0:c0 + n], xb[:, :, c0:c0 + n], tab(tc, n, 1), ALU.mult)
                            i = dve.tensor_tensor(gt[:, 1, :, c0:c0 + n], x2b[:, :, c0:c0 + n], tab(ts, n, 1), ALU.mult)
                        i.then_inc(s.xread, 1)
                        start = 0 if d == 0 else NE - 1
                        dve.tensor_copy(gs[:, d:d + 1, :, start:start + 1], h0[:, d:d + 1, blk].unsqueeze(3))
                        dve.drain()
                        dve.tensor_tensor(gt[:, 0, :, :], gt[:, 0, :, :], gt[:, 1, :, :], ALU.add)
                        dve.tensor_copy(ctmp[:, 0, d, 0, 0, 0:GB], r8[:, d:d + 1, blk].rearrange("p o g -> p (o g)"))
                        dve.drain()
                        for g in range(GB):
                            decay = ctmp[:, 0, d, 0, 0, g:g + 1]
                            for (c0, n), x in zip(spans, (gs, gp)):
                                o = x[:, d, g, 1:n + 1] if d == 0 else x[:, d, g, n - 1::-1]
                                i0 = x[:, d, g, 0:1] if d == 0 else x[:, d, g, n:n + 1]
                                v = gt[:, 0, g, c0:c0 + n]
                                dve.tensor_tensor_scan(o, decay.to_broadcast([P, n]), v if d == 0 else v[:, ::-1], i0, ALU.mult, ALU.add)
                        dve.drain()
                        dve.wait_ge(s.y, b + 2)
                        for (c0, n), x in zip(spans, (gs, gp)):
                            before = x[:, d, :, 0:n] if d == 0 else x[:, d, :, 1:n + 1]
                            for j, t in enumerate((tc, ts)):
                                i = dve.tensor_tensor(pq[:, d, j, :, c0:c0 + n], before, tab(t, n, 0), ALU.mult)
                        dve.drain()
                    dve.drain().then_inc(s.pq, 1)

                dve.sem_inc(s.pq, 2)
                with dve.Fori(0, NB // 2) as i:
                    for slot in range(2):
                        block_scans(2 * i + slot, slot)
                for d in range(2):
                    dve.wait_ge(s.fin_u, d + 1)
                    v = gt[:, :, :, :].rearrange("p a g c -> p (a g c)")[:, 0:G_S5 * P_S5]
                    o = bank[:, 2 * d:2 * d + 2, :].rearrange("p b c -> p (b c)")
                    dve.tensor_tensor(v, bst[:, d, :, :].rearrange("p g c -> p (g c)"), o, ALU.mult)
                    dve.drain()
                    dve.tensor_reduce(fin[:, d, :], v.rearrange("p (g c) -> p g c", c=P_S5), mybir.AxisListType.X, ALU.add)
                    dve.drain().then_inc(s.fin_t, 1)
                dve.wait_ge(s.fin_c, 1)
                dve.tensor_copy(w1[:, 0, 0, :], bank[:, 4, 0:P]).then_inc(s.fin_d, 1)



def split_streams(K, block, tiles):
    @block.sync
    def _(sync):
        for n, q, src, kt in tiles:
            with sync.Fori(0, n) as j:
                for slot in range(2):
                    load_tile(K, sync, q + j, slot, src(j, slot), kt)

    @block.gpsimd
    def _(pool):
        for n, q, src, kt in tiles:
            with pool.Fori(0, n) as j:
                for slot in range(2):
                    split_low(K, pool, q + j, slot, kt)


def one(x, j):
    return x[:, bass.ds(j, 1), :].rearrange("p o t -> p (o t)")


def phase_glu(K, ys):
    with ExitStack() as st:
        y = K.sb("glu_y", [P, 2, L5, NC5], stack=st)
        u = K.sb("glu_u", [P, 2, L5, NC5], stack=st)
        v = K.sb("glu_v", [P, 2, L5, NC5], stack=st)
        g = K.sb("glu_g", [P, 2, T], stack=st)
        s_in = [K.sem("glu_in_0"), K.sem("glu_in_1")]
        s_v, s_g, s_hi, s_lo = (K.sem("glu_" + n) for n in ("sum", "gelu", "high", "low"))
        with K.nc.Block() as block:
            @block.sync
            def _(sync):
                for j in range(KT):
                    if j >= 2:
                        sync.wait_ge(s_v, j - 1)
                    sync.dma_start(y[:, j % 2, :, :], K.scratch_y[j]).then_inc(s_in[j % 2], 16)
                    sync.dma_start(u[:, j % 2, :, :], K.scratch_u[j]).then_inc(s_in[j % 2], 16)

            @block.scalar
            def _(act):
                for j in range(KT):
                    act.wait_ge(s_v, j + 1)
                    if j >= 2:
                        act.wait_ge(s_lo, j - 1)
                    act.activation(g[:, j % 2, :].rearrange("p (c t) -> p t c", t=L5), v[:, j % 2, :, :], ACT.Gelu_apprx_tanh).then_inc(s_g, 1)
                    act.wait_ge(s_g, j + 1)
                    act.activation(ys[:, 0, j, :], g[:, j % 2, :], ACT.Copy).then_inc(s_hi, 1)

            @block.vector
            def _(dve):
                def low(j):
                    dve.wait_ge(s_hi, j + 1)
                    dve.tensor_tensor(ys[:, 1, j, :], g[:, j % 2, :], ys[:, 0, j, :], ALU.subtract).then_inc(s_lo, 1)

                for j in range(KT):
                    dve.wait_ge(s_in[j % 2], 32 * (j // 2 + 1))
                    if j >= 2:
                        dve.wait_ge(s_g, j - 1)
                    dve.scalar_tensor_tensor(out=v[:, j % 2, :, :], in0=u[:, j % 2, :, :], scalar=K.s5_d[:, j:j + 1], in1=y[:, j % 2, :, :],
                                             op0=ALU.mult, op1=ALU.add).then_inc(s_v, 1)
                    if j:
                        low(j - 1)
                low(KT - 1)


def phase_branch_b(K, mg, ys, ys2):
    q0 = K.q
    K.q += KT // 2 + KT
    q1 = q0 + KT // 2
    with ExitStack() as st:
        out = [K.ps(f"b_out{s}", [P, 1536], st) for s in range(2)]
        sg = K.sb("b_sg", [P, 2, T], stack=st)
        y = K.sb("b_y", [P, 2, T], stack=st)
        s_sg, s_y, s_hi, s_lo, s_t, s_mg = (K.sem("b_" + n) for n in ("sig", "y", "high", "low", "prod", "mg"))
        with K.nc.Block() as block:
            gate_b = lambda j: K.i["w_in"][0][:, bass.ds(j * P + GB0, P)]
            split_streams(K, block, [
                (KT // 2, q0, lambda j, slot: K.i["w_glu"][0][:, bass.ds(j * 2 * P + slot * P, P)], KT),
                (KT, q1, lambda j, slot: gate_b(j) if slot == 0 else K.i["w_br_b"][0][:, bass.ds(j * P, P)], KT)])

            @block.tensor
            def _(pe):
                with pe.Fori(0, KT // 2) as j:
                    for slot in range(2):
                        multiply_tile(K, pe, q0 + j, slot, out[slot], ys)
                pe.wait_ge(s_lo, KT + 1)
                with pe.Fori(0, KT) as j:
                    multiply_tile(K, pe, q1 + j, 0, out[0], K.hn)
                    multiply_tile(K, pe, q1 + j, 1, out[1], ys2)

            @block.scalar
            def _(act):
                act.sem_inc(s_hi, 1)
                with act.Fori(0, KT // 2) as j:
                    for slot in range(2):
                        split_high(K, act, q0 + j, slot)
                    for slot in range(2):
                        act.wait_ge(s_y, 2 * j + 1)
                        wait_tile(K, act, q0 + j, slot)
                        act.activation(sg[:, slot, :], out[slot][:, 0:T], ACT.Sigmoid,
                                       bias=K.b_glu[:, bass.ds(2 * j + slot, 1)]).then_inc(K.tile_read[slot], 1)
                    for slot in range(2):
                        act.wait_ge(s_y, 2 * j + slot + 2)
                        act.activation(one(ys2[:, 0, :, :], 2 * j + slot), y[:, slot, :], ACT.Copy).then_inc(s_hi, 1)
                with act.Fori(0, KT) as j:
                    for slot in range(2):
                        split_high(K, act, q1 + j, slot)
                    act.wait_ge(s_t, j + 1)
                    act.wait_ge(s_y, KT + 1)
                    wait_tile(K, act, q1 + j, 0)
                    act.activation(sg[:, 0, :], out[0][:, 0:T], ACT.Sigmoid).then_inc(K.tile_read[0], 1)
                act.wait_ge(s_mg, KT)
                for j in range(KT):
                    act.activation(ys[:, 0, j, :], mg[:, j, :], ACT.Copy).then_inc(s_hi, 1)

            @block.vector
            def _(dve):
                for s in (s_y, s_lo, s_t):
                    dve.sem_inc(s, 1)
                with dve.Fori(0, KT // 2) as j:
                    for slot in range(2):
                        k = 2 * j + slot
                        if slot == 0:
                            dve.wait_ge(s_lo, 2 * j + 1)
                        dve.wait_ge(s_hi, 2 * j + 1)
                        dve.tensor_tensor(y[:, slot, :], one(ys[:, 0, :, :], k), one(ys[:, 1, :, :], k), ALU.add)
                        dve.drain()
                        dve.wait_ge(K.tile_read[slot], q0 + j + 2)
                        dve.tensor_tensor(y[:, slot, :], y[:, slot, :], sg[:, slot, :], ALU.mult).then_inc(s_y, 1)
                    for slot in range(2):
                        k = 2 * j + slot
                        dve.wait_ge(s_y, k + 2)
                        dve.wait_ge(s_hi, k + 2)
                        dve.tensor_tensor(one(ys2[:, 1, :, :], k), y[:, slot, :], one(ys2[:, 0, :, :], k), ALU.subtract).then_inc(s_lo, 1)
                with dve.Fori(0, KT) as j:
                    wait_tile(K, dve, q1 + j, 1)
                    dve.wait_ge(K.tile_read[0], q1 + j + 2)
                    dve.tensor_tensor(y[:, 0, :], out[1][:, 0:T], sg[:, 0, :], ALU.mult).then_inc(s_t, 1)
                    dve.wait_ge(s_t, j + 2)
                    dve.sem_inc(K.tile_read[1], 1)
                    dve.tensor_tensor(one(mg, j), one(mg, j), y[:, 0, :], ALU.add).then_inc(s_mg, 1)
                    dve.wait_ge(s_mg, j + 1)
                for j in range(KT):
                    dve.wait_ge(s_hi, KT + j + 2)
                    dve.tensor_tensor(ys[:, 1, j, :], mg[:, j, :], ys[:, 0, j, :], ALU.subtract)


def add_product(K, dve, q, j, slot, out, x, gate, done):
    wait_tile(K, dve, q, slot)
    for a, n, c in SEGS:
        v = x[:, bass.ds(j, 1), a:a + n].rearrange("p o t -> p (o t)")
        i = dve.scalar_tensor_tensor(out=v, in0=out[:, a:a + n], scalar=K.mod[:, bass.ds(j + gate * KT, 1), c:c + 1].rearrange("p o c -> p (o c)"),
                                     in1=v, op0=ALU.mult, op1=ALU.add)
    i.then_inc(K.tile_read[slot], 1)


def phase_out(K, x, merged):
    q0 = K.q
    K.q += KT // 2
    with ExitStack() as st:
        out = [K.ps(f"o_out{s}", [P, 1536], st) for s in range(2)]
        s_x = K.sem("o_x_in")
        with K.nc.Block() as block:
            @block.sync
            def _(sync):
                sync.dma_start(x[:, :, :], K.scratch_x).then_inc(s_x, 16)
                with sync.Fori(0, KT // 2) as j:
                    for slot in range(2):
                        load_tile(K, sync, q0 + j, slot, K.i["w_out"][0][:, bass.ds(j * 2 * P + slot * P, P)])

            @block.gpsimd
            def _(pool):
                with pool.Fori(0, KT // 2) as j:
                    for slot in range(2):
                        split_low(K, pool, q0 + j, slot)

            @block.tensor
            def _(pe):
                with pe.Fori(0, KT // 2) as j:
                    for slot in range(2):
                        multiply_tile(K, pe, q0 + j, slot, out[slot], merged)

            @block.scalar
            def _(act):
                with act.Fori(0, KT // 2) as j:
                    for slot in range(2):
                        split_high(K, act, q0 + j, slot)

            @block.vector
            def _(dve):
                dve.wait_ge(s_x, 16)
                with dve.Fori(0, KT // 2) as j:
                    for slot in range(2):
                        add_product(K, dve, q0 + j, 2 * j + slot, slot, out[slot], x, 2, None)



def phase_mlp(K, x, acts):
    parts = [(0, 8), (8, 8), (16, FT - 16)]
    loops, q = [], K.q
    for f0, n in parts:
        loops += [(n, q), (KT // 2, q + n)]
        q += n + KT // 2
    K.q = q
    wgu, wd = K.i["w_gu"][0], K.i["w_down"][0]
    with ExitStack() as st:
        out = [K.ps(f"m_out{s}", [P, 1536], st) for s in range(2)]
        sg = K.sb("m_sg", [P, T], stack=st)
        a = K.sb("m_a", [P, T], stack=st)
        s_a, s_hi, s_lo, s_x = (K.sem("m_" + n) for n in ("act", "high", "low", "x"))
        with K.nc.Block() as block:
            tiles = []
            for i, (f0, n) in enumerate(parts):
                tiles.append((n, loops[2 * i][1], lambda j, slot, f0=f0: wgu[:, bass.ds(j * P + (f0 * P + slot * D_FF), P)], KT))
                tiles.append((KT // 2, loops[2 * i + 1][1], lambda j, slot, f0=f0, n=n: wd[f0 * P:(f0 + n) * P, bass.ds(j * 2 * P + slot * P, P)], n))
            split_streams(K, block, tiles)

            @block.tensor
            def _(pe):
                for i, (f0, n) in enumerate(parts):
                    with pe.Fori(0, n) as j:
                        for slot in range(2):
                            multiply_tile(K, pe, loops[2 * i][1] + j, slot, out[slot], K.hn)
                    pe.wait_ge(s_lo, f0 + n)
                    with pe.Fori(0, KT // 2) as j:
                        for slot in range(2):
                            multiply_tile(K, pe, loops[2 * i + 1][1] + j, slot, out[slot], acts[i % 2], n)

            @block.scalar
            def _(act):
                for i, (f0, n) in enumerate(parts):
                    with act.Fori(0, n) as j:
                        q = loops[2 * i][1] + j
                        for slot in range(2):
                            split_high(K, act, q, slot)
                        act.wait_ge(s_a, f0 + j + 1)
                        wait_tile(K, act, q, 0)
                        act.activation(sg[:, :], out[0][:, 0:T], ACT.Silu).then_inc(K.tile_read[0], 1)
                        act.wait_ge(s_a, f0 + j + 2)
                        act.activation(one(acts[i % 2][:, 0, :, :], j), a[:, :], ACT.Copy).then_inc(s_hi, 1)
                    with act.Fori(0, KT // 2) as j:
                        for slot in range(2):
                            split_high(K, act, loops[2 * i + 1][1] + j, slot, n)

            @block.vector
            def _(dve):
                dve.sem_inc(s_a, 1)
                for i, (f0, n) in enumerate(parts):
                    with dve.Fori(0, n) as j:
                        q = loops[2 * i][1] + j
                        wait_tile(K, dve, q, 1)
                        dve.wait_ge(K.tile_read[0], q + 2)
                        dve.tensor_tensor(a[:, :], out[1][:, 0:T], sg[:, :], ALU.mult).then_inc(s_a, 1)
                        dve.wait_ge(s_a, f0 + j + 2)
                        dve.sem_inc(K.tile_read[1], 1)
                        dve.wait_ge(s_hi, f0 + j + 1)
                        dve.tensor_tensor(one(acts[i % 2][:, 1, :, :], j), a[:, :], one(acts[i % 2][:, 0, :, :], j), ALU.subtract).then_inc(s_lo, 1)
                        dve.wait_ge(s_lo, f0 + j + 1)
                    dve.drain()
                    with dve.Fori(0, KT // 2) as j:
                        for slot in range(2):
                            add_product(K, dve, loops[2 * i + 1][1] + j, 2 * j + slot, slot, out[slot], x, 5, None)



def phase_final(K, x):
    with ExitStack() as st:
        act_part, pe_part, rstd, s_r = rstd_stages(K, st, x, "nf")
        rows = K.sb("out_rows", [P, 2, D], stack=st)
        tr = K.ps("out_tr", [P, 4, 512], st)
        s_n, s_t, s_c, s_out = K.sem("nf_scaled"), K.sem("nf_turned"), K.sem("nf_copied"), [K.sem("nf_out_0"), K.sem("nf_out_1")]
        NT = T // P
        with K.nc.Block() as block:
            @block.scalar
            def _(act):
                act_part(act)

            @block.vector
            def _(dve):
                dve.wait_ge(s_r, 1)
                for k in range(KT):
                    dve.scalar_tensor_tensor(out=x[:, k, :], in0=x[:, k, :], scalar=K.norm_g[2][:, k:k + 1], in1=rstd[:, :],
                                             op0=ALU.mult, op1=ALU.mult).then_inc(s_n, 1)
                for t in range(NT):
                    if t >= 2:
                        dve.wait_ge(s_out[t % 2], 16 * (t // 2))
                    for half in range(2):
                        dve.wait_ge(s_t, 2 * t + half + 1)
                        dve.tensor_copy(rows[:, t % 2, half * 512:(half + 1) * 512], tr[:, (2 * t + half) % 4, :]).then_inc(s_c, 1)

            @block.tensor
            def _(pe):
                pe_part(pe)
                pe.wait_ge(s_n, KT)
                for t in range(NT):
                    for half in range(2):
                        n = 2 * t + half
                        if n >= 4:
                            pe.wait_ge(s_c, n - 3)
                        for k in range(4):
                            mm = pe.transpose(tr[:, n % 4, k * P:(k + 1) * P], x[:, half * 4 + k, t * P:(t + 1) * P], K.ident[:, :])
                        mm.then_inc(s_t, 1)

            @block.sync
            def _(sync):
                for t in range(NT):
                    sync.wait_ge(s_c, 2 * t + 2)
                    dst = K.o["y_sample"][0, t * P:(t + 1) * P] if t < NS // P else K.o["y_prompt"][0, t * P - NS:(t + 1) * P - NS]
                    sync.dma_start(dst, rows[:, t % 2, :]).then_inc(s_out[t % 2], 16)
                for slot in range(2):
                    sync.wait_ge(s_out[slot], 16 * (NT // 2))


def build(nc, ins, outs, consts):
    with ExitStack() as ctx:
        K = setup(nc, ins, outs, consts, ctx)
        phase_input(K)
        end_phase(K)
        with ExitStack() as st:
            phase_decays(K, st)
            phase_heads(K, st)
            end_phase(K)
        phase_u(K)
        phase_s5(K)
        end_phase(K)
        with ExitStack() as st:
            mg = K.sb("merged", [P, KT, T], stack=st)
            with ExitStack() as s2:
                opairs = K.sb("o_pairs", [P, 2, KT, T], BF16, stack=s2)
                phase_branch_a(K, mg, opairs)
            ys = K.sb("ys", [P, 2, KT, T], BF16, stack=st)
            phase_glu(K, ys)
            ys2 = K.sb("ys2", [P, 2, KT, T], BF16, stack=st)
            phase_branch_b(K, mg, ys, ys2)
            end_phase(K)
            phase_out(K, mg, ys)
            with ExitStack() as s2:
                norm_modulate(K, s2, mg, K.mul2, 3, "n2")
                end_phase(K)
            phase_mlp(K, mg, (ys, ys2))
            phase_final(K, mg)



OUTS = [((1, NP_, D), "y_prompt"), ((1, NS, D), "y_sample"), ((1, 1, 2, H, DK, DK), "new_state_delta"),
        ((1, 1, 2, G_S5, N_S5), "new_state_s5_re"), ((1, 1, 2, G_S5, N_S5), "new_state_s5_im")]


def kernel(**inputs):
    import concourse.bacc as bacc
    from concourse.bass_utils import run_bass_kernel_spmd

    nc = bacc.Bacc("TRN2", target_bir_lowering=False, num_devices=1)
    arrays, ins, consts = {}, {}, {}
    for name, a in inputs.items():
        arrays["in_" + name] = np.ascontiguousarray(a)
        ins[name] = nc.dram_tensor("in_" + name, list(a.shape), F32, kind="ExternalInput").ap()
    for name, a in constants().items():
        arrays["const_" + name] = a
        consts[name] = nc.dram_tensor("const_" + name, list(a.shape), F32, kind="ExternalInput").ap()
    outs = {name: nc.dram_tensor(name, list(shape), F32, kind="ExternalOutput").ap() for shape, name in OUTS}
    build(nc, ins, outs, consts)
    r = run_bass_kernel_spmd(nc, [arrays], core_ids=[0])
    return tuple(r.results[0][name] for _, name in OUTS)
```

```python
from contextlib import ExitStack

import numpy as np
import concourse.bass as bass
from concourse import mybir

F32 = mybir.dt.float32
BF16 = mybir.dt.bfloat16
ALU = mybir.AluOpType
ACT = mybir.ActivationFunctionType

P = 128
D = 1024
KT = D // P
NS, NP_ = 1024, 256
T = NS + NP_
CHUNKS = ((0, 512), (512, 512), (1024, 256))
SEGS = ((0, NS, 0), (NS, NP_, 1))
GRID_W = 64
EPS = 1e-6
H = 8
DK = 128
C = 64
NC_S, NC_P = NS // C, NP_ // C
NPACK = NC_S + NC_P
QKV = 3 * H * DK
Z0 = QKV
B0 = Z0 + H * DK
A0 = B0 + 2 * H
U0 = A0 + 2 * H
GA0 = U0 + D
GB0 = GA0 + D
IN_DIM = GB0 + D
D_FF = 2816
FT = D_FF // P
CONV_W = 5
PADW = T + 2 * CONV_W - 2
LEVELS = 6
G_S5, N_S5, P_S5 = 64, 64, 16
L5 = 8
NC5_S, NC5_P = NS // L5, NP_ // L5
NC5 = NC5_S + NC5_P
GB = 4
MLP_PARTS = ((0, 8), (8, 8), (16, FT - 16))


class Names:
    pass


def constants():
    c = {}
    c["ident"] = np.eye(P, dtype=np.float32)
    quarter = D // 4
    omega = (1.0 / (np.float32(10000.0) ** (np.arange(quarter, dtype=np.float32) / np.float32(quarter)))).astype(np.float32)
    r = np.arange(NS // GRID_W, dtype=np.float32)[None, :] * omega[:, None]
    col = np.arange(GRID_W, dtype=np.float32)[None, :] * omega[:, None]
    rows = np.concatenate([np.sin(r), np.cos(r)], 0).astype(np.float32)
    cols = np.concatenate([np.sin(col), np.cos(col)], 0).astype(np.float32)
    c["pos_row"] = rows.reshape(4, P, -1).transpose(1, 0, 2).copy()
    c["pos_col"] = cols.reshape(4, P, -1).transpose(1, 0, 2).copy()
    i = np.arange(C)
    lvl = np.zeros((LEVELS, 2, C, 2, C), np.float32)
    for l in range(LEVELS):
        same = (i[:, None] >> (l + 1)) == (i[None, :] >> (l + 1))
        up, lo = (i >> l) & 1 == 1, (i >> l) & 1 == 0
        lvl[l, 0, :, 0] = same & up[:, None] & lo[None, :]
        lvl[l, 1, :, 1] = same & lo[:, None] & up[None, :]
    c["level"] = lvl.reshape(LEVELS, P, P).transpose(1, 0, 2).copy()
    c["level0_t"] = lvl[0].reshape(P, P).T.copy()
    seen = np.stack([i[None, :] >= i[:, None], i[None, :] <= i[:, None]])
    c["seen"] = np.where(seen, np.float32(1e30), np.float32(-1e30)).reshape(P, C).astype(np.float32)
    m = np.ones((2 * 32, T), np.float32)
    m[:, ::C] = 0.0
    c["restart"] = m
    sel = np.zeros((64, H, 2, C), np.float32)
    for h in range(H):
        sel[h, h, 0], sel[32 + h, h, 1] = 1.0, 1.0
    c["pick_head"] = sel.reshape(64, H, P)
    return c


CONST_SHAPES = {k: v.shape for k, v in constants().items()}


def setup(nc, ins, outs, consts, ctx):
    K = Names()
    K.nc, K.i, K.o, K.c = nc, ins, outs, consts

    def sb(name, shape, dt=F32, stack=ctx):
        return stack.enter_context(nc.sbuf_tensor(name, list(shape), dt))

    def ps(name, shape, stack):
        return stack.enter_context(nc.psum_tensor(name, list(shape), F32))

    K.phase_sems = []

    def sem(name):
        K.phase_sems.append(nc.alloc_semaphore(name=name))
        return K.phase_sems[-1]

    K.sb, K.ps, K.sem = sb, ps, sem
    K.hn = sb("hn", [P, 2, KT, T], BF16)
    K.w_raw = sb("w_raw", [P, 2, KT, P])
    K.w_pair = sb("w_pair", [P, 2, 2, KT, P], BF16)
    K.ident = sb("ident", [P, P])
    K.ones = sb("ones", [P, P])
    K.eps = sb("eps", [P, 1])
    K.mod = sb("mod", [P, 6 * KT, 2])
    K.vec = sb("vec", [P, 7 * KT + 1])
    K.conv_w = sb("conv_w_t", [P, CONV_W * 3 * H])
    K.norm_g = [K.vec[:, j * KT:(j + 1) * KT] for j in (2, 3, 4)]
    K.b_glu = K.vec[:, 5 * KT:6 * KT]
    K.s5_d = K.vec[:, 6 * KT:7 * KT]
    K.dn_norm = K.vec[:, 7 * KT:7 * KT + 1]
    K.mul1 = sb("mul1", [P, KT, 2])
    K.mul2 = sb("mul2", [P, KT, 2])
    K.w_loaded = [sem("w_loaded_0"), sem("w_loaded_1")]
    K.w_high = sem("w_high")
    K.w_low = sem("w_low")
    K.tile_done = sem("tile_done")
    K.tile_read = [sem("tile_read_0"), sem("tile_read_1")]
    K.pulse = sem("pulse")
    K.scratch_x = nc.dram_tensor("scratch_x", [P, KT, T], F32, kind="Internal").ap()
    K.scratch_o = nc.dram_tensor("scratch_o", [H, P, 2, T], BF16, kind="Internal").ap()
    K.scratch_u = nc.dram_tensor("scratch_u", [KT, P, L5, NC5], F32, kind="Internal").ap()
    K.scratch_y = nc.dram_tensor("scratch_y", [KT, P, L5, NC5], F32, kind="Internal").ap()
    K.q = 0
    K.phase_sems.clear()
    return K


def end_phase(K):
    K.nc.clear_and_free_semaphores(K.phase_sems)
    K.phase_sems.clear()
    K.nc.all_engine_barrier()



def load_tile(K, sync, q, slot, src, kt=KT):
    sync.wait_ge(K.w_low, 2 * q + slot + 1)
    sync.sem_inc(K.pulse, 1)
    sync.dma_start(K.w_raw[:, slot, 0:kt, :], src.rearrange("(k p) c -> p k c", p=P)).then_inc(K.w_loaded[slot], 16)


def split_high(K, act, q, slot, kt=KT):
    act.wait_ge(K.w_loaded[slot], (q + 1) * 16)
    act.wait_ge(K.tile_done, 2 * q + slot + 1)
    act.activation(K.w_pair[:, slot, 0, 0:kt, :], K.w_raw[:, slot, 0:kt, :], ACT.Copy).then_inc(K.w_high, 1)


def split_low(K, pool, q, slot, kt=KT):
    pool.wait_ge(K.w_high, 2 * q + slot + 1)
    pool.tensor_tensor(K.w_pair[:, slot, 1, 0:kt, :], K.w_raw[:, slot, 0:kt, :], K.w_pair[:, slot, 0, 0:kt, :],
                       ALU.subtract).then_inc(K.w_low, 1)


PASSES = ((0, 0), (0, 1), (1, 0))


def multiply_part(K, pe, slot, out, x, first, n, kt=KT):
    for i in range(first, first + n):
        k, (w, a), (c0, cn) = i // 9, PASSES[i // 3 % 3], CHUNKS[i % 3]
        mm = pe.matmul(out[:, c0:c0 + cn], K.w_pair[:, slot, w, k, :], x[:, a, k, c0:c0 + cn],
                       start=i < 3, stop=i >= 9 * kt - 3)
    if first + n == 9 * kt:
        mm.then_inc(K.tile_done, 1)


def multiply_tile(K, pe, q, slot, out, x, kt=KT):
    pe.wait_ge(K.w_low, 2 * q + slot + 3)
    pe.wait_ge(K.tile_read[slot], q + 1)
    multiply_part(K, pe, slot, out, x, 0, 9 * kt, kt)


def wait_tile(K, eng, q, slot):
    eng.wait_ge(K.tile_done, 2 * q + slot + 3)



def sources(K):
    w = {n: K.i[n][0] for n in ("w_in", "w_br_a", "w_glu", "w_br_b", "w_out")}
    cols = lambda a, j, step, c0: a[:, bass.ds(j * step + c0, P)]
    src = {
        "u": (lambda j, slot: cols(w["w_in"], j, 2 * P, U0 + slot * P), KT),
        "branch_a": (lambda j, slot: cols(w["w_br_a"], j, P, 0) if slot else cols(w["w_in"], j, P, GA0), KT),
        "glu": (lambda j, slot: cols(w["w_glu"], j, 2 * P, slot * P), KT),
        "branch_b": (lambda j, slot: cols(w["w_br_b"], j, P, 0) if slot else cols(w["w_in"], j, P, GB0), KT),
        "out": (lambda j, slot: cols(w["w_out"], j, 2 * P, slot * P), KT),
    }
    wgu, wd = K.i["w_gu"][0], K.i["w_down"][0]
    for i, (f0, n) in enumerate(MLP_PARTS):
        src[f"gate_up_{i}"] = (lambda j, slot, f0=f0: cols(wgu, j, P, f0 * P + slot * D_FF), KT)
        src[f"down_{i}"] = (lambda j, slot, f0=f0, n=n: cols(wd[f0 * P:(f0 + n) * P, :], j, 2 * P, slot * P), n)
    return src


def load_pair(K, sync, q, name, j):
    src, kt = sources(K)[name]
    for slot in range(2):
        load_tile(K, sync, q, slot, src(j, slot), kt)


def low_pair(K, pool, q, name):
    kt = sources(K)[name][1]
    for slot in range(2):
        split_low(K, pool, q, slot, kt)


def stream(K, block, loops, following, before=None):
    order = [n for n, _, _ in loops[1:]] + [following]

    @block.sync
    def _(sync):
        if before:
            before(sync)
        for (name, n, q), after in zip(loops, order):
            with sync.Fori(1, n) as j:
                load_pair(K, sync, q + j, name, j)
            if after:
                load_pair(K, sync, q + n, after, 0)

    @block.gpsimd
    def _(pool):
        for (name, n, q), after in zip(loops, order):
            with pool.Fori(1, n) as j:
                low_pair(K, pool, q + j, name)
            if after:
                low_pair(K, pool, q + n, after)



def phase_input(K):
    nc = K.nc
    with ExitStack() as outer, ExitStack() as st:
        x = K.sb("x_t", [P, KT, T], stack=outer)
        vrow = K.sb("vec_rows", [7 * KT + 1, P], stack=st)
        crow = K.sb("conv_rows", [CONV_W * 3 * H, P], stack=st)
        cond_s = K.sb("cond_s", [P, KT, 2], stack=st)
        HALF = 3 * D
        w = K.sb("w_ada_rows", [P, 2, HALF], stack=st)
        bias = K.sb("b_ada_rows", [2, 6 * D], stack=st)
        row = K.sb("mod_rows", [2, 6 * D], stack=st)
        tok = K.sb("x_rows", [P, 2, D], stack=st)
        pr = K.sb("pos_row_t", [P, 4, NS // GRID_W], stack=st)
        pc = K.sb("pos_col_t", [P, 4, GRID_W], stack=st)
        acc = K.ps("mod_acc", [P, 6, 512], st)
        tr = K.ps("tr", [P, 2, 512], st)
        s_small, s_cond, s_silu, s_w = K.sem("in_small"), K.sem("in_cond"), K.sem("in_silu"), [K.sem("in_w_0"), K.sem("in_w_1")]
        s_bias, s_pc, s_vt, s_vec = K.sem("in_bias"), K.sem("in_pos"), K.sem("vec_turned"), K.sem("vec_done")
        s_modk, s_modrow, s_modt = K.sem("mod_k_done"), K.sem("mod_row_done"), K.sem("mod_t_done")
        s_x, s_tr, s_trr, s_trd = [K.sem("x_in_0"), K.sem("x_in_1")], K.sem("x_turned"), K.sem("x_read_dve"), K.sem("x_spill")
        s_ones = K.sem("ones_done")
        s_modc = K.sem("mod_copied")
        NT = T // P

        with nc.Block() as block:
            @block.sync
            def _(sync):
                flat = {"c": K.i["c"][0], "c_ctx": K.i["c_ctx"], "norm1": K.i["norm1"][0], "norm2": K.i["norm2"][0],
                        "norm_f": K.i["norm_f"], "b_glu": K.i["b_glu"][0], "s5_d": K.i["s5_d"][0].rearrange("g p -> (g p)")}
                for j, v in enumerate(flat.values()):
                    sync.dma_start(vrow[j * KT:(j + 1) * KT, :], v.rearrange("(k p) -> k p", p=P)).then_inc(s_cond, 16)
                sync.dma_start(vrow[7 * KT:7 * KT + 1, :], K.i["dn_norm"]).then_inc(s_cond, 16)
                for j in range(CONV_W):
                    sync.dma_start(crow[j * 3 * H:(j + 1) * 3 * H, :], K.i["conv_w"][0, j].rearrange("(t p) -> t p", p=P)).then_inc(s_cond, 16)
                sync.dma_start(K.ident[:, :], K.c["ident"]).then_inc(s_small, 16)
                sync.dma_start(pr[:, :, :], K.c["pos_row"]).then_inc(s_pc, 16)
                sync.dma_start(pc[:, :, :], K.c["pos_col"]).then_inc(s_pc, 16)
                for half in range(2):
                    for k in range(KT):
                        n = half * KT + k
                        if n >= 2:
                            sync.wait_ge(s_modk, n - 1)
                        sync.dma_start(w[:, n % 2, :], K.i["w_ada"][0, k * P:(k + 1) * P, half * HALF:(half + 1) * HALF]).then_inc(s_w[n % 2], 16)

            @block.gpsimd
            def _(pool):
                pool.memset(K.ones[:, :], 1.0).then_inc(s_ones, 1)
                pool.memset(K.eps[:, :], EPS).then_inc(s_ones, 1)
                for c in range(2):
                    pool.dma_start(bias[c:c + 1, :], K.i["b_ada"]).then_inc(s_bias, 16)
                for s, n in ((K.w_low, 2), (K.tile_done, 2), (K.tile_read[0], 1), (K.tile_read[1], 1)):
                    pool.sem_inc(s, n)
                for t in range(NT):
                    if t >= 2:
                        pool.wait_ge(s_tr, 2 * (t - 1))
                    src = K.i["x_sample"][0, t * P:(t + 1) * P] if t < NS // P else K.i["x_prompt"][0, t * P - NS:(t + 1) * P - NS]
                    pool.dma_start(tok[:, t % 2, :], src).then_inc(s_x[t % 2], 16)
                pool.wait_ge(s_trr, 2 * NT)
                pool.dma_start(K.scratch_x, x[:, :, :]).then_inc(s_trd, 16)
                pool.wait_ge(s_trd, 16)

            @block.tensor
            def _(pe):
                pe.wait_ge(s_small, 16)
                pe.wait_ge(s_cond, 16 * 13)
                pe.transpose(tr[:, 0, 0:7 * KT + 1], vrow[:, :], K.ident[0:7 * KT + 1, 0:7 * KT + 1])
                pe.transpose(tr[:, 1, 0:CONV_W * 3 * H], crow[:, :], K.ident[0:120, 0:120]).then_inc(s_vt, 1)
                pe.wait_ge(s_vec, 1)
                for t in range(NT):
                    pe.wait_ge(s_x[t % 2], 16 * (t // 2 + 1))
                    for half in range(2):
                        n = 2 * t + half
                        if n >= 2:
                            pe.wait_ge(s_trr, n - 1)
                        for k in range(4):
                            c = (half * 4 + k) * P
                            mm = pe.transpose(tr[:, n % 2, k * P:(k + 1) * P], tok[:, t % 2, c:c + P], K.ident[:, :])
                        mm.then_inc(s_tr, 1)
                pe.wait_ge(s_silu, 1)
                for half in range(2):
                    if half:
                        pe.wait_ge(s_modrow, 6)
                    for k in range(KT):
                        n = half * KT + k
                        pe.wait_ge(s_w[n % 2], 16 * (n // 2 + 1))
                        for j in range(6):
                            mm = pe.matmul(acc[0:2, j, :], cond_s[:, k, :], w[:, n % 2, j * 512:(j + 1) * 512],
                                           start=k == 0, stop=k == KT - 1)
                        mm.then_inc(s_modk, 1)
                pe.wait_ge(s_modrow, 12)
                pe.wait_ge(s_trr, 2 * NT)
                for j in range(6 * KT):
                    mm = pe.transpose(tr[:, 0, 2 * j:2 * j + 2], row[0:2, j * P:(j + 1) * P], K.ident[0:2, 0:2])
                mm.then_inc(s_modt, 1)

            @block.scalar
            def _(act):
                act.wait_ge(s_vec, 1)
                for c in range(2):
                    i = act.activation(cond_s[:, :, c], K.vec[:, c * KT:(c + 1) * KT], ACT.Silu)
                i.then_inc(s_silu, 1)

            @block.vector
            def _(dve):
                dve.wait_ge(s_vt, 1)
                dve.tensor_copy(K.vec[:, :], tr[:, 0, 0:7 * KT + 1])
                dve.tensor_copy(K.conv_w[:, :], tr[:, 1, 0:CONV_W * 3 * H]).then_inc(s_vec, 1)
                dve.wait_ge(s_pc, 32)
                for t in range(NT):
                    for half in range(2):
                        n = 2 * t + half
                        dve.wait_ge(s_tr, n + 1)
                        dst = x[:, half * 4:half * 4 + 4, t * P:(t + 1) * P]
                        src = tr[:, n % 2, :]
                        if t < NS // P:
                            dst = dst.rearrange("p k (r c) -> p k r c", c=GRID_W)
                            src = src.rearrange("p (k r c) -> p k r c", k=4, c=GRID_W)
                            rows = P // GRID_W
                            if half == 0:
                                pos = pr[:, :, t * rows:(t + 1) * rows].unsqueeze(3).to_broadcast([P, 4, rows, GRID_W])
                            else:
                                pos = pc[:, :, :].unsqueeze(2).to_broadcast([P, 4, rows, GRID_W])
                            for r in range(rows):
                                i = dve.tensor_tensor(dst[:, :, r, :], src[:, :, r, :], pos[:, :, r, :], ALU.add)
                            i.then_inc(s_trr, 1)
                        else:
                            dve.tensor_copy(dst, src.rearrange("p (k c) -> p k c", k=4)).then_inc(s_trr, 1)
                dve.wait_ge(s_bias, 32)
                for half in range(2):
                    dve.wait_ge(s_modk, KT * (half + 1))
                    for j in range(6):
                        c = half * HALF + j * 512
                        dve.tensor_tensor(row[:, c:c + 512], acc[0:2, j, :], bias[:, c:c + 512], ALU.add).then_inc(s_modrow, 1)
                dve.wait_ge(s_modt, 1)
                dve.tensor_copy(K.mod[:, :, :], tr[:, 0, 0:12 * KT].rearrange("p (j c) -> p j c", c=2)).then_inc(s_modc, 1)
                dve.wait_ge(s_modc, 1)
                for m, j, s in ((K.mul1, 0, 1), (K.mul2, 1, 4)):
                    for c in range(2):
                        dve.tensor_tensor(m[:, :, c], K.norm_g[j], K.mod[:, s * KT:(s + 1) * KT, c], ALU.mult)
                dve.drain()
                for m, j in ((K.mul1, 0), (K.mul2, 1)):
                    for c in range(2):
                        dve.tensor_tensor(m[:, :, c], m[:, :, c], K.norm_g[j], ALU.add)

        st.close()
        norm_modulate(K, outer, x, K.mul1, 0, "n1")


def rstd_stages(K, st, x, name):
    sq = K.sb(name + "_sq", [P, 2, T], stack=st)
    ss = K.ps(name + "_ss", [P, 1536], st)
    rstd = K.sb(name + "_rstd", [P, T], stack=st)
    s_sq, s_k, s_r = K.sem(name + "_squared"), K.sem(name + "_summed"), K.sem(name + "_rstd_done")

    def act_part(act):
        for k in range(KT):
            if k >= 2:
                act.wait_ge(s_k, k - 1)
            act.activation(sq[:, k % 2, :], x[:, k, :], ACT.Square).then_inc(s_sq, 1)
        act.wait_ge(s_k, KT)
        act.activation(rstd[:, :], ss[:, 0:T], ACT.Ln, scale=1.0 / D, bias=K.eps[:, :])
        act.drain()
        act.activation(rstd[:, :], rstd[:, :], ACT.Exp, scale=-0.5).then_inc(s_r, 1)

    def pe_part(pe):
        for k in range(KT):
            pe.wait_ge(s_sq, k + 1)
            for c0, cn in CHUNKS:
                mm = pe.matmul(ss[:, c0:c0 + cn], K.ones[:, :], sq[:, k % 2, c0:c0 + cn], start=k == 0, stop=k == KT - 1)
            mm.then_inc(s_k, 1)

    return act_part, pe_part, rstd, s_r


def norm_modulate(K, st, x, mul, shift, name):
    t = K.sb(name + "_t", [P, 2, T], stack=st)
    act_part, pe_part, rstd, s_r = rstd_stages(K, st, x, name)
    s_t, s_h, s_hi, s_lo = (K.sem(name + n) for n in ("_scaled", "_hn", "_high", "_low"))
    with K.nc.Block() as block:
        @block.scalar
        def _(act):
            act_part(act)
            for k in range(KT):
                act.wait_ge(s_t, k + 1)
                for a, n, c in SEGS:
                    i = act.activation(t[:, k % 2, a:a + n], t[:, k % 2, a:a + n], ACT.Identity,
                                       scale=mul[:, k, c:c + 1], bias=K.mod[:, shift * KT + k, c:c + 1])
                i.then_inc(s_h, 1)
                act.wait_ge(s_h, k + 1)
                act.activation(K.hn[:, 0, k, :], t[:, k % 2, :], ACT.Copy).then_inc(s_hi, 1)

        @block.tensor
        def _(pe):
            pe_part(pe)

        @block.vector
        def _(dve):
            def low(k):
                dve.wait_ge(s_hi, k + 1)
                dve.tensor_tensor(K.hn[:, 1, k, :], t[:, k % 2, :], K.hn[:, 0, k, :], ALU.subtract).then_inc(s_lo, 1)

            dve.wait_ge(s_r, 1)
            for k in range(KT):
                if k >= 2:
                    dve.wait_ge(s_lo, k - 1)
                dve.tensor_tensor(t[:, k % 2, :], x[:, k, :], rstd[:, :], ALU.mult).then_inc(s_t, 1)
                if k:
                    low(k - 1)
            low(KT - 1)



def phase_decays(K, outer):
    rows = ((0, 0), (1, 32))
    K.cum_row = K.sb("cum_row", [64, NPACK, C], stack=outer)
    K.beta = K.sb("beta", [P, H, NPACK], stack=outer)
    K.neg_beta = K.sb("neg_beta", [P, H, NPACK], stack=outer)
    K.cum = K.sb("cum", [P, H, NPACK], stack=outer)
    K.gamma = K.sb("gamma", [P, H, NPACK], stack=outer)
    K.to_end = K.sb("to_end", [P, H, NPACK], stack=outer)
    K.carry = K.sb("carry", [P, 2, H, NPACK], stack=outer)
    with ExitStack() as st:
        w = K.sb("w_ba", [P, KT, 4 * H], stack=st)
        wp = K.sb("w_ba_pair", [P, 2, 2, KT, 64], BF16, stack=st)
        restart = K.sb("restart_t", [64, T], stack=st)
        par = K.sb("decay_par", [64, 2], stack=st)
        neg_a = K.sb("neg_a", [64, 1], stack=st)
        b_row = K.sb("b_row", [64, T], stack=st)
        s_row = K.sb("s_row", [64, T], stack=st)
        e_row = K.sb("e_row", [64, T], stack=st)
        c_row = K.sb("c_row", [64, T], stack=st)
        b_dup = K.sb("b_dup", [64, NPACK, 2, C], stack=st)
        c_dup = K.sb("c_dup", [64, NPACK, 2, C], stack=st)
        end = K.sb("end_rows", [64, NPACK], stack=st)
        diag = K.sb("end_diag", [64, 64, NPACK], stack=st)
        tmp = K.sb("to_end_log", [P, H, NPACK], stack=st)
        pb = K.ps("pb", [P, 1536], st)
        pa = K.ps("pa", [P, 1536], st)
        s_in, s_par, s_z, s_wh, s_wl = (K.sem("ba_" + n) for n in ("in", "par", "zeroed", "high", "low"))
        s_mm, s_act, s_dve, s_tr, s_pool = (K.sem("ba_" + n) for n in ("products", "act", "dve", "turned", "dup"))
        col = lambda x, j: x[:, 2 * H * j + 0:2 * H * (j + 1)]

        def segments():
            return ((0, NC_S), (NC_S, NC_P))

        with K.nc.Block() as block:
            @block.sync
            def _(sync):
                sync.dma_start(w[:, :, :], K.i["w_in"][0, :, B0:B0 + 4 * H].rearrange("(k p) c -> p k c", p=P)).then_inc(s_in, 16)
                sync.dma_start(restart[:, :], K.c["restart"]).then_inc(s_in, 16)
                sync.wait_ge(s_z, 1)
                with K.nc.allow_non_contiguous_dma(reason="32 values"):
                    for j, name in enumerate(("dt_bias", "a_log")):
                        for d, r in rows:
                            sync.dma_start(par[r:r + H, j:j + 1], K.i[name][0, d].rearrange("(h o) -> h o", o=1)).then_inc(s_par, 16)

            @block.gpsimd
            def _(pool):
                pool.memset(par[:, :], 0.0).then_inc(s_z, 1)
                pool.memset(wp[:, :, :, :, :], 0.0).then_inc(s_z, 1)
                pool.wait_ge(s_wh, 4)
                for j in range(2):
                    for d, r in rows:
                        s = w[:, :, 2 * H * j + H * d:2 * H * j + H * (d + 1)]
                        i = pool.tensor_tensor(wp[:, j, 1, :, r:r + H], s, wp[:, j, 0, :, r:r + H], ALU.subtract)
                i.then_inc(s_wl, 1)

            @block.tensor
            def _(pe):
                pe.wait_ge(s_wl, 1)
                for j, out in ((0, pb), (1, pa)):
                    for k in range(KT):
                        for v, a in ((0, 0), (0, 1), (1, 0)):
                            for c0, cn in CHUNKS:
                                mm = pe.matmul(out[0:64, c0:c0 + cn], wp[:, j, v, k, :], K.hn[:, a, k, c0:c0 + cn],
                                               start=(k, v, a) == (0, 0, 0), stop=(k, v, a) == (KT - 1, 1, 0))
                    mm.then_inc(s_mm, 1)
                pe.wait_ge(s_pool, 1)
                for t in range(NPACK):
                    mm = pe.transpose(pb[:, t * 64:(t + 1) * 64], b_dup[:, t, :, :], K.ident[0:64, 0:64])
                mm.then_inc(s_tr, 1)
                pe.wait_ge(s_dve, 6)
                for t in range(NPACK):
                    mm = pe.transpose(pa[:, t * 64:(t + 1) * 64], c_dup[:, t, :, :], K.ident[0:64, 0:64])
                mm.then_inc(s_tr, 1)
                pe.wait_ge(s_dve, 8)
                flat = diag[:, :, :].rearrange("p r t -> p (r t)")
                for c0, cn in CHUNKS:
                    mm = pe.matmul(pb[:, c0:c0 + cn], K.ones[0:64, :], flat[:, c0:c0 + cn], start=True, stop=True)
                mm.then_inc(s_tr, 1)

            @block.scalar
            def _(act):
                act.wait_ge(s_in, 32)
                act.wait_ge(s_z, 2)
                for j in range(2):
                    for d, r in rows:
                        act.activation(wp[:, j, 0, :, r:r + H], w[:, :, 2 * H * j + H * d:2 * H * j + H * (d + 1)], ACT.Copy).then_inc(s_wh, 1)
                act.wait_ge(s_mm, 1)
                act.activation(b_row[:, :], pb[0:64, 0:T], ACT.Sigmoid)
                act.drain()
                for d, r in rows:
                    for t0, tn in segments():
                        src = b_row[r:r + 32, :].rearrange("p (t c) -> p t c", c=C)[:, t0:t0 + tn]
                        src = src[:, ::-1] if d else src
                        for u in range(2):
                            i = act.activation(b_dup[r:r + 32, t0:t0 + tn, u, :], src, ACT.Copy)
                i.then_inc(s_pool, 1)
                act.wait_ge(s_dve, 2)
                act.activation(e_row[:, :], s_row[:, :], ACT.Abs)
                act.activation(neg_a[:, :], par[:, 1:2], ACT.Exp)
                act.drain()
                act.activation(e_row[:, :], e_row[:, :], ACT.Exp, scale=-1.0)
                act.drain()
                act.activation(e_row[:, :], e_row[:, :], ACT.Ln, bias=K.ones[0:64, 0:1]).then_inc(s_act, 1)
                act.wait_ge(s_dve, 9)
                act.activation(K.gamma[:, :, :], K.cum[:, :, :], ACT.Exp)
                act.activation(K.to_end[:, :, :], tmp[:, :, :], ACT.Exp)
                g = pb[:, 0:T].rearrange("p (r t) -> p r t", t=NPACK)
                for d, r in rows:
                    act.activation(K.carry[:, d, :, :], g[:, r:r + H, :], ACT.Exp)

            @block.vector
            def _(dve):
                dve.wait_ge(s_par, 64)
                dve.wait_ge(s_mm, 2)
                dve.tensor_scalar(s_row[:, :], pa[0:64, 0:T], par[:, 0:1], None, ALU.add).then_inc(s_dve, 2)
                dve.wait_ge(s_act, 1)
                dve.scalar_tensor_tensor(out=s_row[:, :], in0=s_row[:, :], scalar=0.0, in1=e_row[:, :], op0=ALU.max, op1=ALU.add)
                dve.drain()
                dve.tensor_scalar(s_row[:, :], s_row[:, :], neg_a[:, :], -1.0, ALU.mult, ALU.mult)
                dve.drain()
                dve.tensor_tensor_scan(c_row[0:32, :], restart[0:32, :], s_row[0:32, :], 0.0, ALU.mult, ALU.add)
                dve.tensor_tensor_scan(c_row[32:64, ::-1], restart[32:64, :], s_row[32:64, ::-1], 0.0, ALU.mult, ALU.add)
                dve.drain()
                for d, r in rows:
                    for t0, tn in segments():
                        src = c_row[r:r + 32, :].rearrange("p (t c) -> p t c", c=C)[:, t0:t0 + tn]
                        src = src[:, ::-1] if d else src
                        dve.tensor_copy(K.cum_row[r:r + 32, t0:t0 + tn, :], src)
                        for u in range(2):
                            i = dve.tensor_copy(c_dup[r:r + 32, t0:t0 + tn, u, :], src)
                dve.drain().then_inc(s_dve, 4)
                dve.tensor_copy(end[0:32, :], K.cum_row[0:32, :, C - 1])
                dve.tensor_copy(end[32:64, :], K.cum_row[32:64, :, 0])
                dve.drain()
                dve.tensor_tensor(diag[:, :, :], end[:, :].unsqueeze(1).to_broadcast([64, 64, NPACK]),
                                  K.ident[0:64, 0:64].unsqueeze(2).to_broadcast([64, 64, NPACK]), ALU.mult)
                dve.wait_ge(s_tr, 2)
                for out, src in ((K.beta, pb), (K.cum, pa)):
                    v = src[:, 0:T].rearrange("p (t r) -> p r t", r=64)
                    for d, r in rows:
                        i = dve.tensor_copy(out[64 * d:64 * d + 64, :, :], v[64 * d:64 * d + 64, r:r + H, :])
                i.then_inc(s_dve, 2)
                dve.wait_ge(s_dve, 8)
                dve.tensor_scalar(K.neg_beta[:, :, :], K.beta[:, :, :], -1.0, None, ALU.mult)
                dve.wait_ge(s_tr, 3)
                g = pb[:, 0:T].rearrange("p (r t) -> p r t", t=NPACK)
                for d, r in rows:
                    i = dve.tensor_tensor(tmp[64 * d:64 * d + 64, :, :], g[64 * d:64 * d + 64, r:r + H, :], K.cum[64 * d:64 * d + 64, :, :], ALU.subtract)
                i.then_inc(s_dve, 1)


D_RING, S_RING = 3, 2
D_USES, S_USES = 153, 50
STEPS = [t for p in zip(range(NC_P), range(NC_S, NPACK)) for t in p] + list(range(NC_P, NC_S))
SEQ_END = {NC_S - 1, NPACK - 1}


def phase_heads(K, outer):
    nc = K.nc
    with ExitStack() as st:
        N = PADW - CONV_W + 1
        size = lambda name: 2 * N if name in ("xti", "vi", "kd") else 2 * PADW if name in ("kp", "vt") else NPACK * P
        big = lambda name: K.sb(name, [P, size(name)], stack=st)
        pack = lambda t: t[:, 0:NPACK * P].rearrange("p (t c) -> p t c", c=P)
        kp_, qp_, at_, mt_, x_, xt_, v_, vt_, gk_, kd_ = (big(n) for n in ("kp", "qp", "at", "mt", "xi", "xti", "vi", "vt", "gk", "kd"))
        kp, qp, at, mt, xi, xti, vi, vt, gk, kd = (pack(t) for t in (kp_, qp_, at_, mt_, x_, xt_, v_, vt_, gk_, kd_))
        op = gk
        uv, wk = vi, xi
        two = lambda t: t[:, :].rearrange("p (a c) -> p a c", a=2)
        silu, sq = two(xt_), two(kd_)
        raw_kq = two(kp_)
        cv = [silu[:, 0, :], silu[:, 1, :], raw_kq[:, 0, :]]
        raw = [raw_kq[:, 0, :], raw_kq[:, 1, :], vt_[:, 0:PADW]]
        dt = K.sb("dt", [P, NPACK, C], stack=st)
        dtb = K.sb("dtb", [P, NPACK, C], stack=st)
        zs = K.sb("zs", [P, T], stack=st)
        os_ = K.sb("os", [P, 2, N], stack=st)
        opair = K.sb("o_pair", [P, 2, T], BF16, stack=st)
        state = K.sb("state", [P, 2, 2, P], stack=st)
        u = K.sb("u", [P, 2, 2, P], stack=st)
        tq = K.sb("tq", [P, 2, P], stack=st)
        hs = K.sb("head_scalars", [P, 5, NPACK], stack=st)
        hc = K.sb("head_carry", [P, 2, NPACK], stack=st)
        hw = K.sb("head_conv", [P, CONV_W, 3], stack=st)
        pick_h = K.sb("pick_h", [64, P], stack=st)
        level = K.sb("level_t", [P, LEVELS, P], stack=st)
        level0_t = K.sb("level0_t_t", [P, P], stack=st)
        seen = K.sb("seen_t", [P, C], stack=st)
        bank = K.ps("bank", [P, 8, 512], st)
        gemm_out = bank[:, D_RING + S_RING:8, :].rearrange("p b c -> p (b c)")
        s = Names()
        s.consts = K.sem("h_consts")
        s.head_end = K.sem("h_head_end")
        s.state_in = K.sem("h_state_in")
        s.pick_in = K.sem("h_pick_in")
        s.pads = K.sem("h_pads")
        s.conv = K.sem("h_conv")
        s.silu = K.sem("h_silu")
        s.squared = K.sem("h_squared")
        s.inv_norm = K.sem("h_inv_norm")
        s.packed = K.sem("h_packed")
        s.turned_packs = K.sem("h_turned_packs")
        s.scal = K.sem("h_scal")
        s.full_d = K.sem("h_full_d")
        s.free_d = K.sem("h_free_d")
        s.full_s = K.sem("h_full_s")
        s.free_s = K.sem("h_free_s")
        s.dt_log = K.sem("h_dt_log")
        s.dt = K.sem("h_dt")
        s.dtb = K.sem("h_dtb")
        s.mt = K.sem("h_mt")
        s.inv = K.sem("h_inv")
        s.vmask = K.sem("h_vmask")
        s.tok_v = K.sem("h_tok_v")
        s.uv = K.sem("h_uv")
        s.xt_level0 = K.sem("h_xt_level0")
        s.wk = K.sem("h_wk")
        s.u = K.sem("h_u")
        s.state_new = K.sem("h_state_new")
        s.o_add = K.sem("h_o_add")
        s.o_sum = K.sem("h_o_sum")
        s.o_sq = K.sem("h_o_sq")
        s.o_rstd = K.sem("h_o_rstd")
        s.o_fin = K.sem("h_o_fin")
        s.o_high = K.sem("h_o_high")
        s.o_low = K.sem("h_o_low")
        s.o_store = K.sem("h_o_store")
        s.s_store = K.sem("h_s_store")
        s.state_zero = K.sem("h_state_zero")
        s.dx = K.sem("h_dx")
        q0 = K.q
        K.q += 2 * H
        SEG = ((0, NC_S, 0, 0), (NC_S, NC_P, NS, NS + CONV_W - 1))
        toks = lambda x, t0, n: x[:, t0:t0 + n * C].rearrange("p (t c) -> p t c", c=C)
        grp = lambda g: slice(4 * g, 4 * g + 4)
        NG = NPACK // 4

        class Ring:
            def __init__(self, full, free, first, size, uses):
                self.full, self.free, self.first, self.size, self.uses = full, free, first, size, uses

            def bank(self, n):
                return bank[:, self.first + n % self.size, :]

            def to_write(self, pe, h, n):
                pe.wait_ge(self.free, h * self.uses + n + 1)
                return self.bank(n)

            def to_read(self, eng, h, n):
                eng.wait_ge(self.full, h * self.uses + n + 1)
                return self.bank(n)

        rd = Ring(s.full_d, s.free_d, 0, D_RING, D_USES)
        rs = Ring(s.full_s, s.free_s, D_RING, S_RING, S_USES)
        D_DT, D_KK, D_INV0 = 0, 3, 3 + 2 * NG
        D_LEVEL = [None] + [D_INV0 + NG + 3 * NG * (l - 1) for l in range(1, LEVELS)]
        D_WK = D_LEVEL[LEVELS - 1] + 2 * NG
        D_SCAN = D_WK + NG
        D_PAD = D_USES - D_SCAN - 3 * NPACK
        assert D_RING == 3 and 0 <= D_PAD < D_RING and D_USES % D_RING == 0 and S_USES % S_RING == 0
        S_SS, S_KT, S_UV, S_Q = 0, 6, 6 + 2 * NG, 6 + 3 * NG
        TURN_AFTER = {8: 0, 9: 4, 12: 1, 16: 2, NPACK - 1: 3}
        s_q, s_ot, n = {}, {}, S_Q
        for i in range(NPACK):
            s_q[i], n = n, n + 1
            if i in TURN_AFTER:
                s_ot[TURN_AFTER[i]], n = n, n + 1
        for i, g in TURN_AFTER.items():
            assert all(t in STEPS[:i + (i == NPACK - 1)] for t in range(4 * g, 4 * g + 4))
        S_RMS = n
        TILE_ENDS = (4, 10, 16)
        TAPS = {5 + w: [(0, w)] for w in range(CONV_W)} | {11 + w: [(1, w)] for w in range(CONV_W)}
        TAPS |= {17: [(2, 0), (2, 1)], 18: [(2, 2), (2, 3)], 19: [(2, 4)]}
        S_PAD = S_USES - S_RMS - 3
        assert 0 <= S_PAD < S_RING
        assert NG == LEVELS - 1
        quad = lambda b: b[:, :].rearrange("p (t c) -> p t c", c=P)

        with nc.Block() as block:
            @block.sync
            def _(sync):
                for dst, name in ((level[:, :, :], "level"), (level0_t[:, :], "level0_t"), (seen[:, :], "seen")):
                    sync.dma_start(dst, K.c[name]).then_inc(s.consts, 16)
                def weights(h):
                    for t, c0 in enumerate((H * DK, 0, 2 * H * DK, Z0)):
                        load_tile(K, sync, q0 + 2 * h + t // 2, t % 2, K.i["w_in"][0][:, bass.ds(h * P + c0, P)])

                def inputs(h):
                    sync.wait_ge(s.head_end, 4 * h + 4)
                    sync.wait_ge(s.s_store, 32 * h + 32)
                    sync.sem_inc(K.pulse, 1)
                    for d in range(2):
                        if d == 0:
                            sync.dma_start(pick_h[:, :].unsqueeze(1), K.c["pick_head"][:, bass.ds(h, 1), :]).then_inc(s.pick_in, 16)
                        sync.dma_start(state[:, 0, d, :], K.i["state_delta"][0, 0, d][bass.ds(h, 1)].rearrange("o k v -> (o k) v")).then_inc(s.state_in, 16)

                weights(0)
                with sync.Fori(0, H - 1) as h:
                    inputs(h)
                    weights(h + 1)
                inputs(H - 1)
                load_pair(K, sync, q0 + 2 * H, "u", 0)

            @block.gpsimd
            def _(pool):
                pool.memset(at[:, :, :], 0.0)
                pool.memset(mt[:, :, :], 0.0)
                pool.memset(u[:, :, :, :], 0.0).then_inc(s.pads, 1)
                pool.wait_ge(s.consts, 48)
                pool.sem_inc(s.free_d, D_RING)
                pool.sem_inc(s.free_s, S_RING)
                pool.sem_inc(s.head_end, 4)

                def zeros_around():
                    for a in (0, 2 + NS, 2 * CONV_W - 4 + NS + NP_ + 0):
                        n = 4 if a == 2 + NS else 2
                        pool.memset(raw_kq[:, :, a:a + n], 0.0)
                        i = pool.memset(raw[2][:, a:a + n], 0.0)
                    i.then_inc(s.pads, 1)

                def low_parts(h, tiles):
                    for t in tiles:
                        split_low(K, pool, q0 + 2 * h + t // 2, t % 2)

                def head(h, following):
                    pool.wait_ge(s.head_end, 4 * h + 4)
                    pool.wait_ge(s.s_store, 32 * h + 32)
                    pool.sem_inc(K.pulse, 1)
                    pool.memset(state[:, 1, :, :], 0.0).then_inc(s.state_zero, 1)
                    pool.wait_ge(s.dt, h + 1)
                    pool.tensor_tensor(dtb[:, :, :], dt[:, :, :], hs[:, 0, :].unsqueeze(2).to_broadcast([P, NPACK, C]), ALU.mult).then_inc(s.dtb, 1)
                    for g in range(NG):
                        pool.wait_ge(s.mt, NG * h + g + 1)
                        pool.tensor_tensor(xti[:, grp(g), :], mt[:, grp(g), :], level0_t[:, :].unsqueeze(1).to_broadcast([P, 4, P]), ALU.mult).then_inc(s.xt_level0, 1)
                    if following:
                        low_parts(h + 1, (0, 1))
                        pool.wait_ge(s.uv, NG * (h + 1))
                        pool.sem_inc(K.pulse, 1)
                        zeros_around()
                        low_parts(h + 1, (2, 3))
                    else:
                        low_pair(K, pool, q0 + 2 * H, "u")
                    pool.sem_inc(s.head_end, 1)

                zeros_around()
                low_parts(0, range(4))
                with pool.Fori(0, H - 1) as h:
                    head(h, True)
                head(H - 1, False)

            @block.tensor
            def _(pe):
                def tile_part(h, t, first, n):
                    q, slot = q0 + 2 * h + t // 2, t % 2
                    if first == 0:
                        pe.wait_ge(K.w_low, 2 * q + slot + 3)
                        pe.wait_ge(K.tile_read[1 - slot], q + 1 + slot)
                    multiply_part(K, pe, slot, gemm_out, K.hn, first, n)

                def next_head(h, i, place):
                    for t, end in enumerate(TILE_ENDS):
                        begin = TILE_ENDS[t - 1] + 1 if t else 0
                        if begin <= i <= end:
                            points = 2 * (end - begin + 1) - 1
                            point = 2 * (i - begin) + place - 1
                            if point >= 0:
                                first = 9 * KT * point // points
                                tile_part(h + 1, t, first, 9 * KT * (point + 1) // points - first)

                def head(h, following):
                    pe.wait_ge(s.head_end, 4 * h + 4)
                    third = 3 * KT
                    tile_part(h, 3, 0, third)
                    n = S_SS
                    for j in range(2):
                        pe.wait_ge(s.squared, 2 * h + j + 1)
                        for c0, cn in ((0, 512), (512, 512), (1024, PADW - 1024 - CONV_W + 1)):
                            if n == S_SS + S_RING:
                                tile_part(h, 3, third, third)
                            b = rs.to_write(pe, h, n)
                            pe.matmul(b[:, 0:cn], K.ones[:, :], sq[:, j, c0:c0 + cn], start=True, stop=True).then_inc(rs.full, 1)
                            n += 1
                    pe.wait_ge(s.pick_in, 16 * (h + 1))
                    for j, (t0, tn) in enumerate(((0, 8), (8, 8), (16, 4))):
                        b = rd.to_write(pe, h, D_DT + j)
                        pe.matmul(b[:, 0:tn * C], pick_h[:, :], K.cum_row[:, t0:t0 + tn, :], start=True, stop=True).then_inc(rd.full, 1)
                    tile_part(h, 3, 2 * third, third)
                    pe.wait_ge(s.turned_packs, 3 * h + 2)
                    for g in range(NG):
                        for j, rhs in enumerate((kp, qp)):
                            b = quad(rd.to_write(pe, h, D_KK + 2 * g + j))
                            for t in range(4):
                                mm = pe.matmul(b[:, t, :], kp[:, 4 * g + t, :], rhs[:, 4 * g + t, :], start=True, stop=True)
                            mm.then_inc(rd.full, 1)
                    for g in range(NG):
                        pe.wait_ge(s.mt, NG * h + g + 1)
                        b = quad(rd.to_write(pe, h, D_INV0 + g))
                        for t in range(4):
                            mm = pe.transpose(b[:, t, :], mt[:, 4 * g + t, :], K.ident[:, :])
                        mm.then_inc(rd.full, 1)
                    pe.wait_ge(s.turned_packs, 3 * h + 3)
                    for l in range(1, LEVELS):
                        for j, src in enumerate((kp, vt)):
                            b = quad(rs.to_write(pe, h, S_KT + 2 * (l - 1) + j))
                            for t in range(4):
                                mm = pe.transpose(b[:, t, :], src[:, 4 * (l - 1) + t, :], K.ident[:, :])
                            mm.then_inc(rs.full, 1)
                        n = D_LEVEL[l]
                        for g in range(NG):
                            pe.wait_ge(s.inv, NG * (LEVELS * h + l - 1) + g + 1)
                            b = quad(rd.to_write(pe, h, n))
                            n += 1
                            for t in range(4):
                                mm = pe.matmul(b[:, t, :], mt[:, 4 * g + t, :], xi[:, 4 * g + t, :], start=True, stop=True)
                            mm.then_inc(rd.full, 1)
                        for g in range(NG):
                            pe.wait_ge(s.vmask, NG * ((LEVELS - 1) * h + l - 1) + g + 1)
                            if l < LEVELS - 1:
                                b = quad(rd.to_write(pe, h, n))
                                n += 1
                                for t in range(4):
                                    mm = pe.matmul(b[:, t, :], xti[:, 4 * g + t, :], vi[:, 4 * g + t, :], start=True, stop=True)
                                mm.then_inc(rd.full, 1)
                            b = quad(rd.to_write(pe, h, n))
                            n += 1
                            for t in range(4):
                                mm = pe.matmul(b[:, t, :], vi[:, 4 * g + t, :], xti[:, 4 * g + t, :], start=True, stop=True)
                            mm.then_inc(rd.full, 1)
                    for g in range(NG):
                        pe.wait_ge(s.inv, NG * (LEVELS * h + LEVELS - 1) + g + 1)
                        pe.wait_ge(s.tok_v, NG * h + g + 1)
                        b = quad(rs.to_write(pe, h, S_UV + g))
                        for t in range(4):
                            mm = pe.matmul(b[:, t, :], xti[:, 4 * g + t, :], vt[:, 4 * g + t, :], start=True, stop=True)
                        mm.then_inc(rs.full, 1)
                        b = quad(rd.to_write(pe, h, D_WK + g))
                        for t in range(4):
                            mm = pe.matmul(b[:, t, :], gk[:, 4 * g + t, :], xti[:, 4 * g + t, :], start=True, stop=True)
                        mm.then_inc(rd.full, 1)
                    pe.wait_ge(s.state_in, 32 * (h + 1))
                    pe.wait_ge(s.state_zero, h + 1)
                    done = {}
                    for i, t in enumerate(STEPS):
                        q = int(t >= NC_S)
                        pe.wait_ge(s.uv, NG * h + t // 4 + 1)
                        pe.wait_ge(s.wk, NG * h + t // 4 + 1)
                        if q in done:
                            pe.wait_ge(s.state_new, NPACK * h + done[q] + 1)
                        done[q] = i
                        if i == 0:
                            pe.wait_ge(rd.free, h * D_USES + D_SCAN + 3)
                        b = rd.bank(D_SCAN + 3 * i)
                        for d in range(2):
                            mm = pe.matmul(b[64 * d:64 * d + 64, 0:P], wk[:, t, 64 * d:64 * d + 64], state[:, q, d, :], start=True, stop=True)
                        mm.then_inc(rd.full, 1)
                        b = rs.to_write(pe, h, s_q[i])
                        for d in range(2):
                            mm = pe.matmul(b[64 * d:64 * d + 64, 0:P], qp[:, t, 64 * d:64 * d + 64], state[:, q, d, :], start=True, stop=True)
                        mm.then_inc(rs.full, 1)
                        if following:
                            next_head(h, i, 0)
                        pe.wait_ge(s.u, NPACK * h + i + 1)
                        if i:
                            pe.wait_ge(s.state_new, NPACK * h + i)
                        b = rd.bank(D_SCAN + 3 * i + 1)
                        pe.matmul(b[:, 0:2 * P], kd[:, t, :], u[:, i % 2, :, :].rearrange("p d c -> p (d c)"), start=True, stop=True).then_inc(rd.full, 1)
                        if i:
                            pe.wait_ge(s.o_add, NPACK * h + i)
                        b = rd.bank(D_SCAN + 3 * i + 2)
                        pe.matmul(b[:, 0:P], at[:, t, :], u[:, i % 2, 0, :], start=True, stop=False)
                        pe.matmul(b[:, 0:P], at[:, t, :], u[:, i % 2, 1, :], start=False, stop=True).then_inc(rd.full, 1)
                        if following:
                            next_head(h, i, 1)
                        if i in TURN_AFTER:
                            g = TURN_AFTER[i]
                            pe.wait_ge(s.o_add, NPACK * h + i + (i == NPACK - 1))
                            b = quad(rs.to_write(pe, h, s_ot[g]))
                            for j in range(4):
                                mm = pe.transpose(b[:, j, :], op[:, 4 * g + j, :], K.ident[:, :])
                            mm.then_inc(rs.full, 1)
                    pe.wait_ge(s.o_sq, h + 1)
                    for j, (c0, cn) in enumerate(CHUNKS):
                        b = rs.to_write(pe, h, S_RMS + j)
                        pe.matmul(b[:, 0:cn], K.ones[:, :], sq[:, 0, c0:c0 + cn], start=True, stop=True).then_inc(rs.full, 1)
                    pe.drain().then_inc(s.head_end, 1)
                    for ring, n in ((rd, D_PAD), (rs, S_PAD)):
                        if n:
                            pe.sem_inc(ring.full, n)

                for t in range(3):
                    tile_part(0, t, 0, 9 * KT)
                with pe.Fori(0, H - 1) as h:
                    head(h, True)
                head(H - 1, False)

            @block.scalar
            def _(act):
                def high_part(h, t):
                    split_high(K, act, q0 + 2 * h + t // 2, t % 2)

                def copy_raw(h, t):
                    wait_tile(K, act, q0 + 2 * h + t // 2, t % 2)
                    for a, n, _ in SEGS:
                        b = 2 + a + (4 if a else 0)
                        i = act.activation(raw[t][:, b:b + n], gemm_out[:, a:a + n], ACT.Copy)
                    i.then_inc(K.tile_read[t % 2], 1)

                def silu_of(h, j):
                    act.wait_ge(s.conv, 3 * h + j + 1)
                    act.activation(silu[:, j, 0:PADW - 4], silu[:, j, 0:PADW - 4], ACT.Silu).then_inc(s.silu, 1)

                def head(h, following):
                    act.wait_ge(s.head_end, 4 * h + 4)
                    act.wait_ge(s.scal, h + 1)
                    act.wait_ge(s.silu, 2 * h + 2)
                    for j in range(2):
                        act.activation(sq[:, j, 0:PADW - 4], silu[:, j, 0:PADW - 4], ACT.Square).then_inc(s.squared, 1)
                    act.wait_ge(s.conv, 3 * h + 3)
                    for t0, tn, _, p0 in SEG:
                        src = toks(cv[2], p0, tn)
                        act.activation(vt[:, t0:t0 + tn, 0:C], src, ACT.Silu)
                        act.activation(vt[:, t0:t0 + tn, C:P], src[:, ::-1], ACT.Silu)
                    for j in range(2):
                        for m, (c0, cn) in enumerate(((0, 512), (512, 512), (1024, PADW - 4 - 1024))):
                            b = rs.to_read(act, h, S_SS + 3 * j + m)
                            act.activation(os_[:, j, c0:c0 + cn], b[:, 0:cn], ACT.Ln, bias=K.eps[:, :]).then_inc(rs.free, 1)
                        act.drain()
                        act.activation(os_[:, j, 0:PADW - 4], os_[:, j, 0:PADW - 4], ACT.Exp, scale=-0.5).then_inc(s.inv_norm, 1)
                    act.wait_ge(s.dt_log, h + 1)
                    act.activation(dt[:, :, :], dt[:, :, :], ACT.Exp).then_inc(s.dt, 1)
                    for j, x in enumerate((kp, qp)):
                        act.wait_ge(s.packed, 2 * h + j + 1)
                        for t0, tn, _, _ in SEG:
                            i = act.activation(x[:, t0:t0 + tn, C:P], x[:, t0:t0 + tn, 0:C][:, ::-1], ACT.Copy)
                        i.then_inc(s.turned_packs, 1)
                    act.drain().then_inc(s.turned_packs, 1)
                    for g in range(NG):
                        b = quad(rs.to_read(act, h, S_KT + 2 * g))
                        for t in range(4):
                            act.activation(gk[:, 4 * g + t, :], b[:, t, :], ACT.Copy, scale=hs[:, 3, 4 * g + t:4 * g + t + 1])
                        for t in range(4):
                            i = act.activation(kd[:, 4 * g + t, :], b[:, t, :], ACT.Copy, scale=hs[:, 4, 4 * g + t:4 * g + t + 1])
                        i.then_inc(rs.free, 1)
                        b = rs.to_read(act, h, S_KT + 2 * g + 1)
                        act.activation(vt[:, grp(g), :], quad(b), ACT.Copy).then_inc(rs.free, 1)
                        act.drain().then_inc(s.tok_v, 1)
                    wait_tile(K, act, q0 + 2 * h + 1, 1)
                    act.activation(zs[:, :], gemm_out[:, 0:T], ACT.Silu).then_inc(K.tile_read[1], 1)
                    high_part(h + 1, 0)
                    high_part(h + 1, 1)
                    for g in range(NG):
                        b = quad(rs.to_read(act, h, S_UV + g))
                        for t in range(4):
                            i = act.activation(uv[:, 4 * g + t, :], b[:, t, :], ACT.Copy, scale=hs[:, 0, 4 * g + t:4 * g + t + 1])
                        i.then_inc(rs.free, 1)
                        act.drain().then_inc(s.uv, 1)
                    for i, t in enumerate(STEPS):
                        b = rs.to_read(act, h, s_q[i])
                        if i >= 2:
                            act.wait_ge(s.o_add, NPACK * h + i - 1)
                        act.activation(tq[:, i % 2, :], b[:, 0:P], ACT.Copy, scale=hs[:, 3, t:t + 1]).then_inc(rs.free, 1)
                        if following and i in TILE_ENDS:
                            copy_raw(h + 1, TILE_ENDS.index(i))
                            if i < TILE_ENDS[2]:
                                high_part(h + 1, TILE_ENDS.index(i) + 2)
                        if following and i in (11, 17):
                            silu_of(h + 1, i // 17)
                        if i not in TURN_AFTER:
                            continue
                        g = TURN_AFTER[i]
                        b = quad(rs.to_read(act, h, s_ot[g]))
                        t0, tn, _, _ = SEG[g // 4]
                        lo = 4 * g - t0
                        f = os_[:, 0, 0:T].rearrange("p (t c) -> p t c", c=C)
                        r = os_[:, 1, 0:T].rearrange("p (t c) -> p t c", c=C)
                        first = t0 + tn - 1 - lo
                        act.activation(f[:, grp(g), :], b[:, :, 0:C], ACT.Copy)
                        act.activation(r[:, first - 3:first + 1, :][:, ::-1], b[:, :, C:P], ACT.Copy).then_inc(rs.free, 1)
                    act.wait_ge(s.state_new, (h + 1) * NPACK)
                    for d in range(2):
                        act.dma_start(K.o["new_state_delta"][0, 0, d][bass.ds(h, 1)].rearrange("o k v -> (o k) v"), state[:, 1, d, :]).then_inc(s.s_store, 16)
                    act.wait_ge(s.o_sum, h + 1)
                    act.activation(sq[:, 0, 0:T], os_[:, 0, 0:T], ACT.Square).then_inc(s.o_sq, 1)
                    for m, (c0, cn) in enumerate(CHUNKS):
                        b = rs.to_read(act, h, S_RMS + m)
                        act.activation(os_[:, 1, c0:c0 + cn], b[:, 0:cn], ACT.Ln, scale=1.0 / DK, bias=K.eps[:, :]).then_inc(rs.free, 1)
                    act.drain()
                    if S_PAD:
                        act.sem_inc(rs.free, S_PAD)
                    act.activation(os_[:, 1, 0:T], os_[:, 1, 0:T], ACT.Exp, scale=-0.5).then_inc(s.o_rstd, 1)
                    act.wait_ge(s.o_fin, h + 1)
                    act.wait_ge(s.o_store, 16 * h + 16)
                    act.activation(opair[:, 0, :], os_[:, 0, 0:T], ACT.Copy).then_inc(s.o_high, 1)
                    act.wait_ge(s.o_low, h + 1)
                    act.wait_ge(s.o_high, h + 1)
                    act.dma_start(K.scratch_o[bass.ds(h, 1)].rearrange("o p a t -> (o p) a t"), opair[:, :, :]).then_inc(s.o_store, 16)
                    act.drain().then_inc(s.head_end, 1)

                act.wait_ge(s.consts, 48)
                act.sem_inc(s.o_store, 16)
                act.sem_inc(s.s_store, 32)
                high_part(0, 0)
                high_part(0, 1)
                for t in range(3):
                    copy_raw(0, t)
                    if t < 2:
                        high_part(0, t + 2)
                for j in range(2):
                    silu_of(0, j)
                with act.Fori(0, H - 1) as h:
                    head(h, True)
                head(H - 1, False)
                act.wait_ge(s.o_store, 16 * (H + 1))
                act.wait_ge(s.s_store, 32 * (H + 1))

            @block.vector
            def _(dve):
                PARTS = (1, 0, 2)

                def conv_weights(h):
                    dve.tensor_copy(hw[:, :, :].unsqueeze(3), K.conv_w[:, :].rearrange("p (w a h) -> p w a h", w=CONV_W, h=H)[:, :, :, bass.ds(h, 1)])

                def conv_tap(h, j, w):
                    part = PARTS[j]
                    if w == 0:
                        if j == 0:
                            dve.wait_ge(s.pads, h + 2)
                        dve.wait_ge(K.tile_read[j % 2], q0 + 2 * h + j // 2 + 2)
                        i = dve.tensor_scalar(cv[j][:, 0:N], raw[j][:, 0:N], hw[:, 0, part:part + 1], None, ALU.mult)
                    else:
                        i = dve.scalar_tensor_tensor(out=cv[j][:, 0:N], in0=raw[j][:, w:w + N], scalar=hw[:, w, part:part + 1],
                                                     in1=cv[j][:, 0:N], op0=ALU.mult, op1=ALU.add)
                    if w == CONV_W - 1:
                        i.then_inc(s.conv, 1)

                def head(h, following):
                    dve.wait_ge(s.head_end, 4 * h + 4)
                    one = bass.ds(h, 1)
                    for j, x in enumerate((K.beta, K.neg_beta, K.cum, K.gamma, K.to_end)):
                        dve.tensor_copy(hs[:, j:j + 1, :], x[:, one, :])
                    dve.tensor_copy(hc[:, :, :].unsqueeze(2), K.carry[:, :, one, :])
                    dve.drain().then_inc(s.scal, 1)
                    for j, (t0, tn) in enumerate(((0, 8), (8, 8), (16, 4))):
                        b = rd.to_read(dve, h, D_DT + j)[:, 0:tn * C].rearrange("p (t c) -> p t c", c=C)
                        dve.tensor_tensor(dt[:, t0:t0 + tn, :], b, hs[:, 2, t0:t0 + tn].unsqueeze(2).to_broadcast([P, tn, C]), ALU.subtract).then_inc(rd.free, 1)
                    dve.drain()
                    dve.tensor_tensor(dt[:, :, :], dt[:, :, :], seen[:, :].unsqueeze(1).to_broadcast([P, NPACK, C]), ALU.min).then_inc(s.dt_log, 1)
                    for j, x in enumerate((kp, qp)):
                        dve.wait_ge(s.inv_norm, 2 * h + j + 1)
                        for t0, tn, _, p0 in SEG:
                            i = dve.scalar_tensor_tensor(out=x[:, t0:t0 + tn, 0:C], in0=toks(silu[:, j, :], p0, tn), scalar=1.0 if j == 0 else DK ** -0.5,
                                                         in1=toks(os_[:, j, :], p0, tn), op0=ALU.mult, op1=ALU.mult)
                        i.then_inc(s.packed, 1)
                    dve.wait_ge(s.dtb, h + 1)
                    for g in range(NG):
                        for j, (out, f) in enumerate(((mt, dtb), (at, dt))):
                            b = quad(rd.to_read(dve, h, D_KK + 2 * g + j))
                            for d in range(2):
                                r = slice(64 * d, 64 * d + 64)
                                i = dve.tensor_tensor(out[r, grp(g), 64 * d:64 * d + 64], b[r, :, 64 * d:64 * d + 64], f[r, grp(g), :], ALU.mult)
                            i.then_inc(rd.free, 1)
                        dve.drain().then_inc(s.mt, 1)
                    ident4 = K.ident[:, :].unsqueeze(1).to_broadcast([P, 4, P])
                    for g in range(NG):
                        b = quad(rd.to_read(dve, h, D_INV0 + g))
                        dve.tensor_tensor(xi[:, grp(g), :], b, level[:, 0, :].unsqueeze(1).to_broadcast([P, 4, P]), ALU.mult).then_inc(rd.free, 1)
                        dve.drain()
                        dve.tensor_tensor(xi[:, grp(g), :], ident4, xi[:, grp(g), :], ALU.subtract)
                        dve.wait_ge(s.xt_level0, NG * h + g + 1)
                        dve.tensor_tensor(xti[:, grp(g), :], ident4, xti[:, grp(g), :], ALU.subtract).then_inc(s.inv, 1)
                    for l in range(1, LEVELS):
                        n = D_LEVEL[l]
                        for g in range(NG):
                            b = quad(rd.to_read(dve, h, n))
                            n += 1
                            dve.tensor_tensor(vi[:, grp(g), :], b, level[:, l, :].unsqueeze(1).to_broadcast([P, 4, P]), ALU.mult).then_inc(rd.free, 1)
                            dve.drain().then_inc(s.vmask, 1)
                        for g in range(NG):
                            for x in (xi, xti) if l < LEVELS - 1 else (xti,):
                                b = quad(rd.to_read(dve, h, n))
                                n += 1
                                dve.tensor_tensor(x[:, grp(g), :], x[:, grp(g), :], b, ALU.subtract).then_inc(rd.free, 1)
                            dve.drain().then_inc(s.inv, 1)
                    if following:
                        conv_weights(h + 1)
                    for g in range(NG):
                        b = rd.to_read(dve, h, D_WK + g)
                        dve.tensor_copy(wk[:, grp(g), :], quad(b)).then_inc(rd.free, 1)
                        dve.drain().then_inc(s.wk, 1)
                    for i, t in enumerate(STEPS):
                        q = int(t >= NC_S)
                        dve.wait_ge(s.uv, NG * h + t // 4 + 1)
                        b = rd.to_read(dve, h, D_SCAN + 3 * i)
                        for d in range(2):
                            r = slice(64 * d, 64 * d + 64)
                            dve.scalar_tensor_tensor(out=u[r, i % 2, d, :], in0=b[r, 0:P], scalar=hs[r, 1, t:t + 1], in1=uv[r, t, :],
                                                     op0=ALU.mult, op1=ALU.add).then_inc(s.u if d else s.dx, 1)
                        b = rd.to_read(dve, h, D_SCAN + 3 * i + 1)
                        for d in range(2):
                            dve.scalar_tensor_tensor(out=state[:, q, d, :], in0=state[:, q, d, :], scalar=hc[:, d, t:t + 1], in1=b[:, d * P:(d + 1) * P],
                                                     op0=ALU.mult, op1=ALU.add).then_inc(s.state_new if d else s.dx, 1)
                        b = rd.to_read(dve, h, D_SCAN + 3 * i + 2)
                        dve.wait_ge(rs.free, S_USES * h + s_q[i] + 1 + S_RING)
                        dve.tensor_tensor(op[:, t, :], tq[:, i % 2, :], b[:, 0:P], ALU.add).then_inc(s.o_add, 1)
                        dve.drain().then_inc(rd.free, 3)
                        for m, (j, w) in enumerate(TAPS.get(i, ()) if following else ()):
                            if m:
                                dve.drain()
                            conv_tap(h + 1, j, w)
                    if D_PAD:
                        dve.sem_inc(rd.free, D_PAD)
                    dve.wait_ge(rs.free, S_USES * h + S_RMS + S_RING)
                    dve.tensor_tensor(os_[:, 0, 0:T], os_[:, 0, 0:T], os_[:, 1, 0:T], ALU.add).then_inc(s.o_sum, 1)
                    dve.wait_ge(s.o_rstd, h + 1)
                    dve.tensor_tensor(os_[:, 0, 0:T], os_[:, 0, 0:T], os_[:, 1, 0:T], ALU.mult)
                    dve.drain()
                    dve.scalar_tensor_tensor(out=os_[:, 0, 0:T], in0=os_[:, 0, 0:T], scalar=K.dn_norm, in1=zs[:, :],
                                             op0=ALU.mult, op1=ALU.mult).then_inc(s.o_fin, 1)
                    dve.wait_ge(s.o_high, h + 1)
                    dve.wait_ge(s.o_fin, h + 1)
                    dve.tensor_tensor(opair[:, 1, :], os_[:, 0, 0:T], opair[:, 0, :], ALU.subtract).then_inc(s.o_low, 1)
                    dve.drain().then_inc(s.head_end, 1)

                dve.wait_ge(s.consts, 48)
                dve.wait_ge(s.pads, 1)
                conv_weights(0)
                for j in range(3):
                    for w in range(CONV_W):
                        dve.drain()
                        conv_tap(0, j, w)
                with dve.Fori(0, H - 1) as h:
                    head(h, True)
                head(H - 1, False)



def phase_branch_a(K, mg, opairs, ys):
    q0 = K.q
    K.q += KT
    with ExitStack() as st:
        sg = K.sb("a_sg", [P, T], stack=st)
        y = K.sb("glu_y", [P, L5, NC5], stack=st)
        u = K.sb("glu_u", [P, L5, NC5], stack=st)
        g = K.sb("glu_g", [P, T], stack=st)
        out = [K.ps(f"a_out{s}", [P, 1536], st) for s in range(2)]
        s_o = [K.sem(f"a_o_in_{h}") for h in range(H)]
        s_sg, s_mg = K.sem("a_gate"), K.sem("a_mg")
        s_in, s_v, s_g, s_hi, s_lo = (K.sem("glu_" + n) for n in ("in", "sum", "gelu", "high", "low"))
        with K.nc.Block() as block:
            @block.sync
            def _(sync):
                def load_y(j):
                    sync.wait_ge(s_g, j + 1)
                    sync.sem_inc(K.pulse, 1)
                    for dst, src in ((y, K.scratch_y), (u, K.scratch_u)):
                        sync.dma_start(dst[:, :, :], src[bass.ds(j, 1)].rearrange("o p t c -> (o p) t c")).then_inc(s_in, 16)

                for h in range(H):
                    sync.dma_start(opairs[:, :, h, :], K.scratch_o[h]).then_inc(s_o[h], 16)
                load_y(0)
                with sync.Fori(1, KT) as j:
                    load_pair(K, sync, q0 + j, "branch_a", j)
                    load_y(j)
                load_pair(K, sync, q0 + KT, "glu", 0)

            @block.gpsimd
            def _(pool):
                with pool.Fori(1, KT) as j:
                    low_pair(K, pool, q0 + j, "branch_a")
                low_pair(K, pool, q0 + KT, "glu")

            @block.tensor
            def _(pe):
                with pe.Fori(0, KT) as j:
                    multiply_tile(K, pe, q0 + j, 0, out[0], K.hn)
                    for h in range(H):
                        pe.wait_ge(s_o[h], 16)
                    multiply_tile(K, pe, q0 + j, 1, out[1], opairs)

            @block.scalar
            def _(act):
                act.sem_inc(s_g, 1)
                with act.Fori(0, KT) as j:
                    act.wait_ge(s_mg, j + 1)
                    wait_tile(K, act, q0 + j, 0)
                    act.activation(sg[:, :], out[0][:, 0:T], ACT.Sigmoid).then_inc(K.tile_read[0], 1)
                    split_high(K, act, q0 + j + 1, 0)
                    act.wait_ge(s_v, j + 1)
                    act.wait_ge(s_lo, j + 1)
                    act.activation(g[:, :].rearrange("p (c t) -> p t c", t=L5), y[:, :, :], ACT.Gelu_apprx_tanh).then_inc(s_g, 1)
                    act.wait_ge(s_g, j + 2)
                    act.activation(one(ys[:, 0, :, :], j), g[:, :], ACT.Copy).then_inc(s_hi, 1)
                    split_high(K, act, q0 + j + 1, 1)

            @block.vector
            def _(dve):
                dve.sem_inc(s_mg, 1)
                dve.sem_inc(s_lo, 1)
                with dve.Fori(0, KT) as j:
                    dve.wait_ge(s_in, 32 * j + 32)
                    dve.scalar_tensor_tensor(out=y[:, :, :], in0=u[:, :, :], scalar=K.s5_d[:, bass.ds(j, 1)], in1=y[:, :, :],
                                             op0=ALU.mult, op1=ALU.add).then_inc(s_v, 1)
                    dve.wait_ge(s_hi, j + 1)
                    dve.tensor_tensor(one(ys[:, 1, :, :], j), g[:, :], one(ys[:, 0, :, :], j), ALU.subtract).then_inc(s_lo, 1)
                    wait_tile(K, dve, q0 + j, 1)
                    dve.wait_ge(K.tile_read[0], q0 + j + 2)
                    dve.tensor_tensor(one(mg, j), out[1][:, 0:T], sg[:, :], ALU.mult).then_inc(s_mg, 1)
                    dve.wait_ge(s_mg, j + 2)
                    dve.sem_inc(K.tile_read[1], 1)


def phase_s5(K):
    nc = K.nc
    q0 = K.q
    K.q += KT // 2
    NG2 = 2 * G_S5
    TWO_PI = 6.283185307179586
    with ExitStack() as st:
        f = lambda name, shape, stack=st: K.sb(name, shape, stack=stack)
        pa = [f(n, [P, 2, G_S5, 9]) for n in ("pa_re", "pa_im")]
        pb = [f(n, [P, 2, G_S5, L5]) for n in ("pb_re", "pb_im")]
        e1 = [f(n, [P, 2, G_S5]) for n in ("e1_cos", "e1_sin")]
        r8 = f("r8", [P, 2, G_S5])
        h0 = f("h0", [P, 2, G_S5])
        bst = f("bst", [P, 2, G_S5, P_S5])
        b2st = f("b2st", [P, 2, G_S5, P_S5])
        c1 = f("c1", [P, 2, G_S5, P_S5])
        c2 = f("c2", [P, 2, G_S5, P_S5])
        fin = f("s5_fin", [P, 2, G_S5])
        with ExitStack() as s2:
            g = lambda name, shape: K.sb(name, shape, stack=s2)
            nat = g("s5_nat", [P, 6, 2, N_S5])
            ldt = g("s5_ldt", [P, 1])
            tr = g("s5_tr", [P, 5, 2, G_S5])
            w = g("s5_w", [P, 8, 2, G_S5])
            b1, b2 = g("s5_b1", [P, 2, G_S5, P_S5]), g("s5_b2", [P, 2, G_S5, P_S5])
            bn = [g(n, [P, 2, N_S5 * P_S5]) for n in ("bn1", "bn2")]
            cn = [g(n, [P, 16, 2, N_S5]) for n in ("cn1", "cn2")]
            ct = g("ct", [P, P])
            u = g("u_rows", [P, 2, L5, NC5])
            bank = K.ps("s5_bank", [P, 8, 512], s2)
            out = [bank[:, 3 * slot:3 * slot + 3, :].rearrange("p b c -> p (b c)") for slot in range(2)]
            s_st = [K.sem("u_stored_0"), K.sem("u_stored_1")]
            s_nat, s_b, s_c = K.sem("s5p_nat"), K.sem("s5p_b"), K.sem("s5p_c")
            s_bm, s_bt = K.sem("s5p_b_turned"), K.sem("s5p_b_read")
            s_dt, s_xy, s_t, s_red, s_trig, s_dve, s_ct, s_ce = (K.sem("s5p_" + n) for n in ("dt", "xy", "turned", "reduced", "trig", "dve", "c_turned", "c_read"))
            dgn = lambda a: a.rearrange("d g n -> (d g) n")
            W = lambda j: w[:, j, :, :]

            def parameters(sync):
                for u in range(2):
                    sync.dma_start(nat[:, 0, u, :], dgn(K.i["s5_a_re"][0])).then_inc(s_nat, 16)
                    sync.dma_start(nat[:, 1, u, :], dgn(K.i["s5_a_im"][0])).then_inc(s_nat, 16)
                sync.dma_start(nat[:, 4, 0, :], dgn(K.i["state_s5_re"][0, 0])).then_inc(s_nat, 16)
                sync.dma_start(nat[:, 4, 1, :], dgn(K.i["state_s5_im"][0, 0])).then_inc(s_nat, 16)
                with nc.allow_non_contiguous_dma(reason="128 values"):
                    sync.dma_start(ldt[:, :], K.i["s5_log_dt"][0].rearrange("d (g o) -> (d g) o", o=1)).then_inc(s_nat, 16)
                for x, names in zip(bn, (("s5_b_re", "s5_b_im"), ("s5_b_im", "s5_b_re"))):
                    for u, name in enumerate(names):
                        sync.dma_start(x[:, u, :], K.i[name][0].rearrange("d g n p -> (d g) (n p)")).then_inc(s_b, 16)
                for j, (x, y) in enumerate((("s5_c_re", "s5_c_im"), ("s5_c_im", "s5_c_re"))):
                    for u, name in enumerate((x, y)):
                        sync.dma_start(cn[j][:, :, u, :], K.i[name][0].rearrange("d (k g) p n -> (g p) (d k) n", g=8)).then_inc(s_c, 16)

            with nc.Block() as block:
                stream(K, block, [("u", KT // 2, q0)], "branch_a", before=parameters)


                @block.tensor
                def _(pe):
                    pe.wait_ge(s_xy, 1)
                    places = lambda j: bank[:, 6 + j // 4, (j % 4) * P:(j % 4 + 1) * P]
                    for j in range(5):
                        mm = pe.transpose(places(j), nat[:, j, :, :], K.ident[:, :])
                    mm.then_inc(s_t, 1)

                    def u_pair(j):
                        for slot in range(2):
                            multiply_tile(K, pe, q0 + j, slot, out[slot], K.hn)

                    u_pair(0)
                    pe.wait_ge(s_b, 64)
                    for j in range(2):
                        rows = bn[j][:, :, :].rearrange("q u (n p) -> q p (u n)", p=P_S5)
                        for c in range(P_S5):
                            n = 4 * j + c // 4
                            if c % 4 == 0:
                                pe.wait_ge(s_bt, max(n, 1))
                            mm = pe.transpose(bank[:, 6 + n % 2, (c % 4) * P:(c % 4 + 1) * P], rows[:, c, :], K.ident[:, :])
                            if c % 4 == 3:
                                mm.then_inc(s_bm, 1)
                    pe.wait_ge(s_c, 64)
                    pe.wait_ge(s_bt, 9)
                    for i in range(16):
                        for j in range(2):
                            n = 2 * i + j
                            if n >= 2:
                                pe.wait_ge(s_ce, n - 1)
                            pe.transpose(bank[:, 6 + j, 0:P], cn[j][:, i, :, :], K.ident[:, :]).then_inc(s_ct, 1)
                    with pe.Fori(1, KT // 2) as j:
                        u_pair(j)

                @block.scalar
                def _(act):
                    def u_pair(j):
                        for slot in range(2):
                            act.wait_ge(s_st[slot], 16 * j + 16)
                            wait_tile(K, act, q0 + j, slot)
                            act.activation(u[:, slot, :, :], out[slot][:, 0:T].rearrange("p (c t) -> p t c", t=L5), ACT.Copy).then_inc(K.tile_read[slot], 1)
                            split_high(K, act, q0 + j + 1, slot)
                            act.wait_ge(K.tile_read[slot], q0 + j + 2)
                            act.dma_start(K.scratch_u[bass.ds(2 * j + slot, 1)].rearrange("o p t c -> (o p) t c"), u[:, slot, :, :]).then_inc(s_st[slot], 16)

                    for slot in range(2):
                        act.sem_inc(s_st[slot], 16)
                    act.wait_ge(s_nat, 16 * 7)
                    act.activation(ldt[:, :], ldt[:, :], ACT.Exp).then_inc(s_dt, 1)
                    act.wait_ge(s_red, 1)
                    act.activation(W(0), tr[:, 2, :, :], ACT.Exp)
                    act.activation(r8[:, :, :], tr[:, 2, :, :], ACT.Exp, scale=float(L5))
                    act.activation(W(1), W(5), ACT.Sin)
                    act.activation(W(2), W(5), ACT.Sin, scale=0.5)
                    act.activation(e1[1][:, :, :], W(6), ACT.Sin)
                    act.activation(W(3), W(6), ACT.Sin, scale=0.5).then_inc(s_trig, 1)
                    u_pair(0)
                    for i in range(16):
                        d, k = i // 8, i % 8
                        gs = slice(8 * k, 8 * k + 8)
                        v = lambda lo, b: bank[lo:lo + 64, 6 + b, 0:P].rearrange("p (g c) -> p g c", c=P_S5)
                        act.wait_ge(s_ct, 2 * i + 1)
                        act.activation(c1[0:64, d, gs, :], v(0, 0), ACT.Copy)
                        act.activation(c1[64:P, d, gs, :], v(64, 0), ACT.Copy, scale=-1.0).then_inc(s_ce, 1)
                        act.wait_ge(s_ct, 2 * i + 2)
                        act.activation(c2[:, d, gs, :], bank[:, 7, 0:P].rearrange("p (g c) -> p g c", c=P_S5), ACT.Copy, scale=-1.0).then_inc(s_ce, 1)
                    with act.Fori(1, KT // 2) as j:
                        u_pair(j)
                    for slot in range(2):
                        act.wait_ge(s_st[slot], 16 * (KT // 2) + 16)

                @block.vector
                def _(dve):
                    def tt(o, a, b, op):
                        return dve.tensor_tensor(o, a, b, op)

                    def reduce_angle(dst, y, k):
                        big = 12582912.0
                        dve.tensor_scalar(k, y, 1.0 / TWO_PI, None, ALU.mult)
                        dve.drain()
                        dve.tensor_scalar(k, k, big, None, ALU.add)
                        dve.drain()
                        dve.tensor_scalar(k, k, big, None, ALU.subtract)
                        dve.drain()
                        dve.scalar_tensor_tensor(out=dst, in0=k, scalar=-6.28125, in1=y, op0=ALU.mult, op1=ALU.add)
                        dve.drain()
                        dve.scalar_tensor_tensor(out=dst, in0=k, scalar=-(TWO_PI - 6.28125), in1=dst, op0=ALU.mult, op1=ALU.add)
                        dve.drain()
                        dve.tensor_scalar(dst, dst, 3.1415925, -3.1415925, ALU.min, ALU.max)
                        dve.drain()

                    dve.wait_ge(s_dt, 1)
                    dve.tensor_scalar(nat[:, 2, :, :], nat[:, 0, :, :], ldt[:, :], None, ALU.mult)
                    dve.tensor_scalar(nat[:, 3, :, :], nat[:, 1, :, :], ldt[:, :], None, ALU.mult).then_inc(s_xy, 1)
                    dve.wait_ge(s_t, 1)
                    for j in range(5):
                        dst = tr[:, j, :, :] if j < 4 else h0[:, :, :]
                        dve.tensor_copy(dst, bank[:, 6 + j // 4, (j % 4) * P:(j % 4 + 1) * P].rearrange("p (d g) -> p d g", d=2))
                    dve.drain().then_inc(s_bt, 1)
                    reduce_angle(W(5), tr[:, 3, :, :], W(7))
                    dve.tensor_scalar(W(4), W(5), float(L5), None, ALU.mult)
                    dve.drain()
                    reduce_angle(W(6), W(4), W(7))
                    dve.drain().then_inc(s_red, 1)
                    dve.wait_ge(s_trig, 1)
                    for src, dst in ((W(2), W(4)), (W(3), e1[0][:, :, :])):
                        tt(dst, src, src, ALU.mult)
                        dve.drain()
                        dve.tensor_scalar(dst, dst, -2.0, 1.0, ALU.mult, ALU.add)
                        dve.drain()
                    sl = lambda t, d, k: t[:, d, :, k if d == 0 else 8 - k]
                    for d in range(2):
                        dve.memset(sl(pa[0], d, 0), 1.0)
                        dve.memset(sl(pa[1], d, 0), 0.0)
                        tt(sl(pa[0], d, 1), w[:, 0, d, :], w[:, 4, d, :], ALU.mult)
                        tt(sl(pa[1], d, 1), w[:, 0, d, :], w[:, 1, d, :], ALU.mult)
                    dve.drain()
                    for k in range(2, 9):
                        for d in range(2):
                            ar, ai, pr, pi = sl(pa[0], d, 1), sl(pa[1], d, 1), sl(pa[0], d, k - 1), sl(pa[1], d, k - 1)
                            for j, (x, y) in enumerate(((pr, ar), (pi, ai), (pr, ai), (pi, ar))):
                                tt(w[:, j if j < 3 else 5, d, :], x, y, ALU.mult)
                        dve.drain()
                        for d in range(2):
                            tt(sl(pa[0], d, k), w[:, 0, d, :], w[:, 1, d, :], ALU.subtract)
                            tt(sl(pa[1], d, k), w[:, 2, d, :], w[:, 5, d, :], ALU.add)
                        dve.drain()
                    for t in range(2):
                        dve.tensor_copy(pb[t][:, 0, :, :], pa[t][:, 0, :, 7::-1])
                        dve.tensor_copy(pb[t][:, 1, :, :], pa[t][:, 1, :, 8:0:-1])
                    lr, li = tr[:, 0, :, :], tr[:, 1, :, :]
                    for d in range(2):
                        dve.tensor_scalar(w[:, 0, d, :], sl(pa[0], d, 1), -1.0, None, ALU.add)
                        dve.tensor_copy(w[:, 1, d, :], sl(pa[1], d, 1))
                    tt(W(2), lr, lr, ALU.mult)
                    tt(W(3), li, li, ALU.mult)
                    dve.drain()
                    tt(W(2), W(2), W(3), ALU.add)
                    dve.drain()
                    dve.reciprocal(W(2), W(2))
                    tt(W(4), W(0), lr, ALU.mult)
                    tt(W(5), W(1), li, ALU.mult)
                    tt(W(6), W(1), lr, ALU.mult)
                    tt(W(7), W(0), li, ALU.mult)
                    dve.drain()
                    tt(W(4), W(4), W(5), ALU.add)
                    tt(W(6), W(6), W(7), ALU.subtract)
                    dve.drain()
                    tt(W(4), W(4), W(2), ALU.mult)
                    tt(W(6), W(6), W(2), ALU.mult)
                    dve.drain()
                    for j, x in enumerate((b1, b2)):
                        for c in range(4):
                            dve.wait_ge(s_bm, 4 * j + c + 1)
                            dve.tensor_copy(x[:, :, :, 4 * c:4 * c + 4].rearrange("p d g c -> p c (d g)"),
                                            bank[:, 6 + (4 * j + c) % 2, :].rearrange("p (c q) -> p c q", c=4)).then_inc(s_bt, 1)
                    dve.drain()
                    dve.tensor_scalar(b2[0:64, :, :, :], b2[0:64, :, :, :], -1.0, None, ALU.mult)
                    dve.drain()
                    cr = W(4).unsqueeze(3).to_broadcast([P, 2, G_S5, P_S5])
                    ci = W(6).unsqueeze(3).to_broadcast([P, 2, G_S5, P_S5])
                    tt(bst[:, :, :, :], b1[:, :, :, :], cr, ALU.mult)
                    tt(b2st[:, :, :, :], b2[:, :, :, :], cr, ALU.mult)
                    tt(b2[:, :, :, :], b2[:, :, :, :], ci, ALU.mult)
                    tt(b1[:, :, :, :], b1[:, :, :, :], ci, ALU.mult)
                    dve.drain()
                    tt(bst[:, :, :, :], bst[:, :, :, :], b2[:, :, :, :], ALU.add)
                    tt(b2st[:, :, :, :], b2st[:, :, :, :], b1[:, :, :, :], ALU.subtract)

        NB = G_S5 // GB
        NE = NC5_S + 1
        tcs, tss = f("rot_cos", [P, 2, 2, GB, NE]), f("rot_sin", [P, 2, 2, GB, NE])
        rt = f("rot_tmp", [P, 4, 2, GB, NC5_S // 2])
        cc, cq = f("cc", [P, 2, 2, GB, 9, P_S5]), f("cq", [P, 2, 2, GB, 9, P_S5])
        ctmp = f("c_tmp", [P, 2, 2, GB, 9, P_S5])
        wt = f("wt", [P, 2, GB, L5, P_S5])
        w1, w2 = f("w1", [P, 2, GB, P]), f("w2", [P, 2, GB, P])
        bb = f("b_block", [P, 2, 2, GB, P_S5])
        ks = f("k_rows", [P_S5, GB, 15 * P_S5])
        m = f("m_block", [P, GB, P])
        u = f("u_block", [P, 2, GB, NC5])
        y = f("y_block", [P, GB, NC5])
        gt = f("g_tmp", [P, 2, GB, NC5])
        gs = f("g_scan", [P, 2, GB, NE])
        gp = f("g_scan_p", [P, 2, GB, NC5_P + 1])
        pq = f("pq", [P, 2, 2, GB, NC5])
        bank = K.ps("s5_banks", [P, 8, 512], st)
        ends = rt[0:1, :, :, :, :].rearrange("p a d g c -> p (a d g c)")[:, 0:2 * D].rearrange("p (d c) -> p d c", d=2)
        halves = lambda b: bank[:, b:b + 2, :].rearrange("p b (g c) -> p (b g) c", c=256)
        xb, x2b, yb = halves(0), halves(2), halves(4)
        s = Names()
        s.u_in = [K.sem("s5_u_in_0"), K.sem("s5_u_in_1")]
        s.tables = K.sem("s5_tables")
        s.cc = K.sem("s5_cc")
        s.wt = K.sem("s5_wt")
        s.wtr = K.sem("s5_wtr")
        s.w = K.sem("s5_w")
        s.k = K.sem("s5_k")
        s.ks = K.sem("s5_ks")
        s.m_in = K.sem("s5_m_in")
        s.x = K.sem("s5_x")
        s.xread = K.sem("s5_xread")
        s.pq = K.sem("s5_pq")
        s.y = K.sem("s5_y")
        s.yread = K.sem("s5_yread")
        s.y_out = K.sem("s5_y_out")
        s.fin_t = K.sem("s5_fin_t")
        s.fin_in = K.sem("s5_fin_in")
        s.fin_u = K.sem("s5_fin_u")
        s.fin_c = K.sem("s5_fin_c")
        s.fin_d = K.sem("s5_fin_d")
        s.fin_out = K.sem("s5_fin_out")
        su = K.scratch_u.rearrange("k q t c -> (k q) t c").rearrange("(g p) t c -> t p g c", p=P_S5)
        sy = K.scratch_y.rearrange("k q t c -> (k q) t c").rearrange("(g p) t c -> t p g c", p=P_S5)
        with nc.Block() as block:
            @block.sync
            def _(sync):
                def load(b, slot):
                    sync.wait_ge(s.y, b + 1)
                    sync.sem_inc(K.pulse, 1)
                    for t in range(L5):
                        sync.dma_start(u[t * P_S5:(t + 1) * P_S5, slot, :, :], su[t][:, bass.ds(b * GB, GB), :]).then_inc(s.u_in[slot], 16)

                def toeplitz(b):
                    sync.wait_ge(s.ks, b + 1)
                    for t in range(L5):
                        sync.dma_start(m[t * P_S5:(t + 1) * P_S5, :, :], ks[:, :, (7 - t) * P_S5:(7 - t) * P_S5 + P]).then_inc(s.m_in, 16)

                def store(b):
                    sync.wait_ge(s.yread, b + 2)
                    sync.sem_inc(K.pulse, 1)
                    for t in range(L5):
                        sync.dma_start(sy[t][:, bass.ds(b * GB, GB), :], y[t * P_S5:(t + 1) * P_S5, :, :]).then_inc(s.y_out, 16)

                sync.sem_inc(s.y_out, 16 * L5)
                load(0, 0)
                toeplitz(0)
                with sync.Fori(0, NB // 2 - 1) as i:
                    for k in (1, 2):
                        load(2 * i + k, k % 2)
                        store(2 * i + (k - 1))
                        toeplitz(2 * i + k)
                load(NB - 1, 1)
                store(NB - 2)
                toeplitz(NB - 1)
                store(NB - 1)
                sync.wait_ge(s.y_out, 16 * L5 * (NB + 1))
                sync.wait_ge(s.tables, NB)
                with nc.allow_non_contiguous_dma(reason="one token's channels"):
                    for d, (t, c) in enumerate(((0, NC5_S), (L5 - 1, NC5 - 1))):
                        sync.dma_start(ends[0:1, d, :], K.scratch_u.rearrange("k q t c -> t c (k q)")[t, c].unsqueeze(0)).then_inc(s.fin_in, 16)
                sync.wait_ge(s.fin_d, 1)
                for j, name in enumerate(("new_state_s5_re", "new_state_s5_im")):
                    sync.dma_start(K.o[name][0, 0].rearrange("d g n -> (d g) n"), w1[:, 0, 0, j * N_S5:(j + 1) * N_S5]).then_inc(s.fin_out, 16)
                sync.wait_ge(s.fin_out, 32)

            @block.gpsimd
            def _(pool):
                def block_tables(b, slot):
                    tc, ts = tcs[:, slot, :, :, :], tss[:, slot, :, :, :]
                    pool.wait_ge(s.pq, b + 1)
                    pool.sem_inc(K.pulse, 1)
                    blk = bass.ds(b * GB, GB)
                    pool.memset(tc[:, :, :, 0:1], 1.0)
                    pool.memset(ts[:, :, :, 0:1], 0.0)
                    pool.tensor_copy(tc[:, :, :, 1:2], e1[0][:, :, blk].unsqueeze(3))
                    pool.tensor_copy(ts[:, :, :, 1:2], e1[1][:, :, blk].unsqueeze(3))
                    pool.tensor_copy(bb[:, slot, :, :, :], bst[:, :, blk, :])
                    pool.drain()
                    n = 1
                    while n < NC5_S:
                        for j, (x, z) in enumerate(((tc, tc), (ts, ts), (ts, tc), (tc, ts))):
                            pool.tensor_tensor(rt[:, j, :, :, 0:n], x[:, :, :, 1:n + 1], z[:, :, :, n:n + 1].to_broadcast([P, 2, GB, n]), ALU.mult)
                        pool.drain()
                        pool.tensor_tensor(tc[:, :, :, n + 1:2 * n + 1], rt[:, 0, :, :, 0:n], rt[:, 1, :, :, 0:n], ALU.subtract)
                        pool.tensor_tensor(ts[:, :, :, n + 1:2 * n + 1], rt[:, 2, :, :, 0:n], rt[:, 3, :, :, 0:n], ALU.add)
                        pool.drain()
                        n *= 2
                    pool.drain().then_inc(s.tables, 1)

                with pool.Fori(0, NB // 2) as i:
                    for slot in range(2):
                        block_tables(2 * i + slot, slot)

            @block.tensor
            def _(pe):
                def block_products(i, slot):
                    b = 2 * i + slot
                    pe.wait_ge(s.wt, b + 1)
                    for d in range(2):
                        for g in range(GB):
                            mm = pe.transpose(bank[:, 6 + d, g * P:(g + 1) * P], wt[:, d, g, :, :], K.ident[:, :])
                    mm.then_inc(s.wtr, 1)
                    pe.wait_ge(s.w, b + 1)
                    pe.wait_ge(s.u_in[slot], 16 * L5 * (i + 1))
                    for d in range(2):
                        if d:
                            pe.wait_ge(s.xread, 2 * b + 1)
                        for out, lhs in ((xb, w1), (x2b, w2)):
                            for g in range(GB):
                                mm = pe.matmul(out[:, g, 0:NC5], lhs[:, d, g, :], u[:, slot, g, :], start=True, stop=True)
                        mm.then_inc(s.x, 1)
                        if d == 0:
                            pe.wait_ge(s.cc, b + 1)
                            pe.wait_ge(s.tables, b + 1)
                            pe.wait_ge(s.yread, b + 1)
                            for g in range(GB):
                                back = cc[:, slot, 1, g, 1:9, :]
                                fwd = cc[:, slot, 0, g, 0:8, :]
                                o = yb[0:P_S5, g, :]
                                pe.matmul(o[:, 0:P], bb[:, slot, 1, g, :], back, start=True, stop=False, skip_group_check=True)
                                pe.matmul(o[:, 7 * P_S5:P], bb[:, slot, 0, g, :], fwd[:, 0:1, :], start=False, stop=True, skip_group_check=True)
                                mm = pe.matmul(o[:, P:15 * P_S5], bb[:, slot, 0, g, :], fwd[:, 1:8, :], start=True, stop=True, skip_group_check=True)
                            mm.then_inc(s.k, 1)
                    pe.wait_ge(s.m_in, 16 * L5 * (b + 1))
                    pe.wait_ge(s.pq, b + 3)
                    for g in range(GB):
                        o = yb[:, g, 0:NC5]
                        pe.matmul(o, m[:, g, :], u[:, slot, g, :], start=True, stop=False, skip_group_check=True)
                        for d in range(2):
                            k0 = 1 - d
                            pe.matmul(o, cc[:, slot, d, g, k0:k0 + 8, :].rearrange("p k c -> p (k c)"), pq[:, d, 0, g, :], start=False, stop=False, skip_group_check=True)
                            mm = pe.matmul(o, cq[:, slot, d, g, k0:k0 + 8, :].rearrange("p k c -> p (k c)"), pq[:, d, 1, g, :], start=False, stop=d == 1, skip_group_check=True)
                    mm.then_inc(s.y, 1)

                pe.sem_inc(s.y, 2)
                pe.sem_inc(s.wtr, 1)
                with pe.Fori(0, NB // 2) as i:
                    for slot in range(2):
                        block_products(i, slot)
                pe.wait_ge(s.pq, NB + 2)
                pe.wait_ge(s.fin_in, 32)
                for d in range(2):
                    for j in range(2):
                        mm = pe.matmul(bank[:, 2 * d + j, :], K.ones[0:1, :], ends[0:1, d, j * 512:(j + 1) * 512], start=True, stop=True)
                    mm.then_inc(s.fin_u, 1)
                pe.wait_ge(s.fin_t, 2)
                mm = pe.transpose(bank[:, 4, 0:P], fin[:, :, :], K.ident[:, :])
                mm.then_inc(s.fin_c, 1)

            @block.scalar
            def _(act):
                def block_copies(b):
                    act.wait_ge(s.wtr, b + 2)
                    for d in range(2):
                        v = bank[:, 6 + d, :].rearrange("p (g c) -> p g c", c=P)
                        act.activation(w1[:, d, :, :], v, ACT.Copy)
                        act.activation(w2[:, d, :, 0:64], v[:, :, 64:P], ACT.Copy)
                        c = act.activation(w2[:, d, :, 64:P], v[:, :, 0:64], ACT.Copy, scale=-1.0)
                    c.then_inc(s.w, 1)
                    act.wait_ge(s.k, b + 1)
                    act.activation(ks[:, :, :], yb[0:P_S5, :, 0:15 * P_S5], ACT.Copy).then_inc(s.ks, 1)
                    act.wait_ge(s.y, b + 3)
                    act.wait_ge(s.y_out, 16 * L5 * (b + 1))
                    act.activation(y[:, :, :], yb[:, :, 0:NC5], ACT.Copy).then_inc(s.yread, 1)

                act.sem_inc(s.yread, 1)
                with act.Fori(0, NB) as b:
                    block_copies(b)

            @block.vector
            def _(dve):
                for d in range(2):
                    dve.memset(gp[:, d, :, 0:1] if d == 0 else gp[:, d, :, NC5_P:], 0.0)

                def block_scans(b, slot):
                    blk = bass.ds(b * GB, GB)
                    tc, ts = tcs[:, slot, :, :, :], tss[:, slot, :, :, :]
                    dve.wait_ge(s.wtr, b + 1)
                    for d in range(2):
                        sh = [P, GB, L5, P_S5]
                        br = lambda x: x[:, d:d + 1, blk, :].rearrange("p o g c -> p (o g) c").unsqueeze(2).to_broadcast(sh)
                        pw = lambda x: x[:, d:d + 1, blk, :].rearrange("p o g c -> p (o g) c").unsqueeze(3).to_broadcast(sh)
                        t = ctmp[:, 0, d, :, 0:8, :]
                        dve.tensor_tensor(wt[:, d, :, :, :], br(bst), pw(pb[0]), ALU.mult)
                        dve.tensor_tensor(t, br(b2st), pw(pb[1]), ALU.mult)
                        dve.drain()
                        i = dve.tensor_tensor(wt[:, d, :, :, :], wt[:, d, :, :, :], t, ALU.add)
                    i.then_inc(s.wt, 1)
                    dve.drain()
                    dve.wait_ge(s.y, b + 1)
                    for d in range(2):
                        sh = [P, GB, 9, P_S5]
                        br = lambda x: x[:, d:d + 1, blk, :].rearrange("p o g c -> p (o g) c").unsqueeze(2).to_broadcast(sh)
                        pw = lambda x: x[:, d:d + 1, blk, :].rearrange("p o g c -> p (o g) c").unsqueeze(3).to_broadcast(sh)
                        dve.tensor_tensor(cc[:, slot, d, :, :, :], br(c1), pw(pa[0]), ALU.mult)
                        dve.tensor_tensor(ctmp[:, 0, d, :, :, :], br(c2), pw(pa[1]), ALU.mult)
                        dve.tensor_tensor(cq[:, slot, d, :, :, :], br(c2), pw(pa[0]), ALU.mult)
                        dve.tensor_tensor(ctmp[:, 1, d, :, :, :], br(c1), pw(pa[1]), ALU.mult)
                        dve.drain()
                        dve.tensor_tensor(cc[:, slot, d, :, :, :], cc[:, slot, d, :, :, :], ctmp[:, 0, d, :, :, :], ALU.add)
                        i = dve.tensor_tensor(cq[:, slot, d, :, :, :], cq[:, slot, d, :, :, :], ctmp[:, 1, d, :, :, :], ALU.subtract)
                    i.then_inc(s.cc, 1)
                    dve.wait_ge(s.tables, b + 1)
                    spans = ((0, NC5_S), (NC5_S, NC5_P))
                    for d in range(2):
                        tab = lambda x, n, o: x[:, d, :, o:n + o] if d == 0 else x[:, d, :, o:n + o][:, :, ::-1]
                        dve.wait_ge(s.x, 2 * b + d + 1)
                        for c0, n in spans:
                            dve.tensor_tensor(gt[:, 0, :, c0:c0 + n], xb[:, :, c0:c0 + n], tab(tc, n, 1), ALU.mult)
                            i = dve.tensor_tensor(gt[:, 1, :, c0:c0 + n], x2b[:, :, c0:c0 + n], tab(ts, n, 1), ALU.mult)
                        i.then_inc(s.xread, 1)
                        start = 0 if d == 0 else NE - 1
                        dve.tensor_copy(gs[:, d:d + 1, :, start:start + 1], h0[:, d:d + 1, blk].unsqueeze(3))
                        dve.drain()
                        dve.tensor_tensor(gt[:, 0, :, :], gt[:, 0, :, :], gt[:, 1, :, :], ALU.add)
                        dve.tensor_copy(ctmp[:, 0, d, 0, 0, 0:GB], r8[:, d:d + 1, blk].rearrange("p o g -> p (o g)"))
                        dve.drain()
                        for g in range(GB):
                            decay = ctmp[:, 0, d, 0, 0, g:g + 1]
                            for (c0, n), x in zip(spans, (gs, gp)):
                                o = x[:, d, g, 1:n + 1] if d == 0 else x[:, d, g, n - 1::-1]
                                i0 = x[:, d, g, 0:1] if d == 0 else x[:, d, g, n:n + 1]
                                v = gt[:, 0, g, c0:c0 + n]
                                dve.tensor_tensor_scan(o, decay.to_broadcast([P, n]), v if d == 0 else v[:, ::-1], i0, ALU.mult, ALU.add)
                        dve.drain()
                        dve.wait_ge(s.y, b + 2)
                        for (c0, n), x in zip(spans, (gs, gp)):
                            before = x[:, d, :, 0:n] if d == 0 else x[:, d, :, 1:n + 1]
                            for j, t in enumerate((tc, ts)):
                                i = dve.tensor_tensor(pq[:, d, j, :, c0:c0 + n], before, tab(t, n, 0), ALU.mult)
                        dve.drain()
                    dve.drain().then_inc(s.pq, 1)

                dve.sem_inc(s.pq, 2)
                with dve.Fori(0, NB // 2) as i:
                    for slot in range(2):
                        block_scans(2 * i + slot, slot)
                for d in range(2):
                    dve.wait_ge(s.fin_u, d + 1)
                    v = gt[:, :, :, :].rearrange("p a g c -> p (a g c)")[:, 0:G_S5 * P_S5]
                    o = bank[:, 2 * d:2 * d + 2, :].rearrange("p b c -> p (b c)")
                    dve.tensor_tensor(v, bst[:, d, :, :].rearrange("p g c -> p (g c)"), o, ALU.mult)
                    dve.drain()
                    dve.tensor_reduce(fin[:, d, :], v.rearrange("p (g c) -> p g c", c=P_S5), mybir.AxisListType.X, ALU.add)
                    dve.drain().then_inc(s.fin_t, 1)
                dve.wait_ge(s.fin_c, 1)
                dve.tensor_copy(w1[:, 0, 0, :], bank[:, 4, 0:P]).then_inc(s.fin_d, 1)



def one(x, j):
    return x[:, bass.ds(j, 1), :].rearrange("p o t -> p (o t)")


def phase_branch_b(K, mg, ys, ys2):
    q0 = K.q
    K.q += KT // 2 + KT
    q1 = q0 + KT // 2
    with ExitStack() as st:
        out = [K.ps(f"b_out{s}", [P, 1536], st) for s in range(2)]
        sg = K.sb("b_sg", [P, 2, T], stack=st)
        y = K.sb("b_y", [P, 2, T], stack=st)
        s_sg, s_y, s_hi, s_lo, s_t, s_mg = (K.sem("b_" + n) for n in ("sig", "y", "high", "low", "prod", "mg"))
        with K.nc.Block() as block:
            stream(K, block, [("glu", KT // 2, q0), ("branch_b", KT, q1)], "out")

            @block.tensor
            def _(pe):
                with pe.Fori(0, KT // 2) as j:
                    for slot in range(2):
                        multiply_tile(K, pe, q0 + j, slot, out[slot], ys)
                pe.wait_ge(s_lo, KT + 1)
                with pe.Fori(0, KT) as j:
                    multiply_tile(K, pe, q1 + j, 0, out[0], K.hn)
                    multiply_tile(K, pe, q1 + j, 1, out[1], ys2)

            @block.scalar
            def _(act):
                act.sem_inc(s_hi, 1)
                with act.Fori(0, KT // 2) as j:
                    for slot in range(2):
                        act.wait_ge(s_y, 2 * j + 1)
                        wait_tile(K, act, q0 + j, slot)
                        act.activation(sg[:, slot, :], out[slot][:, 0:T], ACT.Sigmoid,
                                       bias=K.b_glu[:, bass.ds(2 * j + slot, 1)]).then_inc(K.tile_read[slot], 1)
                        split_high(K, act, q0 + j + 1, slot)
                    for slot in range(2):
                        act.wait_ge(s_y, 2 * j + slot + 2)
                        act.activation(one(ys2[:, 0, :, :], 2 * j + slot), y[:, slot, :], ACT.Copy).then_inc(s_hi, 1)
                with act.Fori(0, KT) as j:
                    act.wait_ge(s_t, j + 1)
                    act.wait_ge(s_y, KT + 1)
                    wait_tile(K, act, q1 + j, 0)
                    act.activation(sg[:, 0, :], out[0][:, 0:T], ACT.Sigmoid).then_inc(K.tile_read[0], 1)
                    split_high(K, act, q1 + j + 1, 0)
                    act.wait_ge(s_mg, j + 1)
                    act.activation(one(ys[:, 0, :, :], j), one(mg, j), ACT.Copy).then_inc(s_hi, 1)
                    split_high(K, act, q1 + j + 1, 1)

            @block.vector
            def _(dve):
                for s in (s_y, s_lo, s_t):
                    dve.sem_inc(s, 1)
                with dve.Fori(0, KT // 2) as j:
                    for slot in range(2):
                        k = 2 * j + slot
                        if slot == 0:
                            dve.wait_ge(s_lo, 2 * j + 1)
                        dve.wait_ge(s_hi, 2 * j + 1)
                        dve.tensor_tensor(y[:, slot, :], one(ys[:, 0, :, :], k), one(ys[:, 1, :, :], k), ALU.add)
                        dve.drain()
                        dve.wait_ge(K.tile_read[slot], q0 + j + 2)
                        dve.tensor_tensor(y[:, slot, :], y[:, slot, :], sg[:, slot, :], ALU.mult).then_inc(s_y, 1)
                    for slot in range(2):
                        k = 2 * j + slot
                        dve.wait_ge(s_y, k + 2)
                        dve.wait_ge(s_hi, k + 2)
                        dve.tensor_tensor(one(ys2[:, 1, :, :], k), y[:, slot, :], one(ys2[:, 0, :, :], k), ALU.subtract).then_inc(s_lo, 1)
                with dve.Fori(0, KT) as j:
                    wait_tile(K, dve, q1 + j, 1)
                    dve.wait_ge(K.tile_read[0], q1 + j + 2)
                    dve.tensor_tensor(y[:, 0, :], out[1][:, 0:T], sg[:, 0, :], ALU.mult).then_inc(s_t, 1)
                    dve.wait_ge(s_t, j + 2)
                    dve.sem_inc(K.tile_read[1], 1)
                    dve.tensor_tensor(one(mg, j), one(mg, j), y[:, 0, :], ALU.add).then_inc(s_mg, 1)
                    dve.wait_ge(s_hi, j + KT + 2)
                    dve.tensor_tensor(one(ys[:, 1, :, :], j), one(mg, j), one(ys[:, 0, :, :], j), ALU.subtract)


def add_product(K, dve, q, j, slot, out, x, gate, done):
    wait_tile(K, dve, q, slot)
    for a, n, c in SEGS:
        v = x[:, bass.ds(j, 1), a:a + n].rearrange("p o t -> p (o t)")
        i = dve.scalar_tensor_tensor(out=v, in0=out[:, a:a + n], scalar=K.mod[:, bass.ds(j + gate * KT, 1), c:c + 1].rearrange("p o c -> p (o c)"),
                                     in1=v, op0=ALU.mult, op1=ALU.add)
    i.then_inc(K.tile_read[slot], 1)


def phase_out(K, x, merged):
    q0 = K.q
    K.q += KT // 2
    with ExitStack() as st:
        out = [K.ps(f"o_out{s}", [P, 1536], st) for s in range(2)]
        s_x = K.sem("o_x_in")
        with K.nc.Block() as block:
            stream(K, block, [("out", KT // 2, q0)], "gate_up_0",
                   before=lambda sync: sync.dma_start(x[:, :, :], K.scratch_x).then_inc(s_x, 16))

            @block.tensor
            def _(pe):
                with pe.Fori(0, KT // 2) as j:
                    for slot in range(2):
                        multiply_tile(K, pe, q0 + j, slot, out[slot], merged)

            @block.scalar
            def _(act):
                with act.Fori(0, KT // 2) as j:
                    for slot in range(2):
                        split_high(K, act, q0 + j + 1, slot)

            @block.vector
            def _(dve):
                dve.wait_ge(s_x, 16)
                with dve.Fori(0, KT // 2) as j:
                    for slot in range(2):
                        add_product(K, dve, q0 + j, 2 * j + slot, slot, out[slot], x, 2, None)



def phase_mlp(K, x, acts):
    parts = MLP_PARTS
    loops, q = [], K.q
    for f0, n in parts:
        loops += [(n, q), (KT // 2, q + n)]
        q += n + KT // 2
    K.q = q
    with ExitStack() as st:
        out = [K.ps(f"m_out{s}", [P, 1536], st) for s in range(2)]
        sg = K.sb("m_sg", [P, T], stack=st)
        a = K.sb("m_a", [P, T], stack=st)
        s_a, s_hi, s_lo, s_x = (K.sem("m_" + n) for n in ("act", "high", "low", "x"))
        with K.nc.Block() as block:
            stream(K, block, [(("gate_up_%d", "down_%d")[i % 2] % (i // 2), n, q) for i, (n, q) in enumerate(loops)], None)

            @block.tensor
            def _(pe):
                for i, (f0, n) in enumerate(parts):
                    with pe.Fori(0, n) as j:
                        for slot in range(2):
                            multiply_tile(K, pe, loops[2 * i][1] + j, slot, out[slot], K.hn)
                    pe.wait_ge(s_lo, f0 + n)
                    with pe.Fori(0, KT // 2) as j:
                        for slot in range(2):
                            multiply_tile(K, pe, loops[2 * i + 1][1] + j, slot, out[slot], acts[i % 2], n)

            @block.scalar
            def _(act):
                for i, (f0, n) in enumerate(parts):
                    with act.Fori(0, n) as j:
                        q = loops[2 * i][1] + j
                        act.wait_ge(s_a, f0 + j + 1)
                        wait_tile(K, act, q, 0)
                        act.activation(sg[:, :], out[0][:, 0:T], ACT.Silu).then_inc(K.tile_read[0], 1)
                        split_high(K, act, q + 1, 0)
                        act.wait_ge(s_a, f0 + j + 2)
                        act.activation(one(acts[i % 2][:, 0, :, :], j), a[:, :], ACT.Copy).then_inc(s_hi, 1)
                        split_high(K, act, q + 1, 1)
                    with act.Fori(0, KT // 2 - int(i == len(parts) - 1)) as j:
                        for slot in range(2):
                            split_high(K, act, loops[2 * i + 1][1] + j + 1, slot)

            @block.vector
            def _(dve):
                dve.sem_inc(s_a, 1)
                for i, (f0, n) in enumerate(parts):
                    with dve.Fori(0, n) as j:
                        q = loops[2 * i][1] + j
                        wait_tile(K, dve, q, 1)
                        dve.wait_ge(K.tile_read[0], q + 2)
                        dve.tensor_tensor(a[:, :], out[1][:, 0:T], sg[:, :], ALU.mult).then_inc(s_a, 1)
                        dve.wait_ge(s_a, f0 + j + 2)
                        dve.sem_inc(K.tile_read[1], 1)
                        dve.wait_ge(s_hi, f0 + j + 1)
                        dve.tensor_tensor(one(acts[i % 2][:, 1, :, :], j), a[:, :], one(acts[i % 2][:, 0, :, :], j), ALU.subtract).then_inc(s_lo, 1)
                        dve.wait_ge(s_lo, f0 + j + 1)
                    dve.drain()
                    with dve.Fori(0, KT // 2) as j:
                        for slot in range(2):
                            add_product(K, dve, loops[2 * i + 1][1] + j, 2 * j + slot, slot, out[slot], x, 5, None)



def phase_final(K, x):
    with ExitStack() as st:
        act_part, pe_part, rstd, s_r = rstd_stages(K, st, x, "nf")
        NT = T // P
        rows = K.sb("out_rows", [P, 2, 2, 512], stack=st)
        tr = K.ps("out_tr", [P, 4, 512], st)
        s_n, s_t = K.sem("nf_scaled"), K.sem("nf_turned")
        s_c = [K.sem("nf_copied_0"), K.sem("nf_copied_1")]
        s_out = [[K.sem(f"nf_out_{half}_{slot}") for slot in range(2)] for half in range(2)]
        with K.nc.Block() as block:
            def copy_out(eng, copy, half):
                for t in range(NT):
                    if t >= 2:
                        eng.wait_ge(s_out[half][t % 2], 16 * (t // 2))
                    eng.wait_ge(s_t, half * NT + t + 1)
                    copy(rows[:, half, t % 2, :], tr[:, (half * NT + t) % 4, :]).then_inc(s_c[half], 1)

            @block.scalar
            def _(act):
                act_part(act)
                copy_out(act, lambda o, i: act.activation(o, i, ACT.Copy), 0)

            @block.vector
            def _(dve):
                dve.wait_ge(s_r, 1)
                for k in range(KT):
                    dve.scalar_tensor_tensor(out=x[:, k, :], in0=x[:, k, :], scalar=K.norm_g[2][:, k:k + 1], in1=rstd[:, :],
                                             op0=ALU.mult, op1=ALU.mult).then_inc(s_n, 1)
                copy_out(dve, dve.tensor_copy, 1)

            @block.tensor
            def _(pe):
                pe_part(pe)
                for half in range(2):
                    pe.wait_ge(s_n, KT // 2 * (half + 1))
                    for t in range(NT):
                        n = half * NT + t
                        if n >= 4:
                            pe.wait_ge(s_c[(n - 4) // NT], (n - 4) % NT + 1)
                        for k in range(4):
                            mm = pe.transpose(tr[:, n % 4, k * P:(k + 1) * P], x[:, half * 4 + k, t * P:(t + 1) * P], K.ident[:, :])
                        mm.then_inc(s_t, 1)

            @block.sync
            def _(sync):
                for half in range(2):
                    for t in range(NT):
                        sync.wait_ge(s_c[half], t + 1)
                        dst = K.o["y_sample"][0, t * P:(t + 1) * P] if t < NS // P else K.o["y_prompt"][0, t * P - NS:(t + 1) * P - NS]
                        sync.dma_start(dst[:, half * 512:(half + 1) * 512], rows[:, half, t % 2, :]).then_inc(s_out[half][t % 2], 16)
                for half in range(2):
                    for slot in range(2):
                        sync.wait_ge(s_out[half][slot], 16 * (NT // 2))




def build(nc, ins, outs, consts):
    with ExitStack() as ctx:
        K = setup(nc, ins, outs, consts, ctx)
        phase_input(K)
        end_phase(K)
        with ExitStack() as st:
            phase_decays(K, st)
            phase_heads(K, st)
            end_phase(K)
        phase_s5(K)
        end_phase(K)
        with ExitStack() as st:
            mg = K.sb("merged", [P, KT, T], stack=st)
            ys = K.sb("ys", [P, 2, KT, T], BF16, stack=st)
            ys2 = K.sb("ys2", [P, 2, KT, T], BF16, stack=st)
            phase_branch_a(K, mg, ys2, ys)
            phase_branch_b(K, mg, ys, ys2)
            end_phase(K)
            phase_out(K, mg, ys)
            with ExitStack() as s2:
                norm_modulate(K, s2, mg, K.mul2, 3, "n2")
                end_phase(K)
            phase_mlp(K, mg, (ys, ys2))
            phase_final(K, mg)



OUTS = [((1, NP_, D), "y_prompt"), ((1, NS, D), "y_sample"), ((1, 1, 2, H, DK, DK), "new_state_delta"),
        ((1, 1, 2, G_S5, N_S5), "new_state_s5_re"), ((1, 1, 2, G_S5, N_S5), "new_state_s5_im")]


def kernel(**inputs):
    import concourse.bacc as bacc
    from concourse.bass_utils import run_bass_kernel_spmd

    nc = bacc.Bacc("TRN2", target_bir_lowering=False, num_devices=1)
    arrays, ins, consts = {}, {}, {}
    for name, a in inputs.items():
        arrays["in_" + name] = np.ascontiguousarray(a)
        ins[name] = nc.dram_tensor("in_" + name, list(a.shape), F32, kind="ExternalInput").ap()
    for name, a in constants().items():
        arrays["const_" + name] = a
        consts[name] = nc.dram_tensor("const_" + name, list(a.shape), F32, kind="ExternalInput").ap()
    outs = {name: nc.dram_tensor(name, list(shape), F32, kind="ExternalOutput").ap() for shape, name in OUTS}
    build(nc, ins, outs, consts)
    r = run_bass_kernel_spmd(nc, [arrays], core_ids=[0])
    return tuple(r.results[0][name] for _, name in OUTS)
```
